# Optimizing a Trainium2 kernel written in Bass

```python
import math
import jax, jax.numpy as jnp
from jax import lax
import numpy as np

D_MODEL = 1024
BATCH = 1
SEQ = 512
DEPTH = 1
DEC_BATCH = 8
DEC_SEQ = 1
PAST_LEN = 4096
PAGE_SIZE = 128

RET_HEADS = 4
RET_DK = 128
RET_DV = 128
RET_WIDTH = RET_HEADS * RET_DV
SSD_HEADS = 8
SSD_HEAD_DIM = 64
SSD_WIDTH = SSD_HEADS * SSD_HEAD_DIM
SSD_GROUPS = 2
SSD_STATE = 128
CONV_WIDTH = 4
CONV_CH = SSD_WIDTH + 2 * SSD_GROUPS * SSD_STATE
MIX_WIDTH = RET_WIDTH + SSD_WIDTH
CHUNK = 128
MEM_TOKENS = 256
X_HEADS = 4
X_HEAD_DIM = D_MODEL // X_HEADS
D_FF = 2816
ROPE_BASE = 10000.0
EPS = 1e-6
Q_END = RET_HEADS * RET_DK
K_END = Q_END + RET_HEADS * RET_DK
V_END = K_END + RET_WIDTH
G_END = V_END + RET_WIDTH
Z_END = G_END + SSD_WIDTH
XBC_END = Z_END + CONV_CH
IN_PROJ_WIDTH = XBC_END + SSD_HEADS

kernel_name = 'hymba_retnet_ssd_macaron_memxattn_step'

def rmsnorm(x, gain):
    xf = x.astype(jnp.float32)
    y = xf * lax.rsqrt(jnp.mean(xf * xf, axis=-1, keepdims=True) + EPS)
    return (y * gain.astype(jnp.float32)).astype(x.dtype)

def swiglu(x, w1, w3, w2):
    return (jax.nn.silu(x @ w1) * (x @ w3)) @ w2

def rotary(x, pos):
    half = x.shape[-1] // 2
    inv_freq = ROPE_BASE ** (-jnp.arange(half, dtype=jnp.float32) / half)
    ang = pos.astype(jnp.float32)[:, None] * inv_freq[None, :]
    cos = jnp.cos(ang)[None, :, None, :]
    sin = jnp.sin(ang)[None, :, None, :]
    xf = x.astype(jnp.float32)
    x1, x2 = xf[..., :half], xf[..., half:]
    return jnp.concatenate([x1 * cos - x2 * sin, x1 * sin + x2 * cos], axis=-1)

def chunk_len(L):
    return CHUNK if L % CHUNK == 0 else L

def retention_chunkwise(q, k, v, state):
    Bsz, L, H, dk = q.shape
    dv = v.shape[-1]
    C = chunk_len(L)
    n = L // C
    log_g = jnp.log1p(-jnp.exp2(-5.0 - jnp.arange(H, dtype=jnp.float32)))
    idx = jnp.arange(C, dtype=jnp.float32)
    diff = idx[:, None] - idx[None, :]
    causal = diff >= 0
    dmat = jnp.where(causal[None], jnp.exp(log_g[:, None, None] * jnp.where(causal, diff, 0.0)[None]), 0.0)
    q_dec = jnp.exp(log_g[None, :] * (idx[:, None] + 1.0))
    k_dec = jnp.exp(log_g[None, :] * (C - 1.0 - idx[:, None]))
    chunk_dec = jnp.exp(log_g * C)
    qc = q.reshape(Bsz, n, C, H, dk)
    kc = k.reshape(Bsz, n, C, H, dk)
    vc = v.reshape(Bsz, n, C, H, dv)
    inner = jnp.einsum('bclhd,bcshd->bchls', qc, kc) * dmat[None, None]
    y_in = jnp.einsum('bchls,bcshe->bclhe', inner, vc)
    kv = jnp.einsum('bcshd,sh,bcshe->bchde', kc, k_dec, vc)

    def step(S, kv_c):
        return chunk_dec[None, :, None, None] * S + kv_c, S

    S_final, S_prev = lax.scan(step, state, jnp.moveaxis(kv, 1, 0))
    S_prev = jnp.moveaxis(S_prev, 0, 1)
    y_x = jnp.einsum('bclhd,bchde->bclhe', qc, S_prev) * q_dec[None, None, :, :, None]
    return (y_in + y_x).reshape(Bsz, L, H, dv), S_final

def ssd_chunked(x, dt, A, Bm, Cm, state):
    Bsz, L, H, P = x.shape
    G, N = Bm.shape[2], Bm.shape[3]
    C = chunk_len(L)
    n = L // C
    rep = H // G
    Bh = jnp.repeat(Bm, rep, axis=2).reshape(Bsz, n, C, H, N)
    Ch = jnp.repeat(Cm, rep, axis=2).reshape(Bsz, n, C, H, N)
    a_cum = jnp.cumsum((dt * A[None, None, :]).reshape(Bsz, n, C, H), axis=2)
    xdt = (x * dt[..., None]).reshape(Bsz, n, C, H, P)
    idx = jnp.arange(C)
    causal = (idx[:, None] >= idx[None, :])[None, None, :, :, None]
    seg = a_cum[:, :, :, None, :] - a_cum[:, :, None, :, :]
    lmat = jnp.where(causal, jnp.exp(jnp.where(causal, seg, 0.0)), 0.0)
    scores = jnp.einsum('bclhn,bcshn->bclsh', Ch, Bh) * lmat
    y_diag = jnp.einsum('bclsh,bcshp->bclhp', scores, xdt)
    decay_s = jnp.exp(a_cum[:, :, -1:, :] - a_cum)
    states = jnp.einsum('bclhn,bclh,bclhp->bchpn', Bh, decay_s, xdt)
    chunk_dec = jnp.exp(a_cum[:, :, -1, :])

    def step(S, inp):
        st, dec = inp
        return dec[:, :, None, None] * S + st, S

    S_final, S_prev = lax.scan(step, state, (jnp.moveaxis(states, 1, 0), jnp.moveaxis(chunk_dec, 1, 0)))
    S_prev = jnp.moveaxis(S_prev, 0, 1)
    y_off = jnp.einsum('bclhn,bchpn,bclh->bclhp', Ch, S_prev, jnp.exp(a_cum))
    return (y_diag + y_off).reshape(Bsz, L, H, P), S_final

def causal_conv(xbc, conv_state, w, b):
    L = xbc.shape[1]
    full = jnp.concatenate([conv_state.astype(xbc.dtype), xbc], axis=1)
    out = b + sum(full[:, i:i + L, :] * w[i] for i in range(CONV_WIDTH))
    return out, full[:, L:, :]

def decoder_layer(x, pos, mem_k, mem_v, ret_state, ssm_state, conv_state, p):
    f32 = jnp.float32
    Bsz, L, _ = x.shape
    h = x + (0.5 * swiglu(rmsnorm(x, p['ffn1_norm']), p['ffn1_w1'], p['ffn1_w3'], p['ffn1_w2'])).astype(x.dtype)
    u = rmsnorm(h, p['mix_norm'])
    proj = u @ p['w_in']
    q, k, v, g, z, xbc, dt_raw = jnp.split(proj, [Q_END, K_END, V_END, G_END, Z_END, XBC_END], axis=-1)
    qr = rotary(q.reshape(Bsz, L, RET_HEADS, RET_DK), pos)
    kr = rotary(k.reshape(Bsz, L, RET_HEADS, RET_DK), pos) * (RET_DK ** -0.5)
    vr = v.reshape(Bsz, L, RET_HEADS, RET_DV).astype(f32)
    r, ret_new = retention_chunkwise(qr, kr, vr, ret_state.astype(f32))
    mu = jnp.mean(r, axis=-1, keepdims=True)
    var = jnp.mean(jnp.square(r - mu), axis=-1, keepdims=True)
    r = ((r - mu) * lax.rsqrt(var + EPS)).reshape(Bsz, L, RET_WIDTH) * p['ret_gn_gain'].astype(f32)
    ret_out = (jax.nn.silu(g.astype(f32)) * r).astype(x.dtype)
    xbc_c, conv_new = causal_conv(xbc, conv_state, p['conv_w'], p['conv_b'])
    xbc_c = jax.nn.silu(xbc_c.astype(f32))
    xs = xbc_c[..., :SSD_WIDTH].reshape(Bsz, L, SSD_HEADS, SSD_HEAD_DIM)
    Bm = xbc_c[..., SSD_WIDTH:SSD_WIDTH + SSD_GROUPS * SSD_STATE].reshape(Bsz, L, SSD_GROUPS, SSD_STATE)
    Cm = xbc_c[..., SSD_WIDTH + SSD_GROUPS * SSD_STATE:].reshape(Bsz, L, SSD_GROUPS, SSD_STATE)
    dt = jax.nn.softplus(dt_raw.astype(f32) + p['dt_bias'].astype(f32))
    A = -jnp.exp(p['A_log'].astype(f32))
    ys, ssm_new = ssd_chunked(xs, dt, A, Bm, Cm, ssm_state.astype(f32))
    ys = ys + p['D_skip'].astype(f32)[:, None] * xs
    ys = ys.reshape(Bsz, L, SSD_WIDTH) * jax.nn.silu(z.astype(f32))
    ssd_out = rmsnorm(ys, p['ssd_norm']).astype(x.dtype)
    h = h + (jnp.concatenate([ret_out, ssd_out], axis=-1) @ p['w_out']).astype(x.dtype)
    c = rmsnorm(h, p['x_norm'])
    qx = (c @ p['w_xq']).reshape(Bsz, L, X_HEADS, X_HEAD_DIM)
    s = jnp.einsum('blhd,bmhd->bhlm', qx, mem_k.astype(x.dtype)).astype(f32) * (X_HEAD_DIM ** -0.5)
    att = jax.nn.softmax(s, axis=-1).astype(x.dtype)
    o = jnp.einsum('bhlm,bmhd->blhd', att, mem_v.astype(x.dtype)).reshape(Bsz, L, X_HEADS * X_HEAD_DIM)
    h = h + (o @ p['w_xo']).astype(x.dtype)
    h = h + (0.5 * swiglu(rmsnorm(h, p['ffn2_norm']), p['ffn2_w1'], p['ffn2_w3'], p['ffn2_w2'])).astype(x.dtype)
    return (h, ret_new.astype(ret_state.dtype), ssm_new.astype(ssm_state.dtype), conv_new.astype(conv_state.dtype))

def setup_inputs(seed: int = 0) -> dict:
    key = jax.random.key(seed)
    ks = iter(jax.random.split(key, 40))

    def nrm(shape, scale):
        return jax.random.normal(next(ks), shape, jnp.float32) * scale

    def gain(shape):
        return 1.0 + nrm(shape, 0.02)

    x_prompt = nrm((BATCH, SEQ, D_MODEL), 1.0)
    x_sample = nrm((DEC_BATCH, DEC_SEQ, D_MODEL), 1.0)
    mem_prompt = nrm((BATCH, MEM_TOKENS, D_MODEL), 1.0)
    state_ret = nrm((DEPTH, DEC_BATCH, RET_HEADS, RET_DK, RET_DV), 0.1)
    state_ssm = nrm((DEPTH, DEC_BATCH, SSD_HEADS, SSD_HEAD_DIM, SSD_STATE), 0.1)
    state_conv = nrm((DEPTH, DEC_BATCH, CONV_WIDTH - 1, CONV_CH), 1.0)
    cache_mem_k = nrm((DEPTH, DEC_BATCH, MEM_TOKENS, X_HEADS, X_HEAD_DIM), 1.0)
    cache_mem_v = nrm((DEPTH, DEC_BATCH, MEM_TOKENS, X_HEADS, X_HEAD_DIM), 1.0)
    ffn1_norm = gain((DEPTH, D_MODEL))
    ffn1_w1 = nrm((DEPTH, D_MODEL, D_FF), D_MODEL ** -0.5)
    ffn1_w3 = nrm((DEPTH, D_MODEL, D_FF), D_MODEL ** -0.5)
    ffn1_w2 = nrm((DEPTH, D_FF, D_MODEL), D_FF ** -0.5)
    mix_norm = gain((DEPTH, D_MODEL))
    w_in = nrm((DEPTH, D_MODEL, IN_PROJ_WIDTH), D_MODEL ** -0.5)
    ret_gn_gain = gain((DEPTH, RET_WIDTH))
    conv_w = nrm((DEPTH, CONV_WIDTH, CONV_CH), CONV_WIDTH ** -0.5)
    conv_b = nrm((DEPTH, CONV_CH), 0.02)
    dt0 = jnp.exp(jax.random.uniform(next(ks), (DEPTH, SSD_HEADS), jnp.float32, math.log(1e-3), math.log(1e-1)))
    dt_bias = dt0 + jnp.log(-jnp.expm1(-dt0))
    A_log = jnp.log(jax.random.uniform(next(ks), (DEPTH, SSD_HEADS), jnp.float32, 1.0, 16.0))
    D_skip = gain((DEPTH, SSD_HEADS))
    ssd_norm = gain((DEPTH, SSD_WIDTH))
    w_out = nrm((DEPTH, MIX_WIDTH, D_MODEL), MIX_WIDTH ** -0.5)
    x_norm = gain((DEPTH, D_MODEL))
    mem_norm = gain((DEPTH, D_MODEL))
    w_xq = nrm((DEPTH, D_MODEL, X_HEADS * X_HEAD_DIM), D_MODEL ** -0.5)
    w_xk = nrm((DEPTH, D_MODEL, X_HEADS * X_HEAD_DIM), D_MODEL ** -0.5)
    w_xv = nrm((DEPTH, D_MODEL, X_HEADS * X_HEAD_DIM), D_MODEL ** -0.5)
    w_xo = nrm((DEPTH, X_HEADS * X_HEAD_DIM, D_MODEL), (X_HEADS * X_HEAD_DIM) ** -0.5)
    ffn2_norm = gain((DEPTH, D_MODEL))
    ffn2_w1 = nrm((DEPTH, D_MODEL, D_FF), D_MODEL ** -0.5)
    ffn2_w3 = nrm((DEPTH, D_MODEL, D_FF), D_MODEL ** -0.5)
    ffn2_w2 = nrm((DEPTH, D_FF, D_MODEL), D_FF ** -0.5)
    final_norm = gain((D_MODEL,))
    return {'x_prompt': x_prompt, 'x_sample': x_sample, 'mem_prompt': mem_prompt,
            'state_ret': state_ret, 'state_ssm': state_ssm, 'state_conv': state_conv,
            'cache_mem_k': cache_mem_k, 'cache_mem_v': cache_mem_v,
            'ffn1_norm': ffn1_norm, 'ffn1_w1': ffn1_w1, 'ffn1_w3': ffn1_w3, 'ffn1_w2': ffn1_w2,
            'mix_norm': mix_norm, 'w_in': w_in, 'ret_gn_gain': ret_gn_gain,
            'conv_w': conv_w, 'conv_b': conv_b, 'dt_bias': dt_bias, 'A_log': A_log,
            'D_skip': D_skip, 'ssd_norm': ssd_norm, 'w_out': w_out,
            'x_norm': x_norm, 'mem_norm': mem_norm, 'w_xq': w_xq, 'w_xk': w_xk,
            'w_xv': w_xv, 'w_xo': w_xo,
            'ffn2_norm': ffn2_norm, 'ffn2_w1': ffn2_w1, 'ffn2_w3': ffn2_w3, 'ffn2_w2': ffn2_w2,
            'final_norm': final_norm}

def reference(x_prompt, x_sample, mem_prompt, state_ret, state_ssm, state_conv,
              cache_mem_k, cache_mem_v, ffn1_norm, ffn1_w1, ffn1_w3, ffn1_w2,
              mix_norm, w_in, ret_gn_gain, conv_w, conv_b, dt_bias, A_log, D_skip,
              ssd_norm, w_out, x_norm, mem_norm, w_xq, w_xk, w_xv, w_xo,
              ffn2_norm, ffn2_w1, ffn2_w3, ffn2_w2, final_norm):
    Bp, Lp, _ = x_prompt.shape
    pos_p = jnp.arange(Lp)
    pos_s = PAST_LEN + jnp.arange(x_sample.shape[1])
    dtp = x_prompt.dtype
    y_p = x_prompt
    y_s = x_sample
    ret_p, ssm_p, conv_p, memk_p, memv_p = [], [], [], [], []
    ret_s, ssm_s, conv_s = [], [], []
    for l in range(DEPTH):
        p = {'ffn1_norm': ffn1_norm[l], 'ffn1_w1': ffn1_w1[l], 'ffn1_w3': ffn1_w3[l], 'ffn1_w2': ffn1_w2[l],
             'mix_norm': mix_norm[l], 'w_in': w_in[l], 'ret_gn_gain': ret_gn_gain[l],
             'conv_w': conv_w[l], 'conv_b': conv_b[l], 'dt_bias': dt_bias[l], 'A_log': A_log[l],
             'D_skip': D_skip[l], 'ssd_norm': ssd_norm[l], 'w_out': w_out[l],
             'x_norm': x_norm[l], 'w_xq': w_xq[l], 'w_xo': w_xo[l],
             'ffn2_norm': ffn2_norm[l], 'ffn2_w1': ffn2_w1[l], 'ffn2_w3': ffn2_w3[l], 'ffn2_w2': ffn2_w2[l]}
        m = rmsnorm(mem_prompt, mem_norm[l])
        mk = (m @ w_xk[l]).reshape(Bp, MEM_TOKENS, X_HEADS, X_HEAD_DIM)
        mv = (m @ w_xv[l]).reshape(Bp, MEM_TOKENS, X_HEADS, X_HEAD_DIM)
        zr = jnp.zeros((Bp, RET_HEADS, RET_DK, RET_DV), dtp)
        zs = jnp.zeros((Bp, SSD_HEADS, SSD_HEAD_DIM, SSD_STATE), dtp)
        zc = jnp.zeros((Bp, CONV_WIDTH - 1, CONV_CH), dtp)
        y_p, rp, sp, cp = decoder_layer(y_p, pos_p, mk, mv, zr, zs, zc, p)
        y_s, rs, ss, cs = decoder_layer(y_s, pos_s, cache_mem_k[l], cache_mem_v[l],
                                        state_ret[l], state_ssm[l], state_conv[l], p)
        ret_p.append(rp)
        ssm_p.append(sp)
        conv_p.append(cp)
        memk_p.append(mk)
        memv_p.append(mv)
        ret_s.append(rs)
        ssm_s.append(ss)
        conv_s.append(cs)
    y_prompt = rmsnorm(y_p, final_norm)
    y_sample = rmsnorm(y_s, final_norm)
    return (y_prompt, y_sample, jnp.stack(ret_p), jnp.stack(ssm_p), jnp.stack(conv_p),
            jnp.stack(memk_p), jnp.stack(memv_p), jnp.stack(ret_s), jnp.stack(ssm_s), jnp.stack(conv_s))


_drawn_inputs = setup_inputs


def setup_inputs(seed=0):
    import zlib

    import numpy as np

    out = dict(_drawn_inputs(seed))
    spreads = {}
    factors = {'ffn1_norm': 4.066,
     'ret_gn_gain': 8.0,
     'D_skip': 8.0,
     'ssd_norm': 4.809,
     'x_norm': 8.0,
     'mem_norm': 2.911,
     'ffn2_norm': 8.0,
     'final_norm': 2.726}
    for name, (base, spread) in spreads.items():
        noise = np.random.default_rng([zlib.crc32(name.encode()), seed]).standard_normal(out[name].shape)
        drawn = base * np.exp(spread * noise) if base else spread * noise
        out[name] = __import__('jax').numpy.asarray(drawn.astype(out[name].dtype))
    for name, factor in factors.items():
        out[name] = (out[name] * factor).astype(out[name].dtype)
    return out
```

```python
from contextlib import ExitStack

import numpy as np

import concourse.bass as bass
from concourse import mybir

F32 = mybir.dt.float32
F32R = mybir.dt.float32r
ALU = mybir.AluOpType
ACT = mybir.ActivationFunctionType
AX_X = mybir.AxisListType.X

P = 128
D = 1024
DT = D // P
SEQ = 512
NS = 8
T = NS + SEQ
HT = T // 2
BANK = 512
FF = 2816
FT = FF // P
KH = FT // 2
HR = 4
HS = 8
HP = 64
SG = 2
CH = 128
NCH = SEQ // CH
MEM = 256
MT = MEM // P
XH = 4
TAPS = 4
EPS = 1e-6
RK_SCALE = 128.0 ** -0.5
X_SCALE = 256.0 ** -0.5
NEG = -1.0e30
TOKT = 5
LEAD = 3
RING = 4
RAW = 2
GAMMA = [float(np.exp(np.log1p(-np.exp2(np.float64(-5.0 - h))))) for h in range(HR)]

STAGE_LIST = [
    ("up1", 2 * FT, 1024, FT),
    ("down1", 2 * DT, KH * P, DT // 2),
    ("qk", 8, 1024, 4),
    ("v", 4, 1024, 1),
    ("xbc", 8, 1024, 4),
    ("gz", 8, 1024, 4),
    ("xk", 8, 1024, 4),
    ("xv", 8, 1024, 1),
    ("out", 8, 1024, 4),
    ("xq", 8, 1024, 4),
    ("xo", 8, 1024, 4),
    ("up2", 2 * FT, 1024, FT),
    ("down2", 2 * DT, KH * P, DT // 2),
]

NORM_LIST = [("ffn1", 8, T), ("mix", 8, T), ("mem", 8, MEM), ("ssd", 4, T), ("x", 8, T), ("ffn2", 8, T),
             ("final", 8, T)]
SPLIT_LIST = [("ffn1", 8), ("mix", 8), ("mem", 8), ("ret", 4), ("ssd", 4), ("x", 8), ("ffn2", 8)]
MADE_LIST = [("ret", 4), ("ssd", 4), ("final", 8)]


class Stage:

    def __init__(self, name, units, cols, u0, freed):
        self.name, self.units, self.cols, self.u0, self.freed = name, units, cols, u0, freed
        self.loops = units // RING


def make_stages():
    out, u0, freed = {}, 0, 1
    for name, units, cols, tiles in STAGE_LIST:
        out[name] = Stage(name, units, cols, u0, freed)
        u0, freed = u0 + units, freed + tiles
    return out, u0


def starts(items, extra):
    out, at = {}, 0
    for it in items:
        out[it[0]] = at
        at += it[1] + extra
    return out


STAGES, UNITS = make_stages()
UNIT_COLS = [s.cols for s in STAGES.values() for _ in range(s.units)]
NORM_AT = {n[0]: i for i, n in enumerate(NORM_LIST)}
NORM_TILES = {n[0]: n[1] for n in NORM_LIST}
NORM_COLS = {n[0]: n[2] for n in NORM_LIST}
SQ0 = starts(NORM_LIST, 1)
SPLIT0 = starts(SPLIT_LIST, 0)
SPLIT_TILES = dict(SPLIT_LIST)
MADE0 = starts(MADE_LIST, 0)


def tables():
    half = 64
    inv = (10000.0 ** (-np.arange(half, dtype=np.float32) / np.float32(half))).astype(np.float32)
    pos = np.concatenate([np.full(NS, 4096.0), np.arange(SEQ)]).astype(np.float32)
    ang = (inv[:, None] * pos[None, :]).astype(np.float32)
    c, s = np.cos(ang), np.sin(ang)
    rope = np.stack([np.concatenate([c, c]), np.concatenate([s, -s])], 1)
    log_g = np.log1p(-np.exp2(-5.0 - np.arange(HR)))
    i = np.arange(CH)
    diff = i[None, :] - i[:, None]
    dmat = np.where(diff >= 0, np.exp(log_g[:, None, None] * np.maximum(diff, 0)), 0.0) * RK_SCALE
    q_dec = np.exp(log_g[:, None] * (i[None, :] + 1.0))
    k_dec = np.exp(log_g[None, :] * (CH - 1.0 - i[:, None])) * RK_SCALE
    ret = np.concatenate([dmat.transpose(1, 0, 2).reshape(P, -1),
                          np.broadcast_to(q_dec.reshape(1, -1), (P, HR * CH)), k_dec], 1)
    eye = np.eye(P)
    upper = (diff >= 0).astype(np.float32)
    mask = np.where(diff >= 0, 0.0, NEG)
    small = np.zeros((P, 8))
    small[:, 0], small[:, 1], small[:, 2], small[:, 3] = 1 / D, 1 / 512, 1 / P, EPS
    square = np.concatenate([eye, np.ones((P, P)), small], 1)
    triangle = np.concatenate([eye - 1.0 / P, upper, mask], 1)
    f = lambda a: np.ascontiguousarray(a, dtype=np.float32)
    return {"c_rope": f(rope), "c_ret": f(ret), "c_square": f(square), "c_triangle": f(triangle)}


def build(nc, A, PLAN=("ffn1", "mix", "xattn", "ffn2")):
    ctx = ExitStack()
    with ctx:
        def sb(name, shape, dt=F32, stack=ctx):
            return stack.enter_context(nc.sbuf_tensor(name, shape, dt))

        def sem(name):
            return ctx.enter_context(nc.semaphore(name))

        ps = ctx.enter_context(nc.psum_tensor("ps", [P, 8 * BANK], F32))

        def bank(b, n=BANK, at=0, rows=P, row0=0):
            return ps[row0:row0 + rows, b * BANK + at:b * BANK + at + n]

        def half(b, x):
            return ps[:, (b + x) * BANK:(b + x) * BANK + HT]

        def tile_halves(b):
            return ps[:, b * BANK:(b + 2) * BANK].rearrange("p (a c) -> p a c", a=2)[:, :, 0:HT]

        def two(ap):
            return ap.rearrange("p (a c) -> p a c", a=2)

        def f32(ap):
            return ap.bitcast(F32)

        h = sb("h", [P, DT, T])
        x_hi = sb("x_hi", [P, DT, T], F32R)
        x_lo = sb("x_lo", [P, DT, T], F32R)
        w_raw = [sb(f"w_raw{i}", [P, KH * P]) for i in range(RAW)]
        w_hi_t = [sb(f"w_hi{i}", [P, KH * P], F32R) for i in range(RING)]
        w_lo_t = [sb(f"w_lo{i}", [P, KH * P], F32R) for i in range(RING)]
        gains = sb("gains", [P, 6 * DT + HR + HR])
        square = sb("square", [P, 2 * P + 8])
        xf = sb("xf", [P, 2, T])
        sq = sb("sq", [P, 2, T])
        sq_sum = sb("sq_sum", [P, T])
        rstd = sb("rstd", [P, T])
        row_std = sb("row_std", [P, 2, TOKT])
        diag = xf[:, :, :].rearrange("p a c -> p (a c)")[:, 0:TOKT * P].rearrange("p (t c) -> p t c", t=TOKT)
        ident, ones = (square[:, i * P:(i + 1) * P] for i in range(2))
        inv_d, inv_512, inv_p, eps = (square[:, 2 * P + i:2 * P + i + 1] for i in range(4))
        GAIN0 = {"ffn1": 0, "mem": 8, "mix": 16, "x": 24, "ffn2": 32, "final": 40, "ret": 48, "ssd": 52}

        def gain(name, k):
            return gains[:, GAIN0[name] + k:GAIN0[name] + k + 1]

        ffn = ExitStack()
        gu_hi = sb("gu_hi", [P, FT, T], F32R, ffn)
        gu_lo = sb("gu_lo", [P, FT, T], F32R, ffn)
        ffn.close()

        mix = ExitStack()

        def region(name, cols, *groups):
            out = []
            for g in groups:
                part = ExitStack()
                out += [sb(n, shape, F32R if n.endswith("_hi") or n.endswith("_lo") else F32, part)
                        for n, shape in g]
                part.close()
            sb("hold_" + name, [P, cols], F32, mix)
            return out

        HT4 = 4 * T
        q_t, att_p, oa_lo = region("q", HT4, [("q_t", [P, HR, T])], [("att_p", [P, 2, XH * MEM])],
                           [("oa_lo", [P, 4, T])])
        k_t, mem_v = region("k", HT4, [("k_t", [P, HR, T])], [("mem_v", [P, MT, D])])
        cx, qx_a, oa_hi = region("cx", HT4, [("cx", [P, 4, T])], [("qx_a", [P, 4, T])], [("oa_hi", [P, 4, T])])
        cb, ssd_hi, qx_b, ob_hi = region("cb", HT4, [("cb", [P, 4, T])], [("ssd_hi", [P, 4, T])],
                                         [("qx_b", [P, 4, T])], [("ob_hi", [P, 4, T])])
        g_t, att_0 = region("g", HT4, [("g_t", [P, HR, T])], [("att_0", [P, XH, SEQ])])
        z_t, ssd_lo, att_1 = region("z", HT4, [("z_t", [P, 4, T])], [("ssd_lo", [P, 4, T])],
                                    [("att_1", [P, XH, SEQ])])
        ret_s, c_ret, mem_t, mem_k, ob_lo = region("h", HT4,
                                            [("ret_s", [P, 2, HR * P]), ("c_ret", [P, 2 * HR * CH + HR])],
                                            [("mem_t", [P, 8, MEM])], [("mem_k", [P, 8, MEM])],
                                            [("ob_lo", [P, 4, T])])
        (v_t, ret_w, ret_k, ret_qd, rope, conv_in,
         ssd_au, ssd_l, ssd_e, xdt, xdd, b_tok, ssd_s, ssd_sd,
         ks, xdts, bs, dm, decb, xm, st_ret, vm,
         _pad, st_ssm,
         gn_s, ret_hi, ret_lo,
         cache, s_rows, s_stat, y_out) = region("scratch", 6528,
                         [("v_t", [P, NCH, HR * P]), ("ret_w", [P, HR * CH]), ("ret_k", [P, HR * P]),
                          ("ret_qd", [P, HR * CH]), ("rope", [P, 2, T]), ("conv_in", [P, 2, SEQ + TAPS - 1])],
                         [("ssd_au", [P, HS * CH]), ("ssd_l", [P, HS * CH]), ("ssd_e", [P, HS * CH]),
                          ("xdt", [P, HS * HP]), ("xdd", [P, HS * HP]), ("b_tok", [P, SG * P]),
                          ("ssd_s", [P, HS * HP]), ("ssd_sd", [P, HS * HP])],
                         [("ks", [NS, HR * P]), ("xdts", [NS, HS * HP]), ("bs", [NS, SG * P]),
                          ("dm", [NS, NS * HS]), ("decb", [P, NS * HS]), ("xm", [NS, 4, 4 * HP]),
                          ("st_ret", [P, 2, NS * P]), ("vm", [NS, 2, NS * P])],
                         [("pad_small", [P, 2432]), ("st_ssm", [P, 2, NS * 4 * HP])],
                         [("gn_s", [P, HR, T]), ("ret_hi", [P, HR, T]), ("ret_lo", [P, HR, T])],
                         [("cache", [P, 3, 2048]), ("s_rows", [NS * XH, MEM]), ("s_stat", [NS * XH, 4])],
                         [("y_out", [P, DT, T])])
        vs = sb("vs", [NS, HR * P], F32, mix)
        triangle = sb("triangle", [P, 3 * P], F32, mix)
        centre, upper, mask = (triangle[:, i * P:(i + 1) * P] for i in range(3))
        small = sb("small", [P, TAPS * 8 + 8 + 8 + 8 + 4], F32, mix)
        conv_w = small[:, 0:TAPS * 8].rearrange("p (t n) -> p t n", t=TAPS)
        conv_b, dt_bias, a_log, d_skip = small[:, 32:40], small[:, 40:48], small[:, 48:56], small[:, 56:60]
        conv_s = sb("conv_s", [P, TAPS, 8 * NS], F32, mix)
        conv_last = sb("conv_last", [P, 8, TAPS - 1], F32, mix)
        wdt = sb("wdt", [P, DT * HS], F32, mix)
        wdt_hi = sb("wdt_hi", [P, DT * HS], F32R, mix)
        wdt_lo = sb("wdt_lo", [P, DT * HS], F32R, mix)
        NDT = TOKT * HS
        dts = sb("dts", [P, 10, NDT], F32, mix)
        dt_x, dt_ab, dt_e, dt_u, dt_d, dt_m, dt_t, a_dt, dt_r, a_cum = (dts[:, i, :] for i in range(10))
        a_exp = sb("a_exp", [P, HS], F32, mix)
        decay = sb("decay", [P, 2, NCH * HS], F32, mix)
        gn_r = sb("gn_r", [P, 2, HR * TOKT], F32, mix)
        att_s = sb("att_s", [P, 2, 3 * XH], F32, mix)
        att_c = sb("att_c", [P, 2, 4 * NS * 2], F32, mix)

        def chunk(c):
            return slice(NS + c * CH, NS + (c + 1) * CH)

        def conv_tile(n):
            return cx[:, n, :] if n < 4 else cb[:, n - 4, :]

        def qx(n):
            return qx_a[:, n, :] if n < 4 else qx_b[:, n - 4, :]

        def o_tiles(n):
            return (oa_hi[:, n, :], oa_lo[:, n, :]) if n < 4 else (ob_hi[:, n - 4, :], ob_lo[:, n - 4, :])

        def flat(t):
            return t[:, :, :].rearrange("p k c -> p (k c)")

        def m_tile(t, k):
            return flat(t)[:, k * MEM:(k + 1) * MEM]

        mix.close()

        consts_loaded = sem("consts_loaded")
        h_loaded = [sem(f"h_loaded{i}") for i in range(4)]
        w_loaded = [sem(f"w_loaded{i}") for i in range(RAW)]
        w_hi = sem("w_hi")
        w_lo = sem("w_lo")
        unit_done = sem("unit_done")
        pair_free = [sem("pair0_free"), sem("pair1_free")]
        gu_hi_done = sem("gu_hi_done")
        gu_lo_done = sem("gu_lo_done")
        sq_done = sem("sq_done")
        sq_added = sem("sq_added")
        rows_done = sem("rows_done")
        row_std_done = sem("row_std_done")
        row_inv_done = sem("row_inv_done")
        diag_done = sem("diag_done")
        spread_done = sem("spread_done")
        rstd_done = sem("rstd_done")
        xf_done = sem("xf_done")
        x_hi_done = sem("x_hi_done")
        x_lo_done = sem("x_lo_done")
        y_stored = sem("y_stored")

        def cols_of(v, stage, dynamic):
            return stage.cols if dynamic else UNIT_COLS[v]

        def unit_hi(v, j, cols):
            nc.scalar.wait_ge(w_loaded[j % RAW], w_load_count(v, j))
            nc.scalar.wait_ge(unit_done, v - RING + 1)
            nc.scalar.activation(w_hi_t[j][:, 0:cols], w_raw[j % RAW][:, 0:cols], ACT.Copy).then_inc(w_hi, 1)

        def w_load_count(v, j):
            if isinstance(v, int):
                return 16 * (v // 2 + 1)
            return (v - j) * 8 + 16 * (j // 2 + 1)

        def unit_lo(v, j, cols):
            nc.vector.wait_ge(w_hi, v + 1)
            nc.vector.tensor_tensor(w_lo_t[j][:, 0:cols], w_raw[j % RAW][:, 0:cols], f32(w_hi_t[j][:, 0:cols]),
                                    ALU.subtract).then_inc(w_lo, 1)

        def ahead(split, stage, i, j):
            if isinstance(i, int):
                v = stage.u0 + RING * i + j + LEAD
                if v < LAST_UNIT[0]:
                    if v < RING and split is unit_hi:
                        split_first(v)
                    else:
                        split(v, v % RING, UNIT_COLS[v])
            else:
                split(i * RING + (stage.u0 + j + LEAD), (j + LEAD) % RING, stage.cols)

        def split_first(v):
            nc.scalar.wait_ge(w_loaded[v % RAW], 16 * (v // RAW + 1))
            nc.scalar.activation(w_hi_t[v][:, 0:UNIT_COLS[v]], w_raw[v % RAW][:, 0:UNIT_COLS[v]],
                                 ACT.Copy).then_inc(w_hi, 1)

        def turns(eng, stage, body):
            first = 1 if stage.u0 == 0 else 0
            if stage.loops > 2:
                if first:
                    body(0)
                with eng.Fori(first, stage.loops - 1) as i:
                    body(i)
                body(stage.loops - 1)
            else:
                for i in range(stage.loops):
                    body(i)

        def three(out, w_h, w_l, m_h, m_l, start, stop):
            nc.tensor.matmul(out, w_h, m_l, start=start, stop=False)
            nc.tensor.matmul(out, w_l, m_h, start=False, stop=False)
            return nc.tensor.matmul(out, w_h, m_h, start=False, stop=stop)

        def tile_products(slot, blocks, b, operand, k0, first, last, width=T, ready=None):
            n = width // 2 if width > BANK else width
            mm = None
            for kk in range(blocks):
                if ready:
                    nc.tensor.wait_ge(ready[0], ready[1] + k0 + kk + 1)
                w_h, w_l = (w[slot][:, kk * P:(kk + 1) * P] for w in (w_hi_t, w_lo_t))
                m_h, m_l = operand(k0 + kk)
                s, e = first and kk == 0, last and kk == blocks - 1
                for a in range(width // n):
                    cut = slice(a * n, (a + 1) * n)
                    mm = three(ps[:, (b + a) * BANK:(b + a) * BANK + n], w_h, w_l, m_h[:, cut], m_l[:, cut], s, e)
            return mm

        def gemm(stage, operand, ready, ready0, per_tile=1, width=T, after=None, after_first=None):
            blocks = stage.cols // P

            def turn(i, steps=None):
                for j in range(RING):
                    u = i * RING + (stage.u0 + j)
                    tile = j // per_tile
                    b = 2 * (tile % 2)
                    first, last = j % per_tile == 0, j % per_tile == per_tile - 1
                    nc.tensor.wait_ge(w_lo, u + 1)
                    if first:
                        nc.tensor.wait_ge(pair_free[tile % 2],
                                          i * (RING // per_tile // 2) + (stage.freed + tile // 2))
                    tile_products(j, blocks, b, operand, (j % per_tile) * blocks, first, last, width,
                                  (ready, ready0) if tile == 0 else None).then_inc(unit_done, 1)
                    if after:
                        after(i * RING + j)
                    elif steps and j in steps:
                        steps[j]()

            if after:
                for i in range(stage.loops):
                    turn(i)
            elif after_first:
                turn(0, after_first)
                with nc.tensor.Fori(1, stage.loops) as i:
                    turn(i)
            else:
                with nc.tensor.Fori(0, stage.loops) as i:
                    turn(i)

        def norm_clear():
            nc.vector.memset(sq_sum[:, :], 0.0).then_inc(sq_added, 1)

        def norm_square(name, n, source, i=None):
            w = NORM_COLS[name]
            nc.scalar.wait_ge(sq_added, SQ0[name] + n if i is None else i * 2 + (SQ0[name] + n))
            nc.scalar.activation(sq[:, n % 2, 0:w], source, ACT.Square).then_inc(sq_done, 1)

        SQD0 = starts(NORM_LIST, 0)

        def norm_add(name, n, i=None):
            w = NORM_COLS[name]
            a, b = SQD0[name] + n + 1, SQ0[name] + n + 1
            nc.vector.wait_ge(sq_done, a if i is None else i * 2 + a)
            nc.vector.wait_ge(sq_added, b if i is None else i * 2 + b)
            nc.vector.tensor_tensor(sq_sum[:, 0:w], sq_sum[:, 0:w], sq[:, n % 2, 0:w],
                                    ALU.add).then_inc(sq_added, 1)

        def row_tiles(w):
            if w == MEM:
                return [(t * P, P, t * P) for t in range(MT)]
            return [(NS + c * CH, CH, c * CH) for c in range(NCH)] + [(0, NS, SEQ)]

        def norm_rows_pe(name, inv_n):
            w, r = NORM_COLS[name], NORM_AT[name]
            nc.tensor.wait_ge(sq_added, SQ0[name] + NORM_TILES[name] + 1)
            for t, (c0, _, _) in enumerate(row_tiles(w)):
                mm = nc.tensor.matmul(bank(6, 1, t), sq_sum[:, c0:c0 + P], inv_n, start=True, stop=True)
            mm.then_inc(rows_done, 1)

        def norm_rows_act(name):
            n = len(row_tiles(NORM_COLS[name]))
            nc.scalar.wait_ge(rows_done, NORM_AT[name] + 1)
            nc.scalar.activation(row_std[:, 0, 0:n], bank(6, n), ACT.Sqrt, bias=eps).then_inc(row_std_done, 1)

        def norm_diag_dve(name):
            n, r = len(row_tiles(NORM_COLS[name])), NORM_AT[name]
            nc.vector.wait_ge(row_std_done, r + 1)
            nc.vector.reciprocal(row_std[:, 1, 0:n], row_std[:, 0, 0:n]).then_inc(row_inv_done, 1)
            nc.vector.wait_ge(row_inv_done, r + 1)
            nc.vector.tensor_tensor(diag[:, 0:n, :], ident.unsqueeze(1).to_broadcast([P, n, P]),
                                    row_std[:, 1, 0:n].unsqueeze(2).to_broadcast([P, n, P]),
                                    ALU.mult).then_inc(diag_done, 1)

        def norm_spread_pe(name):
            nc.tensor.wait_ge(diag_done, NORM_AT[name] + 1)
            for t, (_, n, to) in enumerate(row_tiles(NORM_COLS[name])):
                mm = nc.tensor.matmul(ps[:, 4 * BANK + to:4 * BANK + to + n], ones, diag[:, t, 0:n],
                                      start=True, stop=True)
            mm.then_inc(spread_done, 1)

        def norm_rstd_act(name):
            w = NORM_COLS[name]
            nc.scalar.wait_ge(spread_done, NORM_AT[name] + 1)
            lead = w % P
            if lead:
                nc.scalar.activation(rstd[:, 0:lead], ps[:, 5 * BANK:5 * BANK + lead], ACT.Copy)
            nc.scalar.activation(rstd[:, lead:w], ps[:, 4 * BANK:4 * BANK + w - lead], ACT.Copy).then_inc(rstd_done, 1)


        def gained_hi(name, k, source, dest):
            nc.scalar.activation(dest, source, ACT.Copy, scale=gain(name, k)).then_inc(x_hi_done, 1)

        def gained_lo(name, k, source, hi, dest, count):
            nc.vector.wait_ge(x_hi_done, count)
            nc.vector.scalar_tensor_tensor(out=dest, in0=source, scalar=gain(name, k), in1=f32(hi), op0=ALU.mult,
                                           op1=ALU.subtract).then_inc(x_lo_done, 1)

        def made_hi_act(name, dest):
            for k in range(SPLIT_TILES[name]):
                nc.scalar.wait_ge(xf_done, MADE0[name] + k + 1)
                nc.scalar.activation(dest(k), xf[:, k % 2, :], ACT.Copy).then_inc(x_hi_done, 1)

        def made_dve(name, make, dest_hi, dest_lo):
            s0, n = SPLIT0[name], SPLIT_TILES[name]
            for k in range(n + 1):
                if k < n:
                    nc.vector.wait_ge(x_lo_done, s0 + k - 1)
                    make(k, xf[:, k % 2, :]).then_inc(xf_done, 1)
                if k:
                    nc.vector.wait_ge(x_hi_done, s0 + k)
                    nc.vector.tensor_tensor(dest_lo(k - 1), xf[:, (k - 1) % 2, :], f32(dest_hi(k - 1)),
                                            ALU.subtract).then_inc(x_lo_done, 1)

        def normed(name, source, w=T):
            def make(k, out):
                return nc.vector.scalar_tensor_tensor(out=out, in0=source(k), scalar=gain(name, k),
                                                      in1=rstd[:, 0:w], op0=ALU.mult, op1=ALU.mult)
            return make

        def x_tiles(k):
            return x_hi[:, k, :], x_lo[:, k, :]

        def norm_steps_pe(name):
            return {0: lambda: norm_rows_pe(name, inv_d), 1: lambda: norm_spread_pe(name)}

        def norm_of_h_act(name):
            norm_rows_act(name)
            norm_rstd_act(name)

        def norm_of_h_dve(name):
            norm_diag_dve(name)
            nc.vector.wait_ge(rstd_done, NORM_AT[name] + 1)

        def h_tile_act(name, n, i=None):
            k = n if i is None else i * 2 + n
            norm_square(name, n, h[:, k, :], i)
            if isinstance(k, int):
                nc.scalar.activation(x_hi[:, k, :], h[:, k, :], ACT.Copy, scale=gain(name, k)).then_inc(x_hi_done, 1)
            else:
                nc.scalar.activation(x_hi[:, k, :], h[:, k, :], ACT.Copy,
                                     scale=gains[:, bass.ds(k + GAIN0[name], 1)]).then_inc(x_hi_done, 1)

        def h_tile_dve(name, n, i=None):
            k = n if i is None else i * 2 + n
            g = gain(name, k) if isinstance(k, int) else gains[:, bass.ds(k + GAIN0[name], 1)]
            nc.vector.wait_ge(x_hi_done, k + (SPLIT0[name] + 1))
            nc.vector.scalar_tensor_tensor(out=x_lo[:, k, :], in0=h[:, k, :], scalar=g, in1=f32(x_hi[:, k, :]),
                                           op0=ALU.mult, op1=ALU.subtract).then_inc(x_lo_done, 1)
            norm_add(name, n, i)

        silu_done = sem("silu_done")
        gu_done = sem("gu_done")

        def ffn_pe(up, down, norm, f):
            gemm(STAGES[up], x_tiles, x_lo_done, SPLIT0[norm], after_first=norm_steps_pe(norm))
            gemm(STAGES[down], lambda k: (gu_hi[:, k, :], gu_lo[:, k, :]), gu_lo_done, f * FT, per_tile=2)

        def ffn_act(up, down, norm, next_norm, f):
            up, down = STAGES[up], STAGES[down]
            norm_of_h_act(norm)

            def up_turn(i):
                for j in range(RING):
                    jj = j // 2
                    if j % 2 == 0:
                        ahead(unit_hi, up, i, j)
                        nc.scalar.wait_ge(pair_free[0], i * 2 + (up.freed + jj + 1))
                        nc.scalar.activation(sq[:, 0, :], sq[:, 0, :], ACT.Silu).then_inc(silu_done, 1)
                    else:
                        ahead(unit_hi, up, i, j)
                        nc.scalar.wait_ge(gu_done, i * 2 + (f * FT + jj + 1))
                        nc.scalar.activation(gu_hi[:, i * 2 + jj, :], xf[:, jj, :], ACT.Copy).then_inc(gu_hi_done, 1)

            def down_turn(i):
                for j in range(RING):
                    ahead(unit_hi, down, i, j)
                    if j % 2:
                        nc.scalar.wait_ge(pair_free[j // 2], i + (down.freed + 1))
                        if next_norm == "final":
                            norm_square(next_norm, j // 2, h[:, i * 2 + j // 2, :], i)
                        else:
                            h_tile_act(next_norm, j // 2, i)

            turns(nc.scalar, up, up_turn)
            turns(nc.scalar, down, down_turn)

        def ffn_dve(up, down, norm, next_norm, f):
            up, down = STAGES[up], STAGES[down]
            norm_of_h_dve(norm)

            def up_turn(i):
                for j in range(RING):
                    ahead(unit_lo, up, i, j)
                    jj, product = j // 2, xf[:, j // 2, :]
                    nc.vector.wait_ge(unit_done, i * RING + (up.u0 + j + 1))
                    if j % 2 == 0:
                        nc.vector.tensor_tensor(two(sq[:, 0, :]), tile_halves(0), two(rstd[:, :]),
                                                ALU.mult).then_inc(pair_free[0], 1)
                        continue
                    if not (isinstance(i, int) and f * FT + i * 2 + jj == 0):
                        nc.vector.wait_ge(gu_lo_done, i * 2 + (f * FT + jj))
                    nc.vector.tensor_tensor(two(product), tile_halves(2), two(rstd[:, :]),
                                            ALU.mult).then_inc(pair_free[1], 1)
                    nc.vector.wait_ge(pair_free[1], i * 2 + (up.freed + jj + 1))
                    nc.vector.wait_ge(silu_done, i * 2 + (f * FT + jj + 1))
                    nc.vector.tensor_tensor(product, product, sq[:, 0, :], ALU.mult).then_inc(gu_done, 1)
                    nc.vector.wait_ge(gu_hi_done, i * 2 + (f * FT + jj + 1))
                    nc.vector.tensor_tensor(gu_lo[:, i * 2 + jj, :], product, f32(gu_hi[:, i * 2 + jj, :]),
                                            ALU.subtract).then_inc(gu_lo_done, 1)

            def down_turn(i):
                for j in range(RING):
                    ahead(unit_lo, down, i, j)
                    if j % 2:
                        tile = h[:, i * 2 + j // 2, :]
                        nc.vector.wait_ge(unit_done, i * RING + (down.u0 + j + 1))
                        nc.vector.scalar_tensor_tensor(out=two(tile), in0=tile_halves(2 * (j // 2)), scalar=0.5,
                                                       in1=two(tile), op0=ALU.mult,
                                                       op1=ALU.add).then_inc(pair_free[j // 2], 1)
                        (norm_add if next_norm == "final" else h_tile_dve)(next_norm, j // 2, i)

            turns(nc.vector, up, up_turn)
            norm_clear()
            turns(nc.vector, down, down_turn)

        mix_loaded = sem("mix_loaded")
        pads_clear = sem("pads_clear")
        dt_w_hi = sem("dt_w_hi")
        dt_w_lo = sem("dt_w_lo")
        dve_step = sem("dve_step")
        act_step = sem("act_step")
        pool_step = sem("pool_step")
        rot_done = sem("rot_done")
        vs_done = sem("vs_done")
        dt_raw = sem("dt_raw")
        dt_abs = sem("dt_abs")
        dt_exp = sem("dt_exp")
        dt_one = sem("dt_one")
        dt_log = sem("dt_log")
        dt_done = sem("dt_done")
        a_exp_done = sem("a_exp_done")
        conv_done = sem("conv_done")
        xc_done = sem("xc_done")
        conv_s_sum = sem("conv_s_sum")
        last_kept = sem("last_kept")
        ret_a = sem("ret_a")
        ret_w_done = sem("ret_w_done")
        ret_b = sem("ret_b")
        ret_y = sem("ret_y")
        ret_s_done = sem("ret_s_done")
        ret_stored = sem("ret_stored")
        cum_raw = sem("cum_raw")
        cum_done = sem("cum_done")
        cum_diff = sem("cum_diff")
        decay_done = sem("decay_done")
        au_done = sem("au_done")
        ssd_a = sem("ssd_a")
        xdt_done = sem("xdt_done")
        b_tok_done = sem("b_tok_done")
        lmat_raw = sem("lmat_raw")
        lmat_done = sem("lmat_done")
        ea_done = sem("ea_done")
        ce_done = sem("ce_done")
        xdd_done = sem("xdd_done")
        ssd_sd_done = sem("ssd_sd_done")
        ssd_w_done = sem("ssd_w_done")
        ssd_b = sem("ssd_b")
        ssd_y = sem("ssd_y")
        ssd_s_done = sem("ssd_s_done")
        ssm_stored = sem("ssm_stored")
        mem_loaded = sem("mem_loaded")
        gates_done = sem("gates_done")

        RET_TABLES = 2 * HR * CH
        CDEC = [float(np.exp(np.log1p(-np.exp2(np.float64(-5.0 - i))) * CH)) for i in range(HR)]
        U_MIX = STAGES["qk"].u0
        W_QK, W_V, W_XBC, W_GZ = (STAGES[n] for n in ("qk", "v", "xbc", "gz"))
        W_XK, W_XV, W_OUT = (STAGES[n] for n in ("xk", "xv", "out"))

        class Own:

            def __init__(self, eng, s):
                self.eng, self.sem, self.n = eng, s, 0

            def do(self, ins):
                self.n += 1
                ins.then_inc(self.sem, 1)
                self.eng.wait_ge(self.sem, self.n)

        own_v, own_a, own_p = Own(nc.vector, dve_step), Own(nc.scalar, act_step), Own(nc.gpsimd, pool_step)

        def v4(ap, n=HR):
            return ap.rearrange("p (h c) -> p h c", h=n)

        def qk_dve():
            nc.vector.wait_ge(mix_loaded, 96)
            for a in range(2):
                ins = nc.vector.tensor_tensor(rope[:, a, :], rope[:, a, :], rstd[:, :], ALU.mult)
            own_v.do(ins)
            for j in range(8):
                ahead(unit_lo, W_QK, j // RING, j % RING)
                b, pr = 2 * (j % 2), j % 2
                out = q_t[:, j, :] if j < HR else k_t[:, j - HR, :]
                nc.vector.wait_ge(unit_done, W_QK.u0 + j + 1)
                if j:
                    nc.vector.wait_ge(rot_done, j)
                for lo, hi in ((0, 64), (64, 0)):
                    src = ps[hi:hi + 64, b * BANK:(b + 2) * BANK].rearrange("p (a c) -> p a c", a=2)[:, :, 0:HT]
                    nc.vector.tensor_tensor(two(xf[lo:lo + 64, 0, :]), src, two(rope[hi:hi + 64, 1, :]), ALU.mult)
                nc.vector.tensor_tensor(two(xf[:, 1, :]), tile_halves(b), two(rope[:, 0, :]),
                                        ALU.mult).then_inc(pair_free[pr], 1)
                nc.vector.wait_ge(pair_free[pr], W_QK.freed + j // 2 + 1)
                nc.vector.tensor_tensor(out, xf[:, 0, :], xf[:, 1, :], ALU.add).then_inc(rot_done, 1)

        def qk_act():
            for j in range(8):
                ahead(unit_hi, W_QK, j // RING, j % RING)

        def token_cols(t):
            return chunk(t) if t < NCH else slice(0, P)

        def v_pe():
            for pr in range(2):
                nc.tensor.wait_ge(pair_free[pr], W_V.freed)
            for j in range(4):
                nc.tensor.wait_ge(w_lo, W_V.u0 + j + 1)
                for t in range(TOKT):
                    for kk in range(2):
                        k = 2 * j + kk
                        x_h, x_l = x_hi[:, k, token_cols(t)], x_lo[:, k, token_cols(t)]
                        w_h, w_l = (w[j][:, kk * BANK:(kk + 1) * BANK] for w in (w_hi_t, w_lo_t))
                        mm = three(bank(t), x_h, x_l, w_h, w_l, k == 0, k == DT - 1)
                mm.then_inc(unit_done, 1)
            nc.tensor.wait_ge(dt_w_lo, 1)
            for t in range(TOKT):
                for k in range(DT):
                    x_h, x_l = x_hi[:, k, token_cols(t)], x_lo[:, k, token_cols(t)]
                    cut = slice(k * HS, (k + 1) * HS)
                    mm = three(bank(5, HS, t * HS), x_h, x_l, wdt_hi[:, cut], wdt_lo[:, cut], k == 0, k == DT - 1)
            mm.then_inc(dt_raw, 1)

        def v_act():
            nc.scalar.wait_ge(mix_loaded, 96)
            nc.scalar.activation(wdt_hi[:, :], wdt[:, :], ACT.Copy).then_inc(dt_w_hi, 1)
            nc.scalar.activation(a_exp[:, :], a_log, ACT.Exp).then_inc(a_exp_done, 1)
            for j in range(4):
                ahead(unit_hi, W_V, 0, j)
            nc.scalar.wait_ge(unit_done, W_V.u0 + 4)
            for t in range(NCH):
                ins = nc.scalar.activation(v_t[:, t, :], bank(t), ACT.Copy, scale=row_std[:, 1, t:t + 1])
                if t % 2:
                    ins.then_inc(pair_free[t // 2], 1)
            nc.scalar.activation(vs[:, :], bank(4, rows=NS), ACT.Copy,
                                 scale=row_std[0:NS, 1, NCH:NCH + 1]).then_inc(vs_done, 1)
            nc.scalar.wait_ge(dt_abs, 1)
            nc.scalar.activation(dt_e, dt_ab, ACT.Exp, scale=-1.0).then_inc(dt_exp, 1)
            nc.scalar.wait_ge(dt_one, 1)
            nc.scalar.activation(dt_u, dt_u, ACT.Ln).then_inc(dt_log, 1)

        def v_dve():
            nc.vector.wait_ge(dt_w_hi, 1)
            nc.vector.tensor_tensor(wdt_lo[:, :], wdt[:, :], f32(wdt_hi[:, :]), ALU.subtract).then_inc(dt_w_lo, 1)
            for j in range(4):
                ahead(unit_lo, W_V, 0, j)
            do = own_v.do

            def heads(ap):
                return ap.rearrange("p (t h) -> p t h", h=HS)

            nc.vector.wait_ge(dt_raw, 1)
            do(nc.vector.tensor_tensor(heads(dt_x), heads(bank(5, NDT)),
                                       row_std[:, 1, :].unsqueeze(2).to_broadcast([P, TOKT, HS]), ALU.mult))
            do(nc.vector.tensor_tensor(heads(dt_x), heads(dt_x),
                                       dt_bias.unsqueeze(1).to_broadcast([P, TOKT, HS]), ALU.add))
            nc.vector.scalar_tensor_tensor(out=dt_ab, in0=dt_x, scalar=-1.0, in1=dt_x, op0=ALU.mult,
                                           op1=ALU.max).then_inc(dt_abs, 1)
            nc.vector.wait_ge(dt_exp, 1)
            do(nc.vector.tensor_scalar(dt_u, dt_e, 1.0, None, ALU.add))
            do(nc.vector.tensor_scalar(dt_d, dt_u, -1.0, None, ALU.add))
            do(nc.vector.tensor_scalar(dt_m, dt_d, 0.0, None, ALU.is_equal))
            nc.vector.tensor_tensor(dt_d, dt_d, dt_m, ALU.add).then_inc(dt_one, 1)
            nc.vector.wait_ge(dt_one, 1)
            do(nc.vector.reciprocal(dt_t, dt_d))
            nc.vector.wait_ge(dt_log, 1)
            do(nc.vector.tensor_tensor(dt_u, dt_u, dt_m, ALU.add))
            do(nc.vector.tensor_tensor(dt_u, dt_u, dt_e, ALU.mult))
            do(nc.vector.tensor_tensor(dt_u, dt_u, dt_t, ALU.mult))
            do(nc.vector.scalar_tensor_tensor(out=dt_r, in0=dt_x, scalar=0.0, in1=dt_u, op0=ALU.max, op1=ALU.add))
            nc.vector.wait_ge(a_exp_done, 1)
            nc.vector.scalar_tensor_tensor(out=heads(a_dt), in0=heads(dt_r), scalar=-1.0,
                                           in1=a_exp[:, :].unsqueeze(1).to_broadcast([P, TOKT, HS]),
                                           op0=ALU.mult, op1=ALU.mult).then_inc(dt_done, 1)

        def ret_a_pe(c):
            if c == 0:
                nc.tensor.wait_ge(rot_done, 8)
                nc.tensor.wait_ge(vs_done, 1)
                nc.tensor.wait_ge(dt_abs, 1)
            else:
                nc.tensor.wait_ge(ret_w_done, c)
            for i in range(HR):
                nc.tensor.matmul(bank(4, CH, i * CH), k_t[:, i, chunk(c)], q_t[:, i, chunk(c)], start=True, stop=True)
                mm = nc.tensor.transpose(bank(5, P, i * P), k_t[:, i, chunk(c)], ident)
            mm.then_inc(ret_a, 1)

        def ret_b_pe(c):
            nc.tensor.wait_ge(ret_w_done, c + 1)
            if c:
                nc.tensor.wait_ge(ret_y, c)
                nc.tensor.wait_ge(ret_s_done, c)
            for i in range(HR):
                cut = slice(i * P, (i + 1) * P)
                nc.tensor.matmul(bank(6, CH, i * CH), v_t[:, c, cut], ret_w[:, cut], start=True, stop=c == 0)
                if c:
                    nc.tensor.matmul(bank(6, CH, i * CH), ret_s[:, (c - 1) % 2, cut], ret_qd[:, cut],
                                     start=False, stop=True)
            for i in range(HR):
                cut = slice(i * P, (i + 1) * P)
                mm = nc.tensor.matmul(bank(7, P, i * P), ret_k[:, cut], v_t[:, c, cut], start=True, stop=True)
            mm.then_inc(ret_b, 1)

        def ret_a_dve(c):
            nc.vector.wait_ge(ret_a, c + 1)
            if c:
                nc.vector.wait_ge(ret_b, c)
            nc.vector.tensor_tensor(ret_w[:, :], bank(4), c_ret[:, 0:HR * CH], ALU.mult)
            nc.vector.tensor_tensor(v4(ret_k[:, :]), v4(bank(5)),
                                    c_ret[:, RET_TABLES:RET_TABLES + HR].unsqueeze(2).to_broadcast([P, HR, P]),
                                    ALU.mult)
            nc.vector.tensor_tensor(v4(ret_qd[:, :]), q_t[:, :, chunk(c)], v4(c_ret[:, HR * CH:2 * HR * CH]),
                                    ALU.mult).then_inc(ret_w_done, 1)

        def ret_b_dve(c):
            nc.vector.wait_ge(ret_b, c + 1)
            if c == 0:
                nc.vector.tensor_copy(ret_s[:, 0, :], bank(7)).then_inc(ret_s_done, 1)
                return
            nc.vector.wait_ge(ret_s_done, c)
            for i in range(HR):
                cut = slice(i * P, (i + 1) * P)
                ins = nc.vector.scalar_tensor_tensor(out=ret_s[:, c % 2, cut], in0=ret_s[:, (c - 1) % 2, cut],
                                                     scalar=CDEC[i], in1=bank(7, P, i * P), op0=ALU.mult, op1=ALU.add)
            ins.then_inc(ret_s_done, 1)

        def ret_b_act(c):
            nc.scalar.wait_ge(ret_b, c + 1)
            nc.scalar.activation(q_t[:, :, chunk(c)], v4(bank(6)), ACT.Copy).then_inc(ret_y, 1)

        def xbc_pe():
            def after(j):
                (ret_b_pe if j % 2 else ret_a_pe)(j // 2)

            gemm(W_XBC, x_tiles, x_lo_done, SPLIT0["mix"], after=after)

        def xbc_act():
            nc.scalar.wait_ge(pads_clear, 1)

            def silu(n):
                nc.scalar.wait_ge(conv_done, n + 1)
                nc.scalar.activation(conv_tile(n)[:, NS:T], sq[:, n % 2, 0:SEQ], ACT.Silu).then_inc(xc_done, 1)

            for j in range(8):
                ahead(unit_hi, W_XBC, j // RING, j % RING)
                if j:
                    silu(j - 1)
                if j % 2:
                    ret_b_act(j // 2)
            silu(7)
            nc.scalar.wait_ge(conv_s_sum, 1)
            for n, out in enumerate((cx, cb)):
                ins = nc.scalar.activation(out[:, :, 0:NS],
                                           xf[:, 1, n * 4 * NS:(n + 1) * 4 * NS].rearrange("p (n b) -> p n b", b=NS),
                                           ACT.Silu)
            ins.then_inc(xc_done, 1)

        def xbc_dve():
            do = own_v.do
            nc.vector.wait_ge(pads_clear, 1)
            for j in range(8):
                ahead(unit_lo, W_XBC, j // RING, j % RING)
                acc = sq[:, j % 2, 0:SEQ]
                b, pr, lead = 2 * (j % 2), j % 2, TAPS - 1
                nc.vector.wait_ge(unit_done, W_XBC.u0 + j + 1)
                if j >= 2:
                    nc.vector.wait_ge(last_kept, j - 1)
                nc.vector.tensor_tensor(conv_in[:, j % 2, lead:lead + HT - NS], ps[:, b * BANK + NS:b * BANK + HT],
                                        rstd[:, NS:HT], ALU.mult)
                nc.vector.tensor_tensor(conv_in[:, j % 2, lead + HT - NS:lead + SEQ], half(b, 1), rstd[:, HT:T],
                                        ALU.mult)
                nc.vector.tensor_tensor(conv_s[:, TAPS - 1, j * NS:(j + 1) * NS], ps[:, b * BANK:b * BANK + NS],
                                        rstd[:, 0:NS], ALU.mult).then_inc(pair_free[pr], 1)
                nc.vector.wait_ge(pair_free[pr], W_XBC.freed + j // 2 + 1)
                if j >= 2:
                    nc.vector.wait_ge(xc_done, j - 1)
                do(nc.vector.tensor_scalar(acc, conv_in[:, j % 2, 0:SEQ], conv_w[:, 0, j:j + 1],
                                           conv_b[:, j:j + 1], ALU.mult, ALU.add))
                for t in range(1, TAPS):
                    ins = nc.vector.scalar_tensor_tensor(out=acc, in0=conv_in[:, j % 2, t:t + SEQ],
                                                         scalar=conv_w[:, t, j:j + 1], in1=acc,
                                                         op0=ALU.mult, op1=ALU.add)
                    if t < TAPS - 1:
                        do(ins)
                ins.then_inc(conv_done, 1)
                nc.vector.tensor_copy(conv_last[:, j, :], conv_in[:, j % 2, SEQ:SEQ + TAPS - 1]).then_inc(last_kept, 1)
                if j % 2 == 0:
                    ret_a_dve(j // 2)
                else:
                    ret_b_dve(j // 2)
            taps = xf[:, 0, 0:TAPS * 8 * NS]
            total = xf[:, 1, 0:8 * NS]
            do(nc.vector.tensor_tensor(taps.rearrange("p (x b) -> p x b", b=NS),
                                       conv_s[:, :, :].rearrange("p t (n b) -> p (t n) b", b=NS),
                                       small[:, 0:TAPS * 8].unsqueeze(2).to_broadcast([P, TAPS * 8, NS]), ALU.mult))
            do(nc.vector.tensor_reduce(total, taps.rearrange("p (t x) -> p x t", t=TAPS), AX_X, ALU.add))
            nc.vector.tensor_tensor(total.rearrange("p (n b) -> p n b", b=NS),
                                    total.rearrange("p (n b) -> p n b", b=NS),
                                    conv_b.unsqueeze(2).to_broadcast([P, 8, NS]), ALU.add).then_inc(conv_s_sum, 1)

        def cum_pe():
            nc.tensor.wait_ge(dt_done, 1)
            nc.tensor.wait_ge(ret_w_done, NCH)
            nc.tensor.matmul(bank(4, NCH * HS), upper, a_dt[:, 0:NCH * HS], start=True, stop=True)
            nc.tensor.matmul(bank(4, NCH * HS, NCH * HS), ones, a_dt[:, 0:NCH * HS],
                             start=True, stop=True).then_inc(cum_raw, 1)

        def cum_dve():
            n = NCH * HS
            nc.vector.wait_ge(cum_raw, 1)
            nc.vector.tensor_copy(a_cum[:, 0:n], bank(4, n)).then_inc(cum_done, 1)
            nc.vector.tensor_copy(decay[:, 1, :], bank(4, n, n))
            nc.vector.wait_ge(cum_done, 1)
            nc.vector.tensor_tensor(decay[:, 0, :], bank(4, n, n), a_cum[:, 0:n], ALU.subtract).then_inc(cum_diff, 1)

        def cum_act():
            nc.scalar.wait_ge(cum_diff, 1)
            nc.scalar.activation(decay[:, :, :], decay[:, :, :], ACT.Exp).then_inc(decay_done, 1)

        def ssd_a_pe(c):
            if c == 0:
                nc.tensor.wait_ge(xc_done, 9)
                nc.tensor.wait_ge(cum_diff, 1)
                nc.tensor.wait_ge(ret_y, NCH)
                nc.tensor.wait_ge(ret_s_done, NCH)
            else:
                nc.tensor.wait_ge(ssd_y, c)
                nc.tensor.wait_ge(ssd_s_done, c)
                nc.tensor.wait_ge(lmat_raw, c)
                nc.tensor.wait_ge(ea_done, c)
            nc.tensor.wait_ge(au_done, c + 1)
            for i in range(4):
                nc.tensor.transpose(bank(4, P, i * P), cx[:, i, chunk(c)], ident)
            for g in range(SG):
                nc.tensor.transpose(bank(5, P, g * P), cb[:, g, chunk(c)], ident)
            for g in range(SG):
                nc.tensor.matmul(bank(5, CH, (SG + g) * CH), cb[:, g, chunk(c)], cb[:, SG + g, chunk(c)],
                                 start=True, stop=True)
            for a in range(2):
                mm = nc.tensor.matmul(bank(6 + a), ones, ssd_au[:, a * BANK:(a + 1) * BANK], start=True, stop=True)
            mm.then_inc(ssd_a, 1)

        def ssd_b_pe(c):
            nc.tensor.wait_ge(ssd_w_done, c + 1)
            nc.tensor.wait_ge(ce_done, c + 1)
            nc.tensor.wait_ge(xdd_done, c + 1)
            nc.tensor.wait_ge(b_tok_done, c + 1)
            if c:
                nc.tensor.wait_ge(ssd_s_done, c)
            for i in range(HS):
                out = bank(4, CH, (i // 2) * CH, rows=HP, row0=HP * (i % 2))
                cut, wide = slice(i * HP, (i + 1) * HP), slice(i * CH, (i + 1) * CH)
                nc.tensor.matmul(out, xdt[:, cut], ssd_l[:, wide], start=True, stop=c == 0)
                if c:
                    nc.tensor.matmul(out, ssd_s[:, cut], ssd_e[:, wide], start=False, stop=True)
            for g in range(SG):
                mm = nc.tensor.matmul(bank(5, 4 * HP, g * 4 * HP), b_tok[:, g * P:(g + 1) * P],
                                      xdd[:, g * 4 * HP:(g + 1) * 4 * HP], start=True, stop=True)
            mm.then_inc(ssd_b, 1)

        def ssd_a_dve(c):
            heads = slice(c * HS, (c + 1) * HS)
            nc.vector.wait_ge(ssd_a, c + 1)
            if c:
                nc.vector.wait_ge(ssd_b, c)
            nc.vector.tensor_tensor(v4(xdt[:, :], HS), v4(bank(4), HS),
                                    dt_r[:, heads].unsqueeze(2).to_broadcast([P, HS, HP]),
                                    ALU.mult).then_inc(xdt_done, 1)
            nc.vector.wait_ge(ea_done, c + 1)
            for i in range(HS):
                ins = nc.vector.scalar_tensor_tensor(out=ssd_l[:, i * CH:(i + 1) * CH],
                                                     in0=ps[:, 6 * BANK + i * CH:6 * BANK + (i + 1) * CH],
                                                     scalar=a_cum[:, c * HS + i:c * HS + i + 1], in1=mask,
                                                     op0=ALU.subtract, op1=ALU.min)
            ins.then_inc(lmat_raw, 1)
            nc.vector.wait_ge(lmat_done, c + 1)
            for g in range(SG):
                w = v4(ssd_l[:, g * 4 * CH:(g + 1) * 4 * CH], 4)
                ins = nc.vector.tensor_tensor(w, bank(5, CH, (SG + g) * CH).unsqueeze(1).to_broadcast([P, 4, CH]), w,
                                              ALU.mult)
            ins.then_inc(ssd_w_done, 1)

        def ssd_b_dve(c):
            nc.vector.wait_ge(ssd_b, c + 1)
            for i in range(4):
                ins = nc.vector.scalar_tensor_tensor(out=cx[:, i, chunk(c)], in0=cx[:, i, chunk(c)],
                                                     scalar=d_skip[:, i:i + 1], in1=bank(4, CH, i * CH),
                                                     op0=ALU.mult, op1=ALU.add)
            ins.then_inc(ssd_y, 1)
            if c == 0:
                nc.vector.tensor_copy(ssd_s[:, :], bank(5)).then_inc(ssd_s_done, 1)
            else:
                nc.vector.wait_ge(ssd_sd_done, c)
                nc.vector.tensor_tensor(ssd_s[:, :], ssd_sd[:, :], bank(5), ALU.add).then_inc(ssd_s_done, 1)

        def ssd_a_act(c):
            nc.scalar.wait_ge(ssd_a, c + 1)
            if c:
                nc.scalar.wait_ge(ssd_b, c)
            nc.scalar.activation(ssd_e[:, :], ps[:, 6 * BANK:8 * BANK], ACT.Exp).then_inc(ea_done, 1)
            nc.scalar.activation(b_tok[:, :], bank(5, SG * P), ACT.Copy).then_inc(b_tok_done, 1)
            nc.scalar.wait_ge(lmat_raw, c + 1)
            nc.scalar.activation(ssd_l[:, :], ssd_l[:, :], ACT.Exp).then_inc(lmat_done, 1)

        def ssd_pool(c):
            heads = slice(c * HS, (c + 1) * HS)
            nc.gpsimd.wait_ge(ea_done, c + 1)
            for g in range(SG):
                e = v4(ssd_e[:, g * 4 * CH:(g + 1) * 4 * CH], 4)
                ins = nc.gpsimd.tensor_tensor(e, e, cb[:, SG + g, chunk(c)].unsqueeze(1).to_broadcast([P, 4, CH]),
                                              ALU.mult)
            ins.then_inc(ce_done, 1)
            nc.gpsimd.wait_ge(xdt_done, c + 1)
            if c == 0:
                nc.gpsimd.wait_ge(decay_done, 1)
            nc.gpsimd.tensor_tensor(v4(xdd[:, :], HS), v4(xdt[:, :], HS),
                                    decay[:, 0, heads].unsqueeze(2).to_broadcast([P, HS, HP]),
                                    ALU.mult).then_inc(xdd_done, 1)
            if c:
                nc.gpsimd.wait_ge(ssd_s_done, c)
                nc.gpsimd.tensor_tensor(v4(ssd_sd[:, :], HS), v4(ssd_s[:, :], HS),
                                        decay[:, 1, heads].unsqueeze(2).to_broadcast([P, HS, HP]),
                                        ALU.mult).then_inc(ssd_sd_done, 1)
            if c + 1 < NCH:
                au_pool(c + 1)

        def au_pool(c):
            if c == 0:
                nc.gpsimd.wait_ge(dt_done, 1)
                nc.gpsimd.wait_ge(ret_b, NCH)
                nc.gpsimd.wait_ge(xc_done, 9)
            else:
                nc.gpsimd.wait_ge(ssd_a, c)
            nc.gpsimd.tensor_tensor(v4(ssd_au[:, :], HS), upper.unsqueeze(1).to_broadcast([P, HS, CH]),
                                    a_dt[:, c * HS:(c + 1) * HS].unsqueeze(2).to_broadcast([P, HS, CH]),
                                    ALU.mult).then_inc(au_done, 1)

        def gz_pe():
            cum_pe()

            def after(j):
                (ssd_b_pe if j % 2 else ssd_a_pe)(j // 2)

            gemm(W_GZ, x_tiles, x_lo_done, SPLIT0["mix"], after=after)

        def gz_act():
            cum_act()
            for j in range(8):
                ahead(unit_hi, W_GZ, j // RING, j % RING)
                out = g_t[:, j, :] if j < 4 else z_t[:, j - 4, :]
                nc.scalar.wait_ge(pair_free[j % 2], W_GZ.freed + j // 2 + 1)
                nc.scalar.activation(out, out, ACT.Silu).then_inc(gates_done, 1)
                if j % 2 == 0:
                    ssd_a_act(j // 2)
                else:
                    mem_square(j - 1)
                    mem_square(j)

        def gz_dve():
            cum_dve()
            norm_clear()
            for j in range(8):
                ahead(unit_lo, W_GZ, j // RING, j % RING)
                out = g_t[:, j, :] if j < 4 else z_t[:, j - 4, :]
                nc.vector.wait_ge(unit_done, W_GZ.u0 + j + 1)
                nc.vector.tensor_tensor(two(out), tile_halves(2 * (j % 2)), two(rstd[:, :]),
                                        ALU.mult).then_inc(pair_free[j % 2], 1)
                if j % 2 == 0:
                    ssd_a_dve(j // 2)
                else:
                    norm_add("mem", j - 1)
                    norm_add("mem", j)
                    ssd_b_dve(j // 2)

        def mem_square(n):
            if n == 0:
                nc.scalar.wait_ge(mem_loaded, 16)
            norm_square("mem", n, mem_t[:, n, :])

        smp_rows = sem("smp_rows")
        ks_done = sem("ks_done")
        xdts_done = sem("xdts_done")
        a_s_exp = sem("a_s_exp")
        dm_done = sem("dm_done")
        decb_raw = sem("decb_raw")
        decb_done = sem("decb_done")
        vm_done = sem("vm_done")
        rs_loaded = [sem("rs_loaded0"), sem("rs_loaded1")]
        rs_outer = sem("rs_outer")
        rs_state = sem("rs_state")
        rs_y = sem("rs_y")
        rs_stored = [sem("rs_stored0"), sem("rs_stored1")]
        rs_r = sem("rs_r")
        xm_done = sem("xm_done")
        sm_loaded = [sem("sm_loaded0"), sem("sm_loaded1")]
        sm_decayed = sem("sm_decayed")
        sm_outer = sem("sm_outer")
        sm_state = sem("sm_state")
        sm_y = sem("sm_y")
        sm_stored = sem("sm_stored")
        sm_r = sem("sm_r")
        gn_centred = sem("gn_centred")
        gn_squared = sem("gn_squared")
        gn_rows = sem("gn_rows")
        gn_std = sem("gn_std")
        gn_inv = sem("gn_inv")
        gn_diag = sem("gn_diag")
        gn_spread = sem("gn_spread")
        gn_rstd = sem("gn_rstd")
        gn_scaled = sem("gn_scaled")
        gated = sem("gated")

        def smp_rows_pe():
            nc.tensor.wait_ge(ssd_y, NCH)
            nc.tensor.wait_ge(ssd_s_done, NCH)
            nc.tensor.wait_ge(rstd_done, NORM_AT["mem"] + 1)
            for i in range(HR):
                nc.tensor.transpose(bank(4, P, i * P, rows=NS), k_t[:, i, 0:NS], ident)
                nc.tensor.transpose(bank(5, P, i * P, rows=NS), cx[:, i, 0:NS], ident)
            for g in range(SG):
                mm = nc.tensor.transpose(bank(6, P, g * P, rows=NS), cb[:, g, 0:NS], ident)
            mm.then_inc(smp_rows, 1)

        def decb_pe():
            nc.tensor.wait_ge(dm_done, 1)
            nc.tensor.wait_ge(lmat_raw, NCH)
            nc.tensor.matmul(bank(7, NS * HS, 128), ones[0:NS, :], dm[:, :], start=True, stop=True).then_inc(decb_raw, 1)

        def smp_rows_act():
            nc.scalar.wait_ge(ssd_b, NCH)
            nc.scalar.wait_ge(ssm_stored, 16)
            nc.scalar.activation(dt_e[0:NS, 0:HS], a_dt[0:NS, NCH * HS:TOKT * HS], ACT.Exp).then_inc(a_s_exp, 1)
            nc.scalar.wait_ge(smp_rows, 1)
            nc.scalar.activation(ks[:, :], bank(4, rows=NS), ACT.Copy, scale=RK_SCALE)
            nc.scalar.activation(bs[:, :], bank(6, SG * P, rows=NS), ACT.Copy).then_inc(ks_done, 1)
            nc.scalar.wait_ge(decb_raw, 1)
            nc.scalar.activation(decb[:, :], bank(7, NS * HS, 128), ACT.Copy).then_inc(decb_done, 1)

        def smp_rows_dve():
            nc.vector.wait_ge(smp_rows, 1)
            nc.vector.tensor_tensor(v4(xdts[:, :], HS), v4(bank(5, rows=NS), HS),
                                    dt_r[0:NS, NCH * HS:TOKT * HS].unsqueeze(2).to_broadcast([NS, HS, HP]),
                                    ALU.mult).then_inc(xdts_done, 1)

        def rs_outer_pe(i):
            nc.tensor.wait_ge(ks_done, 1)
            nc.tensor.wait_ge(xdts_done, 1)
            nc.tensor.wait_ge(vm_done, i + 1)
            if i:
                nc.tensor.wait_ge(rs_state, i)
            for a in range(2):
                mm = nc.tensor.matmul(bank(4 + a), ks[:, i * P:(i + 1) * P], vm[:, i % 2, a * BANK:(a + 1) * BANK],
                                      start=True, stop=True)
            mm.then_inc(rs_outer, 1)

        def rs_y_pe(i):
            nc.tensor.wait_ge(rs_state, i + 1)
            if i == 0:
                nc.tensor.wait_ge(decb_done, 1)
            for b in range(NS):
                mm = nc.tensor.matmul(bank(7, 1, i * NS + b), st_ret[:, i % 2, b * P:(b + 1) * P],
                                      q_t[:, i, b:b + 1], start=True, stop=True)
            mm.then_inc(rs_y, 1)

        def rs_dve(i):
            nc.vector.wait_ge(rs_outer, i + 1)
            nc.vector.wait_ge(rs_loaded[i % 2], 16 * (i // 2 + 1))
            nc.vector.scalar_tensor_tensor(out=st_ret[:, i % 2, :], in0=st_ret[:, i % 2, :], scalar=GAMMA[i],
                                           in1=ps[:, 4 * BANK:6 * BANK], op0=ALU.mult, op1=ALU.add).then_inc(rs_state, 1)

        def rs_r_act():
            nc.scalar.wait_ge(rs_y, HR)
            nc.scalar.activation(q_t[:, :, 0:NS], v4(bank(7, HR * NS)), ACT.Copy).then_inc(rs_r, 1)

        def sm_outer_pe(n):
            g = n // 2
            nc.tensor.wait_ge(xm_done, n + 1)
            if n == 0:
                nc.tensor.wait_ge(rs_state, HR)
            else:
                nc.tensor.wait_ge(sm_state, n)
            for a in range(2):
                mm = nc.tensor.matmul(bank(4 + a), bs[:, g * P:(g + 1) * P],
                                      xm[:, 2 * a:2 * a + 2, :].rearrange("p b c -> p (b c)"), start=True, stop=True)
            mm.then_inc(sm_outer, 1)

        def sm_y_pe(g):
            nc.tensor.wait_ge(sm_state, 2 * g + 2)
            if g == 0:
                nc.tensor.wait_ge(rs_r, 1)
            for i in range(2):
                for b in range(NS):
                    at = b * 4 * HP + i * P
                    mm = nc.tensor.matmul(bank(7, 1, (2 * g + i) * NS + b), st_ssm[:, g, at:at + P],
                                          cb[:, SG + g, b:b + 1], start=True, stop=True)
            mm.then_inc(sm_y, 1)

        def sm_dve(n):
            g, q = n // 2, n % 2
            part = st_ssm[:, g, q * 4 * 4 * HP:(q + 1) * 4 * 4 * HP]
            nc.vector.wait_ge(sm_outer, n + 1)
            nc.vector.wait_ge(sm_decayed, g + 1)
            nc.vector.tensor_tensor(part, part, ps[:, 4 * BANK:6 * BANK], ALU.add).then_inc(sm_state, 1)

        def sm_r_dve():
            nc.vector.wait_ge(sm_y, SG)
            for i in range(4):
                ins = nc.vector.scalar_tensor_tensor(out=cx[:, i, 0:NS], in0=cx[:, i, 0:NS], scalar=d_skip[:, i:i + 1],
                                                     in1=bank(7, NS, i * NS), op0=ALU.mult, op1=ALU.add)
            ins.then_inc(sm_r, 1)

        eye_s = ident[0:NS, 0:NS]

        def smp_pool():
            def values(i):
                if i >= 2:
                    nc.gpsimd.wait_ge(rs_outer, i - 1)
                nc.gpsimd.tensor_tensor(vm[:, i % 2, :].rearrange("p (b c) -> p b c", b=NS),
                                        vs[:, i * P:(i + 1) * P].unsqueeze(1).to_broadcast([NS, NS, P]),
                                        eye_s.unsqueeze(2).to_broadcast([NS, NS, P]), ALU.mult).then_inc(vm_done, 1)

            def load_ret(i):
                if i >= 2:
                    nc.gpsimd.wait_ge(rs_stored[i % 2], 16 * (i // 2))
                    nc.gpsimd.wait_ge(rs_y, i - 1)
                nc.gpsimd.dma_start(st_ret[:, i % 2, :], A["st_ret"][i]).then_inc(rs_loaded[i % 2], 16)

            def store_ret(i):
                nc.gpsimd.wait_ge(rs_state, i + 1)
                nc.gpsimd.dma_start(A["o_ret_s"][i], st_ret[:, i % 2, :]).then_inc(rs_stored[i % 2], 16)

            def products(n):
                g, q = n // 2, n % 2
                if n:
                    nc.gpsimd.wait_ge(sm_outer, n)
                nc.gpsimd.tensor_tensor(xm[:, :, :],
                                        xdts[:, g * 4 * HP:(g + 1) * 4 * HP].unsqueeze(1).to_broadcast([NS, 4, 4 * HP]),
                                        eye_s[:, 4 * q:4 * q + 4].unsqueeze(2).to_broadcast([NS, 4, 4 * HP]),
                                        ALU.mult).then_inc(xm_done, 1)

            nc.gpsimd.wait_ge(vs_done, 1)
            nc.gpsimd.wait_ge(ssd_b, NCH)
            load_ret(0)
            load_ret(1)
            values(0)
            nc.gpsimd.wait_ge(a_s_exp, 1)
            nc.gpsimd.tensor_tensor(dm[:, :].rearrange("p (b h) -> p b h", b=NS),
                                    dt_e[0:NS, 0:HS].unsqueeze(1).to_broadcast([NS, NS, HS]),
                                    eye_s.unsqueeze(2).to_broadcast([NS, NS, HS]), ALU.mult).then_inc(dm_done, 1)
            values(1)
            nc.gpsimd.wait_ge(xdts_done, 1)
            products(0)
            for i in range(HR):
                store_ret(i)
                if i + 2 < HR:
                    values(i + 2)
                    load_ret(i + 2)
            nc.gpsimd.wait_ge(decb_done, 1)
            for par in range(2):
                nc.gpsimd.wait_ge(rs_stored[par], 32)
            nc.gpsimd.wait_ge(rs_y, HR)
            for g in range(SG):
                nc.gpsimd.dma_start(st_ssm[:, g, :], A["st_ssm"][g]).then_inc(sm_loaded[g], 16)
            for g in range(SG):
                nc.gpsimd.wait_ge(sm_loaded[g], 16)
                nc.gpsimd.tensor_tensor(st_ssm[:, g, :].rearrange("p (b h c) -> p b h c", b=NS, h=4),
                                        st_ssm[:, g, :].rearrange("p (b h c) -> p b h c", b=NS, h=4),
                                        decb[:, :].rearrange("p (b h) -> p b h", b=NS)[:, :, 4 * g:4 * g + 4]
                                        .unsqueeze(3).to_broadcast([P, NS, 4, HP]), ALU.mult).then_inc(sm_decayed, 1)
            for n in range(1, 4):
                products(n)
            for g in range(SG):
                nc.gpsimd.wait_ge(sm_state, 2 * g + 2)
                nc.gpsimd.dma_start(A["o_ssm_s"][g], st_ssm[:, g, :]).then_inc(sm_stored, 16)

        def gn_centre_pe(i):
            b = 4 + 2 * (i % 2)
            if i == 0:
                nc.tensor.wait_ge(rs_r, 1)
                nc.tensor.wait_ge(sm_state, 4)
            elif i == 1:
                nc.tensor.wait_ge(sm_r, 1)
            else:
                nc.tensor.wait_ge(gn_squared, i - 1)
            for a in range(2):
                mm = nc.tensor.matmul(half(b, a), centre, q_t[:, i, a * HT:(a + 1) * HT], start=True, stop=True)
            mm.then_inc(gn_centred, 1)

        def gn_act(i):
            nc.scalar.wait_ge(gn_centred, i + 1)
            if i == 0:
                nc.scalar.wait_ge(rs_outer, HR)
                nc.scalar.wait_ge(sm_outer, 4)
            b = 4 + 2 * (i % 2)
            nc.scalar.activation(two(q_t[:, i, :]), tile_halves(b), ACT.Copy)
            nc.scalar.activation(two(gn_s[:, i, :]), tile_halves(b), ACT.Square).then_inc(gn_squared, 1)

        def gn_rows_pe():
            nc.tensor.wait_ge(gn_squared, HR)
            for i in range(HR):
                for t, (c0, _, _) in enumerate(row_tiles(T)):
                    mm = nc.tensor.matmul(bank(6, 1, i * TOKT + t), gn_s[:, i, c0:c0 + P], inv_p,
                                          start=True, stop=True)
            mm.then_inc(gn_rows, 1)

        def gn_rows_act():
            nc.scalar.wait_ge(gn_rows, 1)
            nc.scalar.activation(gn_r[:, 0, :], bank(6, HR * TOKT), ACT.Sqrt, bias=eps).then_inc(gn_std, 1)

        def gn_rows_dve():
            nc.vector.wait_ge(gn_std, 1)
            nc.vector.reciprocal(gn_r[:, 1, :], gn_r[:, 0, :]).then_inc(gn_inv, 1)
            nc.vector.wait_ge(gn_inv, 1)

        def gn_diag_dve(i):
            if i:
                nc.vector.wait_ge(gn_spread, i)
            nc.vector.tensor_tensor(diag, ident.unsqueeze(1).to_broadcast([P, TOKT, P]),
                                    gn_r[:, 1, i * TOKT:(i + 1) * TOKT].unsqueeze(2).to_broadcast([P, TOKT, P]),
                                    ALU.mult).then_inc(gn_diag, 1)

        def gn_spread_pe(i):
            nc.tensor.wait_ge(gn_diag, i + 1)
            b = 4 + 2 * (i % 2)
            if i >= 2:
                nc.tensor.wait_ge(gn_scaled, i - 1)
            if i == 1:
                nc.tensor.wait_ge(gn_std, 1)
            for t, (_, n, to) in enumerate(row_tiles(T)):
                mm = nc.tensor.matmul(ps[:, b * BANK + to:b * BANK + to + n], ones, diag[:, t, 0:n],
                                      start=True, stop=True)
            mm.then_inc(gn_spread, 1)

        def gn_scale_dve(i):
            nc.vector.wait_ge(gn_spread, i + 1)
            b = 4 + 2 * (i % 2)
            nc.vector.tensor_tensor(q_t[:, i, 0:NS], q_t[:, i, 0:NS], bank(b + 1, NS), ALU.mult)
            nc.vector.tensor_tensor(q_t[:, i, NS:T], q_t[:, i, NS:T], bank(b), ALU.mult).then_inc(gn_scaled, 1)

        def ret_make(k, out):
            return nc.vector.scalar_tensor_tensor(out=out, in0=q_t[:, k, :], scalar=gain("ret", k), in1=g_t[:, k, :],
                                                  op0=ALU.mult, op1=ALU.mult)

        def mem_tiles(k):
            return m_tile(x_hi, k), m_tile(x_lo, k)

        def slots(engine):
            steps = {n: [] for n in range(16)}

            def put(n, name, f):
                if name == engine:
                    steps[n].append(f)

            put(0, "pe", lambda: norm_rows_pe("mem", inv_d))
            put(1, "pe", lambda: norm_spread_pe("mem"))
            put(1, "act", smp_rows_act)
            put(1, "dve", smp_rows_dve)
            put(1, "pe", smp_rows_pe)
            put(1, "pe", decb_pe)
            for i in range(HR):
                put(i + 2, "pe", lambda i=i: rs_outer_pe(i))
                put(i + 2, "dve", lambda i=i: rs_dve(i))
                put(i + 3, "pe", lambda i=i: rs_y_pe(i))
            put(6, "act", rs_r_act)
            for n in range(4):
                put(n + 7, "pe", lambda n=n: sm_outer_pe(n))
                put(n + 7, "dve", lambda n=n: sm_dve(n))
            put(9, "pe", lambda: sm_y_pe(0))
            put(11, "pe", lambda: sm_y_pe(1))
            put(11, "dve", sm_r_dve)
            for i in range(HR):
                put(i + 12, "pe", lambda i=i: gn_centre_pe(i))
                put(i + 12, "act", lambda i=i: gn_act(i))
            return steps

        def xkv_pe():
            steps = slots("pe")

            def after(j):
                for f in steps[j]:
                    f()

            gemm(W_XK, mem_tiles, x_lo_done, SPLIT0["mem"], width=MEM, after=after)
            for pr in range(2):
                nc.tensor.wait_ge(pair_free[pr], W_XV.freed)
            for k in range(8):
                nc.tensor.wait_ge(w_lo, W_XV.u0 + k + 1)
                m_h, m_l = mem_tiles(k)
                for mt in range(MT):
                    for a in range(2):
                        cut, wide = slice(mt * P, (mt + 1) * P), slice(a * BANK, (a + 1) * BANK)
                        mm = three(bank(2 * mt + a), m_h[:, cut], m_l[:, cut], w_hi_t[k % RING][:, wide],
                                   w_lo_t[k % RING][:, wide], k == 0, k == 7)
                mm.then_inc(unit_done, 1)
                after(8 + k)
            gn_rows_pe()
            for i in range(HR):
                gn_spread_pe(i)
            nc.tensor.wait_ge(gn_scaled, HR)
            norm_rows_pe("ssd", inv_512)
            norm_spread_pe("ssd")

        def xkv_act():
            nc.scalar.wait_ge(unit_done, W_XK.u0)
            for k in range(8):
                gained_hi("mem", k, mem_t[:, k, :], m_tile(x_hi, k))
            for pr in range(2):
                nc.scalar.wait_ge(pair_free[pr], W_XK.freed)
            norm_rows_act("mem")
            norm_rstd_act("mem")
            steps = slots("act")
            for j in range(8):
                ahead(unit_hi, W_XK, j // RING, j % RING)
                for f in steps[j]:
                    f()
            for j in range(8):
                ahead(unit_hi, W_XV, j // RING, j % RING)
                for f in steps[8 + j]:
                    f()
            nc.scalar.wait_ge(unit_done, W_XV.u0 + 8)
            for mt in range(MT):
                nc.scalar.activation(mem_v[:, mt, :], ps[:, 2 * mt * BANK:(2 * mt + 2) * BANK],
                                     ACT.Copy, scale=row_std[:, 1, mt:mt + 1]).then_inc(pair_free[mt], 1)
            gn_rows_act()
            nc.scalar.wait_ge(sm_stored, 32)
            nc.scalar.wait_ge(sm_y, SG)
            made_hi_act("ret", lambda k: ret_hi[:, k, :])
            nc.scalar.wait_ge(gated, 1)
            for n in range(4):
                if n:
                    nc.scalar.wait_ge(gated, n + 1)
                norm_square("ssd", n, cx[:, n, :])
            norm_rows_act("ssd")
            norm_rstd_act("ssd")
            made_hi_act("ssd", lambda k: ssd_hi[:, k, :])

        def xkv_dve():
            for k in range(8):
                gained_lo("mem", k, mem_t[:, k, :], m_tile(x_hi, k), m_tile(x_lo, k), SPLIT0["mem"] + k + 1)
            norm_diag_dve("mem")
            nc.vector.wait_ge(rstd_done, NORM_AT["mem"] + 1)
            steps = slots("dve")
            for j in range(16):
                st = W_XK if j < 8 else W_XV
                ahead(unit_lo, st, (j % 8) // RING, j % RING)
                if j < 8:
                    nc.vector.wait_ge(unit_done, W_XK.u0 + j + 1)
                    nc.vector.wait_ge(x_lo_done, SPLIT0["mem"] + 8)
                    nc.vector.tensor_tensor(mem_k[:, j, :], bank(2 * (j % 2), MEM), rstd[:, 0:MEM],
                                            ALU.mult).then_inc(pair_free[j % 2], 1)
                for f in steps[j]:
                    f()
            gn_rows_dve()
            gn_diag_dve(0)
            for i in range(HR):
                if i + 1 < HR:
                    gn_diag_dve(i + 1)
                gn_scale_dve(i)
            nc.vector.wait_ge(gn_scaled, HR)
            made_dve("ret", ret_make, lambda k: ret_hi[:, k, :], lambda k: ret_lo[:, k, :])
            norm_clear()
            nc.vector.wait_ge(sm_r, 1)
            for n in range(4):
                nc.vector.tensor_tensor(cx[:, n, :], cx[:, n, :], z_t[:, n, :], ALU.mult).then_inc(gated, 1)
            for n in range(4):
                norm_add("ssd", n)
            norm_diag_dve("ssd")
            nc.vector.wait_ge(rstd_done, NORM_AT["ssd"] + 1)
            made_dve("ssd", normed("ssd", lambda k: cx[:, k, :]), lambda k: ssd_hi[:, k, :],
                      lambda k: ssd_lo[:, k, :])

        def out_tiles(k):
            if k < 4:
                return ret_hi[:, k, :], ret_lo[:, k, :]
            return ssd_hi[:, k - 4, :], ssd_lo[:, k - 4, :]

        def residual_pe(stage, operand, ready, ready0):
            gemm(stage, operand, ready, ready0)

        def residual_act(stage, next_norm):
            for j in range(8):
                ahead(unit_hi, stage, j // RING, j % RING)
                nc.scalar.wait_ge(pair_free[j % 2], stage.freed + j // 2 + 1)
                h_tile_act(next_norm, j)

        def residual_dve(stage, next_norm):
            norm_clear()
            for j in range(8):
                ahead(unit_lo, stage, j // RING, j % RING)
                nc.vector.wait_ge(unit_done, stage.u0 + j + 1)
                nc.vector.tensor_tensor(two(h[:, j, :]), two(h[:, j, :]), tile_halves(2 * (j % 2)),
                                        ALU.add).then_inc(pair_free[j % 2], 1)
                h_tile_dve(next_norm, j)

        qx_done = sem("qx_done")
        mem_stored = sem("mem_stored")
        sc_done = sem("sc_done")
        mx_done = sem("mx_done")
        ex_done = sem("ex_done")
        pr_done = sem("pr_done")
        pt_done = sem("pt_done")
        at_done = sem("at_done")
        at_done2 = sem("at_done2")
        o_done = sem("o_done")
        o_hi = sem("o_hi")
        o_lo = sem("o_lo")
        cache_loaded = [sem(f"cache_loaded{i}") for i in range(3)]
        cache_used = sem("cache_used")
        ssc_done = sem("ssc_done")
        srow_done = sem("srow_done")
        smx_done = sem("smx_done")
        sex_done = sem("sex_done")
        spr_done = sem("spr_done")
        spt_done = sem("spt_done")
        sat_done = sem("sat_done")
        so_done = sem("so_done")
        so_hi = sem("so_hi")
        so_lo = sem("so_lo")
        W_XQ, W_XO = STAGES["xq"], STAGES["xo"]
        NROW = NS * XH

        def xq_act():
            for j in range(8):
                ahead(unit_hi, W_XQ, j // RING, j % RING)

        def xq_dve():
            for j in range(8):
                ahead(unit_lo, W_XQ, j // RING, j % RING)
                nc.vector.wait_ge(unit_done, W_XQ.u0 + j + 1)
                nc.vector.tensor_tensor(two(qx(j)), tile_halves(2 * (j % 2)), two(rstd[:, :]),
                                        ALU.mult).then_inc(pair_free[j % 2], 1)

        def score_pe(c):
            b = 4 + 2 * (c % 2)
            if c == 0:
                for pr in range(2):
                    nc.tensor.wait_ge(pair_free[pr], W_XO.freed)
            if c >= 2:
                nc.tensor.wait_ge(ex_done, c - 1)
            for i in range(XH):
                out = ps[:, b * BANK + i * MEM:b * BANK + (i + 1) * MEM]
                for d in range(2):
                    mm = nc.tensor.matmul(out, qx(2 * i + d)[:, chunk(c)], mem_k[:, 2 * i + d, :],
                                          start=d == 0, stop=d == 1)
            mm.then_inc(sc_done, 1)

        def att_stats(c):
            return (att_s[:, c % 2, i * XH:(i + 1) * XH] for i in range(3))

        def softmax_dve(c):
            mx, total, inv = att_stats(c)
            b = 4 + 2 * (c % 2)
            nc.vector.wait_ge(sc_done, c + 1)
            own_v.do(nc.vector.tensor_reduce(mx, ps[:, b * BANK:(b + 2) * BANK].rearrange("p (i m) -> p i m", i=XH),
                                             AX_X, ALU.max))
            nc.vector.tensor_scalar(mx, mx, -X_SCALE, None, ALU.mult).then_inc(mx_done, 1)

        def softmax_act(c):
            mx, total, inv = att_stats(c)
            b = 4 + 2 * (c % 2)
            nc.scalar.wait_ge(mx_done, c + 1)
            if c >= 2:
                nc.scalar.wait_ge(pt_done, c - 1)
            for i in range(XH):
                ins = nc.scalar.activation(att_p[:, c % 2, i * MEM:(i + 1) * MEM],
                                           ps[:, b * BANK + i * MEM:b * BANK + (i + 1) * MEM], ACT.Exp,
                                           bias=mx[:, i:i + 1], scale=X_SCALE, accum_out=total[:, i:i + 1])
            ins.then_inc(ex_done, 1)

        def probs_dve(c):
            mx, total, inv = att_stats(c)
            nc.vector.wait_ge(ex_done, c + 1)
            own_v.do(nc.vector.reciprocal(inv, total))
            p = v4(att_p[:, c % 2, :])
            nc.vector.tensor_tensor(p, p, inv.unsqueeze(2).to_broadcast([P, XH, MEM]), ALU.mult).then_inc(pr_done, 1)

        def turn_pe(c):
            b = 2 * (c % 2)
            nc.tensor.wait_ge(pr_done, c + 1)
            if c < 2:
                nc.tensor.wait_ge(pair_free[c % 2], W_XQ.freed + 4)
            else:
                nc.tensor.wait_ge(at_done, c - 1)
                nc.tensor.wait_ge(at_done2, c - 1)
            for i in range(XH):
                for m in range(MT):
                    mm = nc.tensor.transpose(bank(b + m, P, i * P), att_p[:, c % 2, i * MEM + m * P:i * MEM + (m + 1) * P],
                                             ident)
            mm.then_inc(pt_done, 1)

        def turned_act(c):
            nc.scalar.wait_ge(pt_done, c + 1)
            nc.scalar.activation(att_0[:, :, c * CH:(c + 1) * CH], v4(bank(2 * (c % 2))), ACT.Copy).then_inc(at_done, 1)

        def turned_dve(c):
            nc.vector.wait_ge(pt_done, c + 1)
            nc.vector.tensor_copy(att_1[:, :, c * CH:(c + 1) * CH], v4(bank(2 * (c % 2) + 1))).then_inc(at_done2, 1)

        def o_pe(n):
            i, d = n // 2, n % 2
            b = n % 4
            if n == 0:
                nc.tensor.wait_ge(at_done, NCH)
                nc.tensor.wait_ge(at_done2, NCH)
            if n >= 4:
                nc.tensor.wait_ge(o_lo, n - 3)
            for m, att in enumerate((att_0, att_1)):
                mm = nc.tensor.matmul(bank(b), mem_v[:, m, n * P:(n + 1) * P], att[:, i, :],
                                      start=m == 0, stop=m == 1)
            mm.then_inc(o_done, 1)

        def o_act(n):
            nc.scalar.wait_ge(o_done, n + 1)
            nc.scalar.activation(o_tiles(n)[0][:, NS:T], bank(n % 4), ACT.Copy).then_inc(o_hi, 1)

        def o_dve(n):
            nc.vector.wait_ge(o_hi, n + 1)
            hi, lo = o_tiles(n)
            nc.vector.tensor_tensor(lo[:, NS:T], bank(n % 4), f32(hi[:, NS:T]), ALU.subtract).then_inc(o_lo, 1)

        def cache_pool():
            nc.gpsimd.wait_ge(unit_done, W_OUT.u0 + 8)
            nc.gpsimd.wait_ge(sm_stored, 32)
            nc.gpsimd.wait_ge(sm_y, SG)
            for n in range(2 * NS):
                if n >= 3:
                    nc.gpsimd.wait_ge(cache_used, n - 2)
                nc.gpsimd.dma_start(cache[:, n % 3, :], A["cache"][n]).then_inc(cache_loaded[n % 3], 16)

        def s_keys_pe(b):
            nc.tensor.wait_ge(cache_loaded[b % 3], 16 * (b // 3 + 1))
            if b == 0:
                nc.tensor.wait_ge(ex_done, NCH)
            for i in range(XH):
                for m in range(MT):
                    for d in range(2):
                        at = (2 * i + d) * MEM + m * P
                        mm = nc.tensor.matmul(bank(6 + m, 1, b * XH + i), cache[:, b % 3, at:at + P],
                                              qx(2 * i + d)[:, b:b + 1], start=d == 0, stop=d == 1)
            mm.then_inc(cache_used, 1)

        def s_softmax_pe():
            nc.tensor.wait_ge(ssc_done, 1)
            for m in range(MT):
                mm = nc.tensor.transpose(bank(5, P, m * P, rows=NROW), att_c[:, 0, m * NROW:(m + 1) * NROW], ident)
            mm.then_inc(srow_done, 1)

        def s_turn_pe():
            nc.tensor.wait_ge(spr_done, 1)
            for m in range(MT):
                mm = nc.tensor.transpose(bank(6, NROW, m * NROW), s_rows[:, m * P:(m + 1) * P], ident[0:NROW, 0:NROW])
            mm.then_inc(spt_done, 1)

        def s_softmax_dve():
            nc.vector.wait_ge(cache_used, NS)
            nc.vector.tensor_copy(att_c[:, 0, 0:NROW], bank(6, NROW))
            nc.vector.tensor_copy(att_c[:, 0, NROW:2 * NROW], bank(7, NROW)).then_inc(ssc_done, 1)
            nc.vector.wait_ge(srow_done, 1)
            own_v.do(nc.vector.tensor_reduce(s_stat[:, 0:1], bank(5, MEM, rows=NROW), AX_X, ALU.max))
            nc.vector.tensor_scalar(s_stat[:, 0:1], s_stat[:, 0:1], -X_SCALE, None, ALU.mult).then_inc(smx_done, 1)
            nc.vector.wait_ge(sex_done, 1)
            own_v.do(nc.vector.reciprocal(s_stat[:, 2:3], s_stat[:, 1:2]))
            nc.vector.tensor_scalar(s_rows[:, :], s_rows[:, :], s_stat[:, 2:3], None, ALU.mult).then_inc(spr_done, 1)

        def s_turned_dve():
            nc.vector.wait_ge(spt_done, 1)
            nc.vector.tensor_copy(att_c[:, 1, :], bank(6, 2 * NROW)).then_inc(sat_done, 1)

        def s_softmax_act():
            nc.scalar.wait_ge(smx_done, 1)
            nc.scalar.activation(s_rows[:, :], bank(5, MEM, rows=NROW), ACT.Exp, bias=s_stat[:, 0:1], scale=X_SCALE,
                                 accum_out=s_stat[:, 1:2]).then_inc(sex_done, 1)

        def s_values_pe(b):
            n = NS + b
            nc.tensor.wait_ge(cache_loaded[n % 3], 16 * (n // 3 + 1))
            if b == 0:
                nc.tensor.wait_ge(sat_done, 1)
            for t in range(8):
                for m in range(MT):
                    at = m * D + t * P
                    mm = nc.tensor.matmul(bank(7, 1, t * NS + b), cache[:, n % 3, at:at + P],
                                          att_c[:, 1, m * NROW + b * XH + t // 2:m * NROW + b * XH + t // 2 + 1],
                                          start=m == 0, stop=m == 1)
            mm.then_inc(cache_used, 1)

        def so_act():
            nc.scalar.wait_ge(cache_used, 2 * NS)
            for a, hi in enumerate((oa_hi, ob_hi)):
                ins = nc.scalar.activation(hi[:, :, 0:NS], v4(bank(7, 4 * NS, a * 4 * NS)), ACT.Copy)
            ins.then_inc(so_hi, 1)

        def so_dve():
            nc.vector.wait_ge(so_hi, 1)
            for a, (hi, lo) in enumerate(((oa_hi, oa_lo), (ob_hi, ob_lo))):
                ins = nc.vector.tensor_tensor(lo[:, :, 0:NS], v4(bank(7, 4 * NS, a * 4 * NS)), f32(hi[:, :, 0:NS]),
                                              ALU.subtract)
            ins.then_inc(so_lo, 1)

        def att_pe():
            for c in range(NCH):
                score_pe(c)
                if c:
                    turn_pe(c - 1)
            turn_pe(NCH - 1)
            for b in range(NS):
                s_keys_pe(b)
            s_softmax_pe()
            for n in range(8):
                o_pe(n)
            s_turn_pe()
            for b in range(NS):
                s_values_pe(b)
            nc.tensor.wait_ge(so_lo, 1)

        def att_act():
            for c in range(NCH):
                softmax_act(c)
                if c:
                    turned_act(c - 1)
            turned_act(NCH - 1)
            s_softmax_act()
            for n in range(8):
                o_act(n)
            so_act()

        def att_dve():
            nc.vector.wait_ge(cache_loaded[0], 16)
            for c in range(NCH):
                softmax_dve(c)
                if c:
                    turned_dve(c - 1)
                probs_dve(c)
            turned_dve(NCH - 1)
            s_softmax_dve()
            for n in range(8):
                o_dve(n)
            s_turned_dve()
            so_dve()

        def final_dve():
            norm_diag_dve("final")
            nc.vector.wait_ge(rstd_done, NORM_AT["final"] + 1)
            nc.vector.wait_ge(unit_done, UNITS)
            for k in range(DT):
                normed("final", lambda k: h[:, k, :])(k, y_out[:, k, :]).then_inc(xf_done, 1)


        LAST_UNIT = [UNITS if len(PLAN) == 4 else STAGES[{"ffn1": "qk", "mix": "xq", "xattn": "up2"}[PLAN[-1]]].u0]
        block = ctx.enter_context(nc.Block())

        def load_unit(v, j, src, cols, first=False):
            if not first:
                nc.sync.wait_ge(w_lo, v - RAW + 1)
            nc.sync.dma_start(w_raw[j % RAW][:, 0:cols], src).then_inc(w_loaded[j % RAW], 16)

        @block.sync
        def _(sp):
            sp.dma_start(gains[:, :], A["gains"]).then_inc(consts_loaded, 16)
            sp.dma_start(h[:, 0:2, :], A["xT"][:, 0:2, :]).then_inc(h_loaded[0], 16)
            for name, st in STAGES.items():
                if st.u0 >= LAST_UNIT[0]:
                    break
                src = A["w_" + name]
                head = RAW if st.u0 == 0 else 0
                for n in range(head):
                    load_unit(n, n, src[n], st.cols, first=True)
                    if n == 0:
                        for q in range(1, 4):
                            sp.dma_start(h[:, 2 * q:2 * q + 2, :], A["xT"][:, 2 * q:2 * q + 2, :]).then_inc(h_loaded[q], 16)
                    else:
                        sp.dma_start(square[:, :], A["c_square"]).then_inc(consts_loaded, 16)
                with sp.Fori(head // 2, st.units // 2) as i:
                    for j in range(2):
                        load_unit(i * 2 + (st.u0 + j), (st.u0 + j) % 2,
                                  src[bass.ds(i * 2 + j, 1)].rearrange("o p c -> (o p) c"), st.cols)
            r = NORM_AT["final"]
            if len(PLAN) == 4:
                for k in range(0, DT, 2):
                    sp.wait_ge(xf_done, MADE0["final"] + k + 2)
                    sp.dma_start(A["o_y"][:, k:k + 2, :], y_out[:, k:k + 2, :]).then_inc(y_stored, 16)
                sp.wait_ge(y_stored, 16 * (DT // 2))

        @block.scalar
        def _(act):
            act.sem_inc(pair_free[0], 1)
            act.sem_inc(pair_free[1], 1)
            act.wait_ge(consts_loaded, 32)
            split_first(0)
            for n in range(DT):
                if n % 2 == 0:
                    act.wait_ge(h_loaded[n // 2], 16)
                h_tile_act("ffn1", n)
                if n in (0, 4):
                    split_first(1 + n // 4)
            ffn_act("up1", "down1", "ffn1", "mix", 0)
            if len(PLAN) > 1:
                norm_of_h_act("mix")
                qk_act()
                v_act()
                xbc_act()
                gz_act()
                xkv_act()
                residual_act(W_OUT, "x")
            if len(PLAN) > 2:
                norm_of_h_act("x")
                xq_act()
                att_act()
                residual_act(W_XO, "ffn2")
            if len(PLAN) > 3:
                act.wait_ge(mem_stored, 32)
                ffn_act("up2", "down2", "ffn2", "final", 1)
                norm_rows_act("final")
                norm_rstd_act("final")

        @block.vector
        def _(dve):
            norm_clear()
            dve.wait_ge(consts_loaded, 32)
            unit_lo(0, 0, UNIT_COLS[0])
            for n in range(DT):
                h_tile_dve("ffn1", n)
                if n in (0, 4):
                    unit_lo(1 + n // 4, 1 + n // 4, UNIT_COLS[1])
            ffn_dve("up1", "down1", "ffn1", "mix", 0)
            if len(PLAN) > 1:
                norm_of_h_dve("mix")
                qk_dve()
                v_dve()
                xbc_dve()
                gz_dve()
                xkv_dve()
                residual_dve(W_OUT, "x")
            if len(PLAN) > 2:
                norm_of_h_dve("x")
                xq_dve()
                att_dve()
                residual_dve(W_XO, "ffn2")
            if len(PLAN) > 3:
                dve.wait_ge(mem_stored, 32)
                ffn_dve("up2", "down2", "ffn2", "final", 1)
                final_dve()

        @block.tensor
        def _(pe):
            pe.wait_ge(consts_loaded, 32)
            ffn_pe("up1", "down1", "ffn1", 0)
            if len(PLAN) > 1:
                gemm(W_QK, x_tiles, x_lo_done, SPLIT0["mix"], after_first=norm_steps_pe("mix"))
                v_pe()
                xbc_pe()
                gz_pe()
                xkv_pe()
                gemm(W_OUT, out_tiles, x_lo_done, SPLIT0["ret"])
            if len(PLAN) > 2:
                gemm(W_XQ, x_tiles, x_lo_done, SPLIT0["x"], after_first=norm_steps_pe("x"))
                att_pe()
                gemm(W_XO, o_tiles, o_lo, 0)
            if len(PLAN) > 3:
                ffn_pe("up2", "down2", "ffn2", 1)
                norm_rows_pe("final", inv_d)
                norm_spread_pe("final")

        @block.gpsimd
        def _(pool):
            if len(PLAN) > 1:
                pool.wait_ge(unit_done, U_MIX)
                for dst, src in ((rope[:, :, :], "c_rope"), (c_ret[:, :], "c_ret"), (triangle[:, :], "c_triangle"),
                                 (small[:, :], "small"), (wdt[:, :], "wdt"), (conv_s[:, 0:TAPS - 1, :], "conv_s")):
                    pool.dma_start(dst, A[src]).then_inc(mix_loaded, 16)
                nc.gpsimd.memset(conv_in[:, :, 0:TAPS - 1], 0.0).then_inc(pads_clear, 1)
                pool.wait_ge(ret_s_done, NCH)
                pool.dma_start(A["o_ret_p"], ret_s[:, (NCH - 1) % 2, :]).then_inc(ret_stored, 16)
                pool.wait_ge(ret_stored, 16)
                pool.dma_start(mem_t[:, :, :], A["memT"]).then_inc(mem_loaded, 16)
                au_pool(0)
                for c in range(NCH):
                    ssd_pool(c)
                pool.wait_ge(ssd_s_done, NCH)
                pool.dma_start(A["o_ssm_p"], ssd_s[:, :]).then_inc(ssm_stored, 16)
                pool.wait_ge(ssm_stored, 16)
                pool.wait_ge(conv_s_sum, 1)
                pool.dma_start(A["o_conv_p"], conv_last[:, :, :]).then_inc(ssm_stored, 16)
                pool.dma_start(A["o_conv_s"], conv_s[:, 1:TAPS, :]).then_inc(ssm_stored, 16)
                smp_pool()
                pool.wait_ge(rs_loaded[0], 32)
            if len(PLAN) > 2:
                pool.wait_ge(unit_done, W_XK.u0 + 8)
                for pr in range(2):
                    pool.wait_ge(pair_free[pr], W_XV.freed)
                pool.dma_start(A["o_mem_k"], mem_k[:, :, :]).then_inc(mem_stored, 16)
                for pr in range(2):
                    pool.wait_ge(pair_free[pr], W_OUT.freed)
                pool.dma_start(A["o_mem_v"], mem_v[:, :, :]).then_inc(mem_stored, 16)
                cache_pool()
                pool.wait_ge(ssm_stored, 48)
                pool.wait_ge(sm_stored, 32)
                pool.wait_ge(mem_stored, 32)


def tiled(w):
    k, n = w.shape
    return w.reshape(k // P, P, n // P, P).transpose(2, 1, 0, 3).reshape(n // P, P, -1)


def feature_major(x):
    return x.T.reshape(-1, P, x.shape[0]).transpose(1, 0, 2)


def columns(v):
    return v.reshape(-1, P).T


def lay_out(i):
    i = {k: np.asarray(v) for k, v in i.items()}
    a = dict(tables())
    cat = np.concatenate
    a["xT"] = feature_major(cat([i["x_sample"][:, 0], i["x_prompt"][0]], 0))
    a["gains"] = cat([columns(i[n].reshape(-1)) for n in
                      ("ffn1_norm", "mem_norm", "mix_norm", "x_norm", "ffn2_norm", "final_norm", "ret_gn_gain",
                       "ssd_norm")], 1)
    for f in ("1", "2"):
        up = [tiled(i[f"ffn{f}_w{w}"][0]) for w in ("1", "3")]
        a["w_up" + f] = np.stack(up, 1).reshape(2 * FT, P, -1)
        down = i[f"ffn{f}_w2"][0].reshape(2, KH, P, DT, P)
        a["w_down" + f] = down.transpose(3, 0, 2, 1, 4).reshape(2 * DT, P, -1)
    w_in = i["w_in"][0]
    a["w_qk"] = tiled(w_in[:, 0:1024])
    a["w_v"] = w_in[:, 1024:1536].reshape(4, 2, P, 512).transpose(0, 2, 1, 3).reshape(4, P, 1024)
    a["w_gz"] = tiled(w_in[:, 1536:2560])
    a["w_xbc"] = tiled(w_in[:, 2560:3584])
    a["wdt"] = w_in[:, 3584:].reshape(DT, P, HS).transpose(1, 0, 2).reshape(P, DT * HS)
    a["small"] = cat([i["conv_w"][0].reshape(TAPS, 8, P).transpose(2, 0, 1).reshape(P, TAPS * 8),
                      columns(i["conv_b"][0]), np.broadcast_to(i["dt_bias"][0], (P, HS)),
                      np.broadcast_to(i["A_log"][0], (P, HS)),
                      columns(np.repeat(i["D_skip"][0], HP))], 1)
    a["conv_s"] = i["state_conv"][0].reshape(NS, TAPS - 1, 8, P).transpose(3, 1, 2, 0).reshape(P, TAPS - 1, 8 * NS)
    a["memT"] = feature_major(i["mem_prompt"][0])
    a["w_out"] = tiled(i["w_out"][0])
    a["w_xk"], a["w_xq"], a["w_xo"] = tiled(i["w_xk"][0]), tiled(i["w_xq"][0]), tiled(i["w_xo"][0])
    a["w_xv"] = i["w_xv"][0].reshape(8, P, D)
    a["st_ret"] = i["state_ret"][0].transpose(1, 2, 0, 3).reshape(HR, P, NS * P)
    a["st_ssm"] = i["state_ssm"][0].reshape(NS, SG, 4, HP, P).transpose(1, 4, 0, 2, 3).reshape(SG, P, -1)
    keys = i["cache_mem_k"][0].reshape(NS, MEM, DT, P).transpose(0, 3, 2, 1).reshape(NS, P, DT * MEM)
    values = i["cache_mem_v"][0].reshape(NS, MT, P, D).transpose(0, 2, 1, 3).reshape(NS, P, MT * D)
    a["cache"] = cat([keys, values], 0)
    return a


OUTS = {"o_y": (P, DT, T), "o_ret_p": (P, HR * P), "o_ssm_p": (P, HS * HP), "o_conv_p": (P, 8, TAPS - 1),
        "o_conv_s": (P, TAPS - 1, 8 * NS), "o_ret_s": (HR, P, NS * P), "o_ssm_s": (SG, P, NS * 4 * HP),
        "o_mem_k": (P, DT, MEM), "o_mem_v": (P, MT, D)}


def give(r):
    y = r["o_y"].transpose(2, 1, 0).reshape(T, D)
    return (y[NS:].reshape(1, SEQ, D), y[:NS].reshape(NS, 1, D),
            r["o_ret_p"].reshape(P, HR, P).transpose(1, 0, 2)[None, None],
            r["o_ssm_p"].reshape(P, HS, HP).transpose(1, 2, 0)[None, None],
            r["o_conv_p"].transpose(2, 1, 0).reshape(1, 1, TAPS - 1, D),
            r["o_mem_k"].transpose(2, 1, 0).reshape(1, 1, MEM, XH, D // XH),
            r["o_mem_v"].transpose(1, 0, 2).reshape(1, 1, MEM, XH, D // XH),
            r["o_ret_s"].reshape(HR, P, NS, P).transpose(2, 0, 1, 3)[None],
            r["o_ssm_s"].reshape(SG, P, NS, 4, HP).transpose(2, 0, 3, 4, 1).reshape(1, NS, HS, HP, P),
            r["o_conv_s"].reshape(P, TAPS - 1, 8, NS).transpose(3, 1, 2, 0).reshape(1, NS, TAPS - 1, D))


def kernel(**inputs):
    import numpy as _np
    import concourse.bacc as _bacc
    from concourse.bass_utils import run_bass_kernel_spmd as _run

    nc = _bacc.Bacc("TRN2", target_bir_lowering=False, num_devices=1)
    arrays = {"in_" + n: _np.ascontiguousarray(a) for n, a in lay_out(inputs).items()}
    A = {n[3:]: nc.dram_tensor(n, a.shape, F32, kind="ExternalInput").ap() for n, a in arrays.items()}
    for n, shape in OUTS.items():
        A[n] = nc.dram_tensor(n, shape, F32, kind="ExternalOutput").ap()
    build(nc, A)
    r = _run(nc, [arrays], core_ids=[0]).results[0]
    return give(r)
```

```python
from contextlib import ExitStack

import numpy as np

import concourse.bass as bass
from concourse import mybir

F32 = mybir.dt.float32
F32R = mybir.dt.float32r
ALU = mybir.AluOpType
ACT = mybir.ActivationFunctionType
AX_X = mybir.AxisListType.X

P = 128
D = 1024
DT = D // P
SEQ = 512
NS = 8
T = NS + SEQ
HT = T // 2
BANK = 512
FF = 2816
FT = FF // P
KH = FT // 2
HR = 4
HS = 8
HP = 64
SG = 2
CH = 128
NCH = SEQ // CH
MEM = 256
MT = MEM // P
XH = 4
TAPS = 4
EPS = 1e-6
RK_SCALE = 128.0 ** -0.5
X_SCALE = 256.0 ** -0.5
NEG = -1.0e30
TOKT = 5
LEAD = 3
RING = 4
RAW = 2
GAMMA = [float(np.exp(np.log1p(-np.exp2(np.float64(-5.0 - h))))) for h in range(HR)]

STAGE_LIST = [
    ("up1", 2 * FT, 1024, FT),
    ("down1", 2 * DT, KH * P, DT // 2),
    ("qk", 8, 1024, 4),
    ("v", 4, 1024, 1),
    ("xbc", 8, 1024, 4),
    ("gz", 8, 1024, 4),
    ("xk", 8, 1024, 4),
    ("xv", 8, 1024, 1),
    ("out", 8, 1024, 4),
    ("xq", 8, 1024, 4),
    ("xo", 8, 1024, 4),
    ("up2", 2 * FT, 1024, FT),
    ("down2", 2 * DT, KH * P, DT // 2),
]

NORM_LIST = [("ffn1", 8, T), ("mix", 8, T), ("mem", 8, MEM), ("ssd", 5, T), ("x", 8, T), ("ffn2", 8, T),
             ("final", 8, T)]
SPLIT_LIST = [("ffn1", 8), ("mix", 8), ("mem", 8), ("ret", 4), ("ssd", 4), ("x", 8), ("ffn2", 8)]
MADE_LIST = [("ret", 4), ("ssd", 4), ("final", 8)]


class Stage:

    def __init__(self, name, units, cols, u0, freed):
        self.name, self.units, self.cols, self.u0, self.freed = name, units, cols, u0, freed
        self.loops = units // RING


def make_stages():
    out, u0, freed = {}, 0, 1
    for name, units, cols, tiles in STAGE_LIST:
        out[name] = Stage(name, units, cols, u0, freed)
        u0, freed = u0 + units, freed + tiles
    return out, u0


def starts(items, extra):
    out, at = {}, 0
    for it in items:
        out[it[0]] = at
        at += it[1] + extra
    return out


STAGES, UNITS = make_stages()
UNIT_COLS = [s.cols for s in STAGES.values() for _ in range(s.units)]
NORM_AT = {n[0]: i for i, n in enumerate(NORM_LIST)}
NORM_TILES = {n[0]: n[1] for n in NORM_LIST}
NORM_COLS = {n[0]: n[2] for n in NORM_LIST}
SQ0 = starts(NORM_LIST, 1)
SPLIT0 = starts(SPLIT_LIST, 0)
SPLIT_TILES = dict(SPLIT_LIST)
MADE0 = starts(MADE_LIST, 0)


def tables():
    half = 64
    inv = (10000.0 ** (-np.arange(half, dtype=np.float32) / np.float32(half))).astype(np.float32)
    pos = np.concatenate([np.full(NS, 4096.0), np.arange(SEQ)]).astype(np.float32)
    ang = (inv[:, None] * pos[None, :]).astype(np.float32)
    c, s = np.cos(ang), np.sin(ang)
    rope = np.stack([np.concatenate([c, c]), np.concatenate([s, -s])], 1)
    log_g = np.log1p(-np.exp2(-5.0 - np.arange(HR)))
    i = np.arange(CH)
    diff = i[None, :] - i[:, None]
    dmat = np.where(diff >= 0, np.exp(log_g[:, None, None] * np.maximum(diff, 0)), 0.0) * RK_SCALE
    q_dec = np.exp(log_g[:, None] * (i[None, :] + 1.0))
    k_dec = np.exp(log_g[None, :] * (CH - 1.0 - i[:, None])) * RK_SCALE
    ret = np.concatenate([dmat.transpose(1, 0, 2).reshape(P, -1),
                          np.broadcast_to(q_dec.reshape(1, -1), (P, HR * CH)), k_dec], 1)
    eye = np.eye(P)
    upper = (diff >= 0).astype(np.float32)
    mask = np.where(diff >= 0, 0.0, NEG)
    small = np.zeros((P, 8))
    small[:, 0], small[:, 1], small[:, 2], small[:, 3] = 1 / D, 1 / 512, 1 / P, EPS
    square = np.concatenate([eye, np.ones((P, P)), small], 1)
    triangle = np.concatenate([eye - 1.0 / P, upper, mask], 1)
    f = lambda a: np.ascontiguousarray(a, dtype=np.float32)
    own_column = np.broadcast_to(np.eye(NS).reshape(1, -1), (P, NS * NS))
    smp = np.concatenate([own_column, np.broadcast_to(np.eye(HR).reshape(1, -1) / P, (P, HR * HR))], 1)
    return {"c_smp": f(smp), "c_rope": f(rope), "c_ret": f(ret), "c_square": f(square), "c_triangle": f(triangle)}


def build(nc, A, PLAN=("ffn1", "mix", "xattn", "ffn2")):
    ctx = ExitStack()
    with ctx:
        def sb(name, shape, dt=F32, stack=ctx):
            return stack.enter_context(nc.sbuf_tensor(name, shape, dt))

        def sem(name):
            return ctx.enter_context(nc.semaphore(name))

        ps = ctx.enter_context(nc.psum_tensor("ps", [P, 8 * BANK], F32))

        def bank(b, n=BANK, at=0, rows=P, row0=0):
            return ps[row0:row0 + rows, b * BANK + at:b * BANK + at + n]

        def half(b, x):
            return ps[:, (b + x) * BANK:(b + x) * BANK + HT]

        def tile_halves(b):
            return ps[:, b * BANK:(b + 2) * BANK].rearrange("p (a c) -> p a c", a=2)[:, :, 0:HT]

        def two(ap):
            return ap.rearrange("p (a c) -> p a c", a=2)

        def f32(ap):
            return ap.bitcast(F32)

        h = sb("h", [P, DT, T])
        x_hi = sb("x_hi", [P, DT, T], F32R)
        x_lo = sb("x_lo", [P, DT, T], F32R)
        w_raw = [sb(f"w_raw{i}", [P, KH * P]) for i in range(RAW)]
        w_hi_t = [sb(f"w_hi{i}", [P, KH * P], F32R) for i in range(RING)]
        w_lo_t = [sb(f"w_lo{i}", [P, KH * P], F32R) for i in range(RING)]
        gains = sb("gains", [P, 6 * DT + HR + HR])
        square = sb("square", [P, 2 * P + 8])
        xf = sb("xf", [P, 2, T])
        sq = sb("sq", [P, 2, T])
        sq_sum = sb("sq_sum", [P, T])
        rstd = sb("rstd", [P, T])
        row_std = sb("row_std", [P, 2, TOKT + MT])
        diag = sq[:, :, :].rearrange("p a c -> p (a c)")[:, 0:TOKT * P].rearrange("p (t c) -> p t c", t=TOKT)
        ident, ones = (square[:, i * P:(i + 1) * P] for i in range(2))
        inv_d, inv_512, inv_p, eps = (square[:, 2 * P + i:2 * P + i + 1] for i in range(4))
        GAIN0 = {"ffn1": 0, "mem": 8, "mix": 16, "x": 24, "ffn2": 32, "final": 40, "ret": 48, "ssd": 52}

        def gain(name, k):
            return gains[:, GAIN0[name] + k:GAIN0[name] + k + 1]

        ffn = ExitStack()
        gu_hi = sb("gu_hi", [P, FT, T], F32R, ffn)
        gu_lo = sb("gu_lo", [P, FT, T], F32R, ffn)
        ffn.close()

        mix = ExitStack()

        def region(name, cols, *groups):
            out = []
            for g in groups:
                part = ExitStack()
                out += [sb(n, shape, F32R if n.endswith("_hi") or n.endswith("_lo") else F32, part)
                        for n, shape in g]
                part.close()
            sb("hold_" + name, [P, cols], F32, mix)
            return out

        HT4 = 4 * T
        q_t, att_p, oa_lo = region("q", HT4, [("q_t", [P, HR, T])], [("att_p", [P, 2, XH * MEM])],
                           [("oa_lo", [P, 4, T])])
        k_t, gn_s, mem_v = region("k", HT4, [("k_t", [P, HR, T])], [("gn_s", [P, HR, T])], [("mem_v", [P, MT, D])])
        cx, qx_a, oa_hi = region("cx", HT4, [("cx", [P, 4, T])], [("qx_a", [P, 4, T])], [("oa_hi", [P, 4, T])])
        cb, ssd_hi, qx_b, ob_hi = region("cb", HT4, [("cb", [P, 4, T])], [("ssd_hi", [P, 4, T])],
                                         [("qx_b", [P, 4, T])], [("ob_hi", [P, 4, T])])
        g_t, ret_lo, pick_q_hi, qr_hi, qr_lo, att_0 = region("g", HT4, [("g_t", [P, HR, T])],
                                                             [("ret_lo", [P, HR, T])],
                                                             [("pick_q_hi", [NS, NS, P]), ("qr_hi", [NS, 2 * P]),
                                                              ("qr_lo", [NS, 2 * P])],
                                                             [("att_0", [P, XH, SEQ])])
        z_t, ssd_lo, att_1 = region("z", HT4, [("z_t", [P, 4, T])], [("ssd_lo", [P, 4, T])],
                                    [("att_1", [P, XH, SEQ])])
        ret_s, c_ret, mem_t, mem_k, ob_lo = region("h", HT4,
                                            [("ret_s", [P, 2, HR * P]), ("c_ret", [P, 2 * HR * CH + HR])],
                                            [("mem_t", [P, 8, MEM])], [("mem_k", [P, 8, MEM])],
                                            [("ob_lo", [P, 4, T])])
        (v_t, ret_w, ret_k, ret_qd, rope, conv_in,
         ssd_au, ssd_l, ssd_e, xdt, xdd, b_tok, ssd_s, ssd_sd,
         ks, xdts, bs, dm, decb, xm, st_ret, vm,
         _pad, st_ssm,
         ret_hi,
         cache, s_rows, s_stat, y_out) = region("scratch", 6528,
                         [("v_t", [P, NCH, HR * P]), ("ret_w", [P, HR * CH]), ("ret_k", [P, HR * P]),
                          ("ret_qd", [P, HR * CH]), ("rope", [P, 2, T]), ("conv_in", [P, 2, SEQ + TAPS - 1])],
                         [("ssd_au", [P, HS * CH]), ("ssd_l", [P, HS * CH]), ("ssd_e", [P, HS * CH]),
                          ("xdt", [P, HS * HP]), ("xdd", [P, HS * HP]), ("b_tok", [P, SG * P]),
                          ("ssd_s", [P, HS * HP]), ("ssd_sd", [P, HS * HP])],
                         [("ks", [NS, HR * P]), ("xdts", [NS, HS * HP]), ("bs", [NS, SG * P]),
                          ("dm", [NS, NS * HS]), ("decb", [P, NS * HS]), ("xm", [NS, 4, 4 * HP]),
                          ("st_ret", [P, 2, NS * P]), ("vm", [NS, 2, NS * P])],
                         [("pad_small", [P, 2432]), ("st_ssm", [P, 2, NS * 4 * HP])],
                         [("ret_hi", [P, HR, T])],
                         [("cache", [P, 3, 2048]), ("s_rows", [NS * XH, MEM]), ("s_stat", [NS * XH, 4])],
                         [("y_out", [P, DT, T])])
        vs = sb("vs", [NS, HR * P], F32, mix)
        triangle = sb("triangle", [P, 3 * P], F32, mix)
        centre, upper, mask = (triangle[:, i * P:(i + 1) * P] for i in range(3))
        small = sb("small", [P, TAPS * 8 + 8 + 8 + 8 + 4], F32, mix)
        conv_w = small[:, 0:TAPS * 8].rearrange("p (t n) -> p t n", t=TAPS)
        conv_b, dt_bias, a_log, d_skip = small[:, 32:40], small[:, 40:48], small[:, 48:56], small[:, 56:60]
        conv_s = sb("conv_s", [P, TAPS, 8 * NS], F32, mix)
        conv_last = sb("conv_last", [P, 8, TAPS - 1], F32, mix)
        wdt = sb("wdt", [P, DT * HS], F32, mix)
        wdt_hi = sb("wdt_hi", [P, DT * HS], F32R, mix)
        wdt_lo = sb("wdt_lo", [P, DT * HS], F32R, mix)
        NDT = TOKT * HS
        dts = sb("dts", [P, 10, NDT], F32, mix)
        dt_x, dt_ab, dt_e, dt_u, dt_d, dt_m, dt_t, a_dt, dt_r, a_cum = (dts[:, i, :] for i in range(10))
        a_exp = sb("a_exp", [P, HS], F32, mix)
        decay = sb("decay", [P, 2, NCH * HS], F32, mix)
        att_s = sb("att_s", [P, 2, 3 * XH], F32, mix)
        att_c = sb("att_c", [P, 2, 4 * NS * 2], F32, mix)

        def chunk(c):
            return slice(NS + c * CH, NS + (c + 1) * CH)

        def conv_tile(n):
            return cx[:, n, :] if n < 4 else cb[:, n - 4, :]

        def qx(n):
            return qx_a[:, n, :] if n < 4 else qx_b[:, n - 4, :]

        def o_tiles(n):
            return (oa_hi[:, n, :], oa_lo[:, n, :]) if n < 4 else (ob_hi[:, n - 4, :], ob_lo[:, n - 4, :])

        def flat(t):
            return t[:, :, :].rearrange("p k c -> p (k c)")

        def m_tile(t, k):
            return flat(t)[:, k * MEM:(k + 1) * MEM]

        y_rows = cb[0:NS, 0, NS:T]
        q_mask, c_mask = cb[:, 1, NS:NS + HR * NS * NS], cb[:, 1, NS + HR * NS * NS:NS + (HR + SG) * NS * NS]
        gn_inv, gn_inv_s = cb[0:HR, 2, NS:T], cb[0:HR, 3, NS:2 * NS]
        c_smp = cb[:, 3, 2 * NS:2 * NS + NS * NS + HR * HR]
        own_column, pick_mean = c_smp[:, 0:NS * NS], c_smp[:, NS * NS:NS * NS + HR * HR]

        pick_h = flat(x_hi)[0:HR, DT * MEM:DT * MEM + HR * P].rearrange("p (h c) -> p h c", h=HR)
        inv_hi, inv_lo = (flat(t)[0:HR, DT * MEM + HR * P:DT * MEM + HR * P + T] for t in (x_hi, x_lo))

        pick_r = flat(x_hi)[0:NS * XH, 0:NS * XH * P].rearrange("p (r c) -> p r c", r=NS * XH)
        sr_hi, sr_lo = (flat(x_lo)[0:NS * XH, i * MEM:(i + 1) * MEM] for i in range(2))

        mix.close()

        gains_loaded = sem("gains_loaded")
        square_loaded = sem("square_loaded")
        h_loaded = [sem(f"h_loaded{i}") for i in range(4)]
        w_loaded = [sem(f"w_loaded{i}") for i in range(RAW)]
        w_hi = sem("w_hi")
        w_lo = sem("w_lo")
        unit_done = sem("unit_done")
        pair_free = [sem("pair0_free"), sem("pair1_free")]
        gu_hi_done = sem("gu_hi_done")
        gu_lo_done = sem("gu_lo_done")
        sq_done = sem("sq_done")
        sq_added = sem("sq_added")
        rows_done = sem("rows_done")
        row_std_done = sem("row_std_done")
        row_inv_done = sem("row_inv_done")
        diag_done = sem("diag_done")
        spread_done = sem("spread_done")
        rstd_done = sem("rstd_done")
        xf_done = sem("xf_done")
        x_hi_done = sem("x_hi_done")
        x_lo_done = sem("x_lo_done")
        y_stored = sem("y_stored")

        def cols_of(v, stage, dynamic):
            return stage.cols if dynamic else UNIT_COLS[v]

        def unit_hi(v, j, cols):
            nc.scalar.wait_ge(w_loaded[j % RAW], w_load_count(v, j))
            nc.scalar.wait_ge(unit_done, v - RING + 1)
            nc.scalar.activation(w_hi_t[j][:, 0:cols], w_raw[j % RAW][:, 0:cols], ACT.Copy).then_inc(w_hi, 1)

        def w_load_count(v, j):
            if isinstance(v, int):
                return 16 * (v // 2 + 1)
            return (v - j) * 8 + 16 * (j // 2 + 1)

        def unit_lo(v, j, cols):
            nc.vector.wait_ge(w_hi, v + 1)
            nc.vector.tensor_tensor(w_lo_t[j][:, 0:cols], w_raw[j % RAW][:, 0:cols], f32(w_hi_t[j][:, 0:cols]),
                                    ALU.subtract).then_inc(w_lo, 1)

        def ahead(split, stage, i, j):
            if isinstance(i, int):
                v = stage.u0 + RING * i + j + LEAD
                if v < LAST_UNIT[0]:
                    if v < RING and split is unit_hi:
                        split_first(v)
                    else:
                        split(v, v % RING, UNIT_COLS[v])
            else:
                split(i * RING + (stage.u0 + j + LEAD), (j + LEAD) % RING, stage.cols)

        def split_first(v):
            nc.scalar.wait_ge(w_loaded[v % RAW], 16 * (v // RAW + 1))
            nc.scalar.activation(w_hi_t[v][:, 0:UNIT_COLS[v]], w_raw[v % RAW][:, 0:UNIT_COLS[v]],
                                 ACT.Copy).then_inc(w_hi, 1)

        def turns(eng, stage, body):
            first = 1 if stage.u0 == 0 else 0
            if stage.loops > 2:
                if first:
                    body(0)
                with eng.Fori(first, stage.loops - 1) as i:
                    body(i)
                body(stage.loops - 1)
            else:
                for i in range(stage.loops):
                    body(i)

        def three(out, w_h, w_l, m_h, m_l, start, stop):
            nc.tensor.matmul(out, w_h, m_l, start=start, stop=False)
            nc.tensor.matmul(out, w_l, m_h, start=False, stop=False)
            return nc.tensor.matmul(out, w_h, m_h, start=False, stop=stop)

        def tile_products(slot, blocks, b, operand, k0, first, last, width=T, ready=None, within=None):
            n = width // 2 if width > BANK else width
            mm = None
            for kk in range(blocks):
                if ready:
                    nc.tensor.wait_ge(ready[0], ready[1] + k0 + kk + 1)
                w_h, w_l = (w[slot][:, kk * P:(kk + 1) * P] for w in (w_hi_t, w_lo_t))
                m_h, m_l = operand(k0 + kk)
                s, e = first and kk == 0, last and kk == blocks - 1
                for a in range(width // n):
                    cut = slice(a * n, (a + 1) * n)
                    mm = three(ps[:, (b + a) * BANK:(b + a) * BANK + n], w_h, w_l, m_h[:, cut], m_l[:, cut], s, e)
                if within and kk == blocks // 2:
                    within()
            return mm

        def gemm(stage, operand, ready, ready0, per_tile=1, width=T, after=None, norm=None):
            blocks = stage.cols // P

            def turn(i, norm=None):
                for j in range(RING):
                    u = i * RING + (stage.u0 + j)
                    tile = j // per_tile
                    b = 2 * (tile % 2)
                    first, last = j % per_tile == 0, j % per_tile == per_tile - 1
                    nc.tensor.wait_ge(w_lo, u + 1)
                    if first:
                        nc.tensor.wait_ge(pair_free[tile % 2],
                                          i * (RING // per_tile // 2) + (stage.freed + tile // 2))
                    tile_products(j, blocks, b, operand, (j % per_tile) * blocks, first, last, width,
                                  (ready, ready0) if tile == 0 else None,
                                  (lambda: norm_spread_pe(norm)) if norm and j == 1 else None).then_inc(unit_done, 1)
                    if norm and j == 0:
                        norm_rows_pe(norm, inv_d)
                    if after:
                        after(i * RING + j)

            if after:
                for i in range(stage.loops):
                    turn(i, norm if i == 0 else None)
            elif norm:
                turn(0, norm)
                with nc.tensor.Fori(1, stage.loops) as i:
                    turn(i)
            else:
                with nc.tensor.Fori(0, stage.loops) as i:
                    turn(i)

        def norm_clear(eng=nc.vector):
            eng.memset(sq_sum[:, :], 0.0).then_inc(sq_added, 1)

        def norm_square(name, n, source, i=None):
            w = NORM_COLS[name]
            nc.scalar.wait_ge(sq_added, SQ0[name] + n if i is None else i * 2 + (SQ0[name] + n))
            nc.scalar.activation(sq[:, n % 2, 0:w], source, ACT.Square).then_inc(sq_done, 1)

        SQD0 = starts(NORM_LIST, 0)

        def norm_add(name, n, i=None, eng=nc.vector):
            w = NORM_COLS[name]
            a, b = SQD0[name] + n + 1, SQ0[name] + n + 1
            eng.wait_ge(sq_done, a if i is None else i * 2 + a)
            eng.wait_ge(sq_added, b if i is None else i * 2 + b)
            eng.tensor_tensor(sq_sum[:, 0:w], sq_sum[:, 0:w], sq[:, n % 2, 0:w],
                                    ALU.add).then_inc(sq_added, 1)

        def row_tiles(w):
            if w == MEM:
                return [(t * P, P, t * P) for t in range(MT)]
            return [(NS + c * CH, CH, c * CH) for c in range(NCH)] + [(0, NS, SEQ)]

        def norm_rows_pe(name, inv_n):
            w, r = NORM_COLS[name], NORM_AT[name]
            nc.tensor.wait_ge(sq_added, SQ0[name] + NORM_TILES[name] + 1)
            for t, (c0, _, _) in enumerate(row_tiles(w)):
                mm = nc.tensor.matmul(bank(6, 1, t), sq_sum[:, c0:c0 + P], inv_n, start=True, stop=True)
            mm.then_inc(rows_done, 1)

        def row_parts(name):
            n, at = len(row_tiles(NORM_COLS[name])), TOKT if name == "mem" else 0
            return row_std[:, 0, at:at + n], row_std[:, 1, at:at + n], n

        def norm_rows_act(name):
            root, _, n = row_parts(name)
            nc.scalar.wait_ge(rows_done, NORM_AT[name] + 1)
            nc.scalar.activation(root, bank(6, n), ACT.Sqrt, bias=eps).then_inc(row_std_done, 1)

        def norm_diag_dve(name):
            root, inv, n = row_parts(name)
            r = NORM_AT[name]
            nc.vector.wait_ge(row_std_done, r + 1)
            nc.vector.reciprocal(inv, root).then_inc(row_inv_done, 1)
            nc.vector.wait_ge(row_inv_done, r + 1)
            nc.vector.tensor_tensor(diag[:, 0:n, :], ident.unsqueeze(1).to_broadcast([P, n, P]),
                                    inv.unsqueeze(2).to_broadcast([P, n, P]),
                                    ALU.mult).then_inc(diag_done, 1)

        def norm_spread_pe(name):
            nc.tensor.wait_ge(diag_done, NORM_AT[name] + 1)
            for t, (_, n, to) in enumerate(row_tiles(NORM_COLS[name])):
                mm = nc.tensor.matmul(ps[:, 4 * BANK + to:4 * BANK + to + n], ones, diag[:, t, 0:n],
                                      start=True, stop=True)
            mm.then_inc(spread_done, 1)

        def norm_rstd_act(name):
            w = NORM_COLS[name]
            nc.scalar.wait_ge(spread_done, NORM_AT[name] + 1)
            lead = w % P
            if lead:
                nc.scalar.activation(rstd[:, 0:lead], ps[:, 5 * BANK:5 * BANK + lead], ACT.Copy)
            nc.scalar.activation(rstd[:, lead:w], ps[:, 4 * BANK:4 * BANK + w - lead], ACT.Copy).then_inc(rstd_done, 1)


        def gained_hi(name, k, source, dest):
            nc.scalar.activation(dest, source, ACT.Copy, scale=gain(name, k)).then_inc(x_hi_done, 1)

        def gained_lo(name, k, source, hi, dest, count):
            nc.vector.wait_ge(x_hi_done, count)
            nc.vector.scalar_tensor_tensor(out=dest, in0=source, scalar=gain(name, k), in1=f32(hi), op0=ALU.mult,
                                           op1=ALU.subtract).then_inc(x_lo_done, 1)

        def made_hi_act(name, dest):
            for k in range(SPLIT_TILES[name]):
                nc.scalar.wait_ge(xf_done, MADE0[name] + k + 1)
                nc.scalar.activation(dest(k), xf[:, k % 2, :], ACT.Copy).then_inc(x_hi_done, 1)

        def made_dve(name, make, dest_hi, dest_lo):
            s0, n = SPLIT0[name], SPLIT_TILES[name]
            for k in range(n + 1):
                if k < n:
                    nc.vector.wait_ge(x_lo_done, s0 + k - 1)
                    make(k, xf[:, k % 2, :]).then_inc(xf_done, 1)
                if k:
                    nc.vector.wait_ge(x_hi_done, s0 + k)
                    nc.vector.tensor_tensor(dest_lo(k - 1), xf[:, (k - 1) % 2, :], f32(dest_hi(k - 1)),
                                            ALU.subtract).then_inc(x_lo_done, 1)

        def normed(name, source, w=T):
            def make(k, out):
                return nc.vector.scalar_tensor_tensor(out=out, in0=source(k), scalar=gain(name, k),
                                                      in1=rstd[:, 0:w], op0=ALU.mult, op1=ALU.mult)
            return make

        def x_tiles(k):
            return x_hi[:, k, :], x_lo[:, k, :]

        def norm_of_h_act(name):
            norm_rows_act(name)
            norm_rstd_act(name)

        def norm_of_h_dve(name):
            norm_diag_dve(name)
            nc.vector.wait_ge(rstd_done, NORM_AT[name] + 1)

        def h_tile_act(name, n, i=None):
            k = n if i is None else i * 2 + n
            norm_square(name, n, h[:, k, :], i)
            if isinstance(k, int):
                nc.scalar.activation(x_hi[:, k, :], h[:, k, :], ACT.Copy, scale=gain(name, k)).then_inc(x_hi_done, 1)
            else:
                nc.scalar.activation(x_hi[:, k, :], h[:, k, :], ACT.Copy,
                                     scale=gains[:, bass.ds(k + GAIN0[name], 1)]).then_inc(x_hi_done, 1)

        def h_tile_dve(name, n, i=None):
            k = n if i is None else i * 2 + n
            g = gain(name, k) if isinstance(k, int) else gains[:, bass.ds(k + GAIN0[name], 1)]
            nc.vector.wait_ge(x_hi_done, k + (SPLIT0[name] + 1))
            nc.vector.scalar_tensor_tensor(out=x_lo[:, k, :], in0=h[:, k, :], scalar=g, in1=f32(x_hi[:, k, :]),
                                           op0=ALU.mult, op1=ALU.subtract).then_inc(x_lo_done, 1)
            norm_add(name, n, i)

        silu_done = sem("silu_done")
        gu_done = sem("gu_done")

        def ffn_pe(up, down, norm, f):
            gemm(STAGES[up], x_tiles, x_lo_done, SPLIT0[norm], norm=norm)
            gemm(STAGES[down], lambda k: (gu_hi[:, k, :], gu_lo[:, k, :]), gu_lo_done, f * FT, per_tile=2)

        def ffn_act(up, down, norm, next_norm, f):
            up, down = STAGES[up], STAGES[down]
            norm_of_h_act(norm)

            def up_turn(i):
                for j in range(RING):
                    jj = j // 2
                    if j % 2 == 0:
                        ahead(unit_hi, up, i, j)
                        nc.scalar.wait_ge(pair_free[0], i * 2 + (up.freed + jj + 1))
                        nc.scalar.activation(sq[:, 0, :], sq[:, 0, :], ACT.Silu).then_inc(silu_done, 1)
                    else:
                        ahead(unit_hi, up, i, j)
                        nc.scalar.wait_ge(gu_done, i * 2 + (f * FT + jj + 1))
                        nc.scalar.activation(gu_hi[:, i * 2 + jj, :], xf[:, jj, :], ACT.Copy).then_inc(gu_hi_done, 1)

            def down_turn(i):
                for j in range(RING):
                    ahead(unit_hi, down, i, j)
                    if j % 2:
                        nc.scalar.wait_ge(pair_free[j // 2], i + (down.freed + 1))
                        if next_norm == "final":
                            norm_square(next_norm, j // 2, h[:, i * 2 + j // 2, :], i)
                        else:
                            h_tile_act(next_norm, j // 2, i)

            turns(nc.scalar, up, up_turn)
            turns(nc.scalar, down, down_turn)

        def ffn_dve(up, down, norm, next_norm, f):
            up, down = STAGES[up], STAGES[down]
            norm_of_h_dve(norm)

            def up_turn(i):
                for j in range(RING):
                    ahead(unit_lo, up, i, j)
                    jj, product = j // 2, xf[:, j // 2, :]
                    nc.vector.wait_ge(unit_done, i * RING + (up.u0 + j + 1))
                    if j % 2 == 0:
                        nc.vector.tensor_tensor(two(sq[:, 0, :]), tile_halves(0), two(rstd[:, :]),
                                                ALU.mult).then_inc(pair_free[0], 1)
                        continue
                    if not (isinstance(i, int) and f * FT + i * 2 + jj == 0):
                        nc.vector.wait_ge(gu_lo_done, i * 2 + (f * FT + jj))
                    nc.vector.tensor_tensor(two(product), tile_halves(2), two(rstd[:, :]),
                                            ALU.mult).then_inc(pair_free[1], 1)
                    nc.vector.wait_ge(pair_free[1], i * 2 + (up.freed + jj + 1))
                    nc.vector.wait_ge(silu_done, i * 2 + (f * FT + jj + 1))
                    nc.vector.tensor_tensor(product, product, sq[:, 0, :], ALU.mult).then_inc(gu_done, 1)
                    nc.vector.wait_ge(gu_hi_done, i * 2 + (f * FT + jj + 1))
                    nc.vector.tensor_tensor(gu_lo[:, i * 2 + jj, :], product, f32(gu_hi[:, i * 2 + jj, :]),
                                            ALU.subtract).then_inc(gu_lo_done, 1)

            def down_turn(i):
                for j in range(RING):
                    ahead(unit_lo, down, i, j)
                    if j % 2:
                        tile = h[:, i * 2 + j // 2, :]
                        nc.vector.wait_ge(unit_done, i * RING + (down.u0 + j + 1))
                        nc.vector.scalar_tensor_tensor(out=two(tile), in0=tile_halves(2 * (j // 2)), scalar=0.5,
                                                       in1=two(tile), op0=ALU.mult,
                                                       op1=ALU.add).then_inc(pair_free[j // 2], 1)
                        (norm_add if next_norm == "final" else h_tile_dve)(next_norm, j // 2, i)

            turns(nc.vector, up, up_turn)
            norm_clear()
            turns(nc.vector, down, down_turn)

        mix_loaded = sem("mix_loaded")
        pads_clear = sem("pads_clear")
        dt_w_hi = sem("dt_w_hi")
        dt_w_lo = sem("dt_w_lo")
        dve_step = sem("dve_step")
        act_step = sem("act_step")
        pool_step = sem("pool_step")
        rot_done = sem("rot_done")
        vs_done = sem("vs_done")
        dt_first = sem("dt_first")
        dt_copied = sem("dt_copied")
        dt_raw = sem("dt_raw")
        dt_abs = sem("dt_abs")
        dt_exp = sem("dt_exp")
        dt_one = sem("dt_one")
        dt_log = sem("dt_log")
        dt_done = sem("dt_done")
        a_exp_done = sem("a_exp_done")
        conv_done = sem("conv_done")
        xc_done = sem("xc_done")
        conv_s_sum = sem("conv_s_sum")
        last_kept = sem("last_kept")
        ret_a = sem("ret_a")
        ret_w_done = sem("ret_w_done")
        ret_b = sem("ret_b")
        ret_y = sem("ret_y")
        ret_s_done = sem("ret_s_done")
        ret_stored = sem("ret_stored")
        cum_raw = sem("cum_raw")
        cum_done = sem("cum_done")
        cum_diff = sem("cum_diff")
        decay_done = sem("decay_done")
        au_done = sem("au_done")
        ssd_a = sem("ssd_a")
        xdt_done = sem("xdt_done")
        b_tok_done = sem("b_tok_done")
        lmat_raw = sem("lmat_raw")
        lmat_done = sem("lmat_done")
        ea_done = sem("ea_done")
        ce_done = sem("ce_done")
        xdd_done = sem("xdd_done")
        ssd_sd_done = sem("ssd_sd_done")
        ssd_w_done = sem("ssd_w_done")
        ssd_b = sem("ssd_b")
        ssd_y = sem("ssd_y")
        ssd_s_done = sem("ssd_s_done")
        ssm_stored = sem("ssm_stored")
        mem_loaded = sem("mem_loaded")
        gates_done = sem("gates_done")

        RET_TABLES = 2 * HR * CH
        CDEC = [float(np.exp(np.log1p(-np.exp2(np.float64(-5.0 - i))) * CH)) for i in range(HR)]
        U_MIX = STAGES["qk"].u0
        W_QK, W_V, W_XBC, W_GZ = (STAGES[n] for n in ("qk", "v", "xbc", "gz"))
        W_XK, W_XV, W_OUT = (STAGES[n] for n in ("xk", "xv", "out"))

        class Own:

            def __init__(self, eng, s):
                self.eng, self.sem, self.n = eng, s, 0

            def do(self, ins):
                self.n += 1
                ins.then_inc(self.sem, 1)
                self.eng.wait_ge(self.sem, self.n)

        own_v, own_a, own_p = Own(nc.vector, dve_step), Own(nc.scalar, act_step), Own(nc.gpsimd, pool_step)

        def v4(ap, n=HR):
            return ap.rearrange("p (h c) -> p h c", h=n)

        def qk_dve():
            nc.vector.wait_ge(mix_loaded, 96)
            for a in range(2):
                ins = nc.vector.tensor_tensor(rope[:, a, :], rope[:, a, :], rstd[:, :], ALU.mult)
            own_v.do(ins)
            for j in range(8):
                ahead(unit_lo, W_QK, j // RING, j % RING)
                b, pr = 2 * (j % 2), j % 2
                out = q_t[:, j, :] if j < HR else k_t[:, j - HR, :]
                nc.vector.wait_ge(unit_done, W_QK.u0 + j + 1)
                if j:
                    nc.vector.wait_ge(rot_done, j)
                for lo, hi in ((0, 64), (64, 0)):
                    src = ps[hi:hi + 64, b * BANK:(b + 2) * BANK].rearrange("p (a c) -> p a c", a=2)[:, :, 0:HT]
                    nc.vector.tensor_tensor(two(xf[lo:lo + 64, 0, :]), src, two(rope[hi:hi + 64, 1, :]), ALU.mult)
                nc.vector.tensor_tensor(two(xf[:, 1, :]), tile_halves(b), two(rope[:, 0, :]),
                                        ALU.mult).then_inc(pair_free[pr], 1)
                nc.vector.wait_ge(pair_free[pr], W_QK.freed + j // 2 + 1)
                nc.vector.tensor_tensor(out, xf[:, 0, :], xf[:, 1, :], ALU.add).then_inc(rot_done, 1)

        def qk_act():
            for j in range(8):
                ahead(unit_hi, W_QK, j // RING, j % RING)

        def token_cols(t):
            return chunk(t) if t < NCH else slice(0, P)

        def v_pe():
            nc.tensor.wait_ge(dt_w_lo, 1)
            nc.tensor.wait_ge(rot_done, 4)
            for k in range(DT):
                cut = slice(k * HS, (k + 1) * HS)
                for a in range(2):
                    cols = slice(a * HT, (a + 1) * HT)
                    mm = three(bank(6 + a, HT, rows=HS), wdt_hi[:, cut], wdt_lo[:, cut], x_hi[:, k, cols],
                               x_lo[:, k, cols], k == 0, k == DT - 1)
            mm.then_inc(dt_first, 1)
            for pr in range(2):
                nc.tensor.wait_ge(pair_free[pr], W_V.freed)
            for j in range(4):
                nc.tensor.wait_ge(w_lo, W_V.u0 + j + 1)
                for t in range(TOKT):
                    for kk in range(2):
                        k = 2 * j + kk
                        x_h, x_l = x_hi[:, k, token_cols(t)], x_lo[:, k, token_cols(t)]
                        w_h, w_l = (w[j][:, kk * BANK:(kk + 1) * BANK] for w in (w_hi_t, w_lo_t))
                        mm = three(bank(t), x_h, x_l, w_h, w_l, k == 0, k == DT - 1)
                mm.then_inc(unit_done, 1)
            nc.tensor.wait_ge(dt_copied, 1)
            for t in range(TOKT):
                mm = nc.tensor.transpose(bank(5, HS, t * HS), xf[0:HS, 0, token_cols(t)], ident[0:HS, 0:HS])
            mm.then_inc(dt_raw, 1)

        def v_act():
            nc.scalar.wait_ge(mix_loaded, 96)
            nc.scalar.activation(wdt_hi[:, :], wdt[:, :], ACT.Copy).then_inc(dt_w_hi, 1)
            nc.scalar.activation(a_exp[:, :], a_log, ACT.Exp).then_inc(a_exp_done, 1)
            for j in range(4):
                ahead(unit_hi, W_V, 0, j)
                if j == 0:
                    nc.scalar.wait_ge(dt_first, 1)
                    nc.scalar.wait_ge(rot_done, 8)
                    nc.scalar.activation(two(xf[0:HS, 0, :]), tile_halves(6)[0:HS], ACT.Copy).then_inc(dt_copied, 1)
            nc.scalar.wait_ge(unit_done, W_V.u0 + 4)
            for t in range(NCH):
                ins = nc.scalar.activation(v_t[:, t, :], bank(t), ACT.Copy, scale=row_std[:, 1, t:t + 1])
                if t % 2:
                    ins.then_inc(pair_free[t // 2], 1)
            nc.scalar.activation(vs[:, :], bank(4, rows=NS), ACT.Copy,
                                 scale=row_std[0:NS, 1, NCH:NCH + 1]).then_inc(vs_done, 1)
            nc.scalar.wait_ge(dt_abs, 1)
            nc.scalar.activation(dt_e, dt_ab, ACT.Exp, scale=-1.0).then_inc(dt_exp, 1)
            nc.scalar.wait_ge(dt_one, 1)
            nc.scalar.activation(dt_u, dt_u, ACT.Ln).then_inc(dt_log, 1)

        def v_dve():
            nc.vector.wait_ge(dt_w_hi, 1)
            nc.vector.tensor_tensor(wdt_lo[:, :], wdt[:, :], f32(wdt_hi[:, :]), ALU.subtract).then_inc(dt_w_lo, 1)
            for j in range(4):
                ahead(unit_lo, W_V, 0, j)
            do = own_v.do

            def heads(ap):
                return ap.rearrange("p (t h) -> p t h", h=HS)

            nc.vector.wait_ge(dt_raw, 1)
            do(nc.vector.tensor_tensor(heads(dt_x), heads(bank(5, NDT)),
                                       row_parts("mix")[1].unsqueeze(2).to_broadcast([P, TOKT, HS]), ALU.mult))
            do(nc.vector.tensor_tensor(heads(dt_x), heads(dt_x),
                                       dt_bias.unsqueeze(1).to_broadcast([P, TOKT, HS]), ALU.add))
            nc.vector.scalar_tensor_tensor(out=dt_ab, in0=dt_x, scalar=-1.0, in1=dt_x, op0=ALU.mult,
                                           op1=ALU.max).then_inc(dt_abs, 1)
            nc.vector.wait_ge(dt_exp, 1)
            do(nc.vector.tensor_scalar(dt_u, dt_e, 1.0, None, ALU.add))
            do(nc.vector.tensor_scalar(dt_d, dt_u, -1.0, None, ALU.add))
            do(nc.vector.tensor_scalar(dt_m, dt_d, 0.0, None, ALU.is_equal))
            nc.vector.tensor_tensor(dt_d, dt_d, dt_m, ALU.add).then_inc(dt_one, 1)
            nc.vector.wait_ge(dt_one, 1)
            do(nc.vector.reciprocal(dt_t, dt_d))
            nc.vector.wait_ge(dt_log, 1)
            do(nc.vector.tensor_tensor(dt_u, dt_u, dt_m, ALU.add))
            do(nc.vector.tensor_tensor(dt_u, dt_u, dt_e, ALU.mult))
            do(nc.vector.tensor_tensor(dt_u, dt_u, dt_t, ALU.mult))
            do(nc.vector.scalar_tensor_tensor(out=dt_r, in0=dt_x, scalar=0.0, in1=dt_u, op0=ALU.max, op1=ALU.add))
            nc.vector.wait_ge(a_exp_done, 1)
            nc.vector.scalar_tensor_tensor(out=heads(a_dt), in0=heads(dt_r), scalar=-1.0,
                                           in1=a_exp[:, :].unsqueeze(1).to_broadcast([P, TOKT, HS]),
                                           op0=ALU.mult, op1=ALU.mult).then_inc(dt_done, 1)

        def ret_a_pe(c):
            if c == 0:
                nc.tensor.wait_ge(rot_done, 8)
                nc.tensor.wait_ge(vs_done, 1)
                nc.tensor.wait_ge(dt_abs, 1)
            else:
                nc.tensor.wait_ge(ret_w_done, c)
            for i in range(HR):
                nc.tensor.matmul(bank(4, CH, i * CH), k_t[:, i, chunk(c)], q_t[:, i, chunk(c)], start=True, stop=True)
                mm = nc.tensor.transpose(bank(5, P, i * P), k_t[:, i, chunk(c)], ident)
            mm.then_inc(ret_a, 1)

        def ret_b_pe(c):
            nc.tensor.wait_ge(ret_w_done, c + 1)
            if c:
                nc.tensor.wait_ge(ret_y, c)
                nc.tensor.wait_ge(ret_s_done, c)
            for i in range(HR):
                cut = slice(i * P, (i + 1) * P)
                nc.tensor.matmul(bank(6, CH, i * CH), v_t[:, c, cut], ret_w[:, cut], start=True, stop=c == 0)
                if c:
                    nc.tensor.matmul(bank(6, CH, i * CH), ret_s[:, (c - 1) % 2, cut], ret_qd[:, cut],
                                     start=False, stop=True)
            for i in range(HR):
                cut = slice(i * P, (i + 1) * P)
                mm = nc.tensor.matmul(bank(7, P, i * P), ret_k[:, cut], v_t[:, c, cut], start=True, stop=True)
            mm.then_inc(ret_b, 1)

        def ret_a_dve(c):
            nc.vector.wait_ge(ret_a, c + 1)
            if c:
                nc.vector.wait_ge(ret_b, c)
            nc.vector.tensor_tensor(ret_w[:, :], bank(4), c_ret[:, 0:HR * CH], ALU.mult)
            nc.vector.tensor_tensor(v4(ret_k[:, :]), v4(bank(5)),
                                    c_ret[:, RET_TABLES:RET_TABLES + HR].unsqueeze(2).to_broadcast([P, HR, P]),
                                    ALU.mult)
            nc.vector.tensor_tensor(v4(ret_qd[:, :]), q_t[:, :, chunk(c)], v4(c_ret[:, HR * CH:2 * HR * CH]),
                                    ALU.mult).then_inc(ret_w_done, 1)

        def ret_b_dve(c):
            nc.vector.wait_ge(ret_b, c + 1)
            if c == 0:
                nc.vector.tensor_copy(ret_s[:, 0, :], bank(7)).then_inc(ret_s_done, 1)
                return
            nc.vector.wait_ge(ret_s_done, c)
            for i in range(HR):
                cut = slice(i * P, (i + 1) * P)
                ins = nc.vector.scalar_tensor_tensor(out=ret_s[:, c % 2, cut], in0=ret_s[:, (c - 1) % 2, cut],
                                                     scalar=CDEC[i], in1=bank(7, P, i * P), op0=ALU.mult, op1=ALU.add)
            ins.then_inc(ret_s_done, 1)

        def ret_b_act(c):
            nc.scalar.wait_ge(ret_b, c + 1)
            nc.scalar.activation(q_t[:, :, chunk(c)], v4(bank(6)), ACT.Copy).then_inc(ret_y, 1)

        def xbc_pe():
            def after(j):
                (ret_b_pe if j % 2 else ret_a_pe)(j // 2)

            gemm(W_XBC, x_tiles, x_lo_done, SPLIT0["mix"], after=after)

        def xbc_act():
            nc.scalar.wait_ge(pads_clear, 1)

            def silu(n):
                nc.scalar.wait_ge(conv_done, n + 1)
                nc.scalar.activation(conv_tile(n)[:, NS:T], sq[:, n % 2, 0:SEQ], ACT.Silu).then_inc(xc_done, 1)

            for j in range(8):
                ahead(unit_hi, W_XBC, j // RING, j % RING)
                if j:
                    silu(j - 1)
                if j % 2:
                    ret_b_act(j // 2)
            silu(7)

        def xbc_dve():
            do = own_v.do
            nc.vector.wait_ge(pads_clear, 1)
            for j in range(8):
                ahead(unit_lo, W_XBC, j // RING, j % RING)
                acc = sq[:, j % 2, 0:SEQ]
                b, pr, lead = 2 * (j % 2), j % 2, TAPS - 1
                nc.vector.wait_ge(unit_done, W_XBC.u0 + j + 1)
                if j >= 2:
                    nc.vector.wait_ge(last_kept, j - 1)
                nc.vector.tensor_tensor(conv_in[:, j % 2, lead:lead + HT - NS], ps[:, b * BANK + NS:b * BANK + HT],
                                        rstd[:, NS:HT], ALU.mult)
                nc.vector.tensor_tensor(conv_in[:, j % 2, lead + HT - NS:lead + SEQ], half(b, 1), rstd[:, HT:T],
                                        ALU.mult)
                nc.vector.tensor_tensor(conv_s[:, TAPS - 1, j * NS:(j + 1) * NS], ps[:, b * BANK:b * BANK + NS],
                                        rstd[:, 0:NS], ALU.mult).then_inc(pair_free[pr], 1)
                nc.vector.wait_ge(pair_free[pr], W_XBC.freed + j // 2 + 1)
                if j >= 2:
                    nc.vector.wait_ge(xc_done, j - 1)
                do(nc.vector.tensor_scalar(acc, conv_in[:, j % 2, 0:SEQ], conv_w[:, 0, j:j + 1],
                                           conv_b[:, j:j + 1], ALU.mult, ALU.add))
                for t in range(1, TAPS):
                    ins = nc.vector.scalar_tensor_tensor(out=acc, in0=conv_in[:, j % 2, t:t + SEQ],
                                                         scalar=conv_w[:, t, j:j + 1], in1=acc,
                                                         op0=ALU.mult, op1=ALU.add)
                    if t < TAPS - 1:
                        do(ins)
                ins.then_inc(conv_done, 1)
                nc.vector.tensor_copy(conv_last[:, j, :], conv_in[:, j % 2, SEQ:SEQ + TAPS - 1]).then_inc(last_kept, 1)
                if j % 2 == 0:
                    ret_a_dve(j // 2)
                else:
                    ret_b_dve(j // 2)

        def conv_s_dve():
            do = own_v.do
            taps = xf[:, 0, 0:TAPS * 8 * NS]
            total = xf[:, 1, 0:8 * NS]
            do(nc.vector.tensor_tensor(taps.rearrange("p (x b) -> p x b", b=NS),
                                       conv_s[:, :, :].rearrange("p t (n b) -> p (t n) b", b=NS),
                                       small[:, 0:TAPS * 8].unsqueeze(2).to_broadcast([P, TAPS * 8, NS]), ALU.mult))
            do(nc.vector.tensor_reduce(total, taps.rearrange("p (t x) -> p x t", t=TAPS), AX_X, ALU.add))
            nc.vector.tensor_tensor(total.rearrange("p (n b) -> p n b", b=NS),
                                    total.rearrange("p (n b) -> p n b", b=NS),
                                    conv_b.unsqueeze(2).to_broadcast([P, 8, NS]), ALU.add).then_inc(conv_s_sum, 1)

        def conv_s_act():
            nc.scalar.wait_ge(conv_s_sum, 1)
            for n, out in enumerate((cx, cb)):
                ins = nc.scalar.activation(out[:, :, 0:NS],
                                           xf[:, 1, n * 4 * NS:(n + 1) * 4 * NS].rearrange("p (n b) -> p n b", b=NS),
                                           ACT.Silu)
            ins.then_inc(xc_done, 1)

        def cum_pe():
            nc.tensor.wait_ge(dt_done, 1)
            nc.tensor.wait_ge(ret_w_done, NCH)
            nc.tensor.matmul(bank(4, NCH * HS), upper, a_dt[:, 0:NCH * HS], start=True, stop=True)
            nc.tensor.matmul(bank(4, NCH * HS, NCH * HS), ones, a_dt[:, 0:NCH * HS],
                             start=True, stop=True).then_inc(cum_raw, 1)

        def cum_dve():
            n = NCH * HS
            nc.vector.wait_ge(cum_raw, 1)
            nc.vector.tensor_copy(a_cum[:, 0:n], bank(4, n)).then_inc(cum_done, 1)
            nc.vector.tensor_copy(decay[:, 1, :], bank(4, n, n))
            nc.vector.wait_ge(cum_done, 1)
            nc.vector.tensor_tensor(decay[:, 0, :], bank(4, n, n), a_cum[:, 0:n], ALU.subtract).then_inc(cum_diff, 1)

        def cum_act():
            nc.scalar.wait_ge(cum_diff, 1)
            nc.scalar.activation(decay[:, :, :], decay[:, :, :], ACT.Exp).then_inc(decay_done, 1)

        def ssd_a_pe(c):
            if c == 0:
                nc.tensor.wait_ge(xc_done, 8)
                nc.tensor.wait_ge(cum_diff, 1)
                nc.tensor.wait_ge(ret_y, NCH)
                nc.tensor.wait_ge(ret_s_done, NCH)
            else:
                nc.tensor.wait_ge(ssd_y, c)
                nc.tensor.wait_ge(ssd_s_done, c)
                nc.tensor.wait_ge(lmat_raw, c)
                nc.tensor.wait_ge(ea_done, c)
            nc.tensor.wait_ge(au_done, c + 1)
            for i in range(4):
                nc.tensor.transpose(bank(4, P, i * P), cx[:, i, chunk(c)], ident)
            for g in range(SG):
                nc.tensor.transpose(bank(5, P, g * P), cb[:, g, chunk(c)], ident)
            for g in range(SG):
                nc.tensor.matmul(bank(5, CH, (SG + g) * CH), cb[:, g, chunk(c)], cb[:, SG + g, chunk(c)],
                                 start=True, stop=True)
            for a in range(2):
                mm = nc.tensor.matmul(bank(6 + a), ones, ssd_au[:, a * BANK:(a + 1) * BANK], start=True, stop=True)
            mm.then_inc(ssd_a, 1)

        def ssd_b_pe(c):
            nc.tensor.wait_ge(ssd_w_done, c + 1)
            nc.tensor.wait_ge(ce_done, c + 1)
            nc.tensor.wait_ge(xdd_done, c + 1)
            nc.tensor.wait_ge(b_tok_done, c + 1)
            if c:
                nc.tensor.wait_ge(ssd_s_done, c)
            for i in range(HS):
                out = bank(4, CH, (i // 2) * CH, rows=HP, row0=HP * (i % 2))
                cut, wide = slice(i * HP, (i + 1) * HP), slice(i * CH, (i + 1) * CH)
                nc.tensor.matmul(out, xdt[:, cut], ssd_l[:, wide], start=True, stop=c == 0)
                if c:
                    nc.tensor.matmul(out, ssd_s[:, cut], ssd_e[:, wide], start=False, stop=True)
            for g in range(SG):
                mm = nc.tensor.matmul(bank(5, 4 * HP, g * 4 * HP), b_tok[:, g * P:(g + 1) * P],
                                      xdd[:, g * 4 * HP:(g + 1) * 4 * HP], start=True, stop=True)
            mm.then_inc(ssd_b, 1)

        def ssd_a_dve(c):
            heads = slice(c * HS, (c + 1) * HS)
            nc.vector.wait_ge(ssd_a, c + 1)
            if c:
                nc.vector.wait_ge(ssd_b, c)
            nc.vector.tensor_tensor(v4(xdt[:, :], HS), v4(bank(4), HS),
                                    dt_r[:, heads].unsqueeze(2).to_broadcast([P, HS, HP]),
                                    ALU.mult).then_inc(xdt_done, 1)
            nc.vector.wait_ge(ea_done, c + 1)
            for i in range(HS):
                ins = nc.vector.scalar_tensor_tensor(out=ssd_l[:, i * CH:(i + 1) * CH],
                                                     in0=ps[:, 6 * BANK + i * CH:6 * BANK + (i + 1) * CH],
                                                     scalar=a_cum[:, c * HS + i:c * HS + i + 1], in1=mask,
                                                     op0=ALU.subtract, op1=ALU.min)
            ins.then_inc(lmat_raw, 1)
            nc.vector.wait_ge(lmat_done, c + 1)
            for g in range(SG):
                w = v4(ssd_l[:, g * 4 * CH:(g + 1) * 4 * CH], 4)
                ins = nc.vector.tensor_tensor(w, bank(5, CH, (SG + g) * CH).unsqueeze(1).to_broadcast([P, 4, CH]), w,
                                              ALU.mult)
            ins.then_inc(ssd_w_done, 1)

        def ssd_b_dve(c):
            nc.vector.wait_ge(ssd_b, c + 1)
            for i in range(4):
                ins = nc.vector.scalar_tensor_tensor(out=cx[:, i, chunk(c)], in0=cx[:, i, chunk(c)],
                                                     scalar=d_skip[:, i:i + 1], in1=bank(4, CH, i * CH),
                                                     op0=ALU.mult, op1=ALU.add)
            ins.then_inc(ssd_y, 1)
            if c == 0:
                nc.vector.tensor_copy(ssd_s[:, :], bank(5)).then_inc(ssd_s_done, 1)
            else:
                nc.vector.wait_ge(ssd_sd_done, c)
                nc.vector.tensor_tensor(ssd_s[:, :], ssd_sd[:, :], bank(5), ALU.add).then_inc(ssd_s_done, 1)

        def ssd_a_act(c):
            nc.scalar.wait_ge(ssd_a, c + 1)
            if c:
                nc.scalar.wait_ge(ssd_b, c)
            nc.scalar.activation(ssd_e[:, :], ps[:, 6 * BANK:8 * BANK], ACT.Exp).then_inc(ea_done, 1)
            nc.scalar.activation(b_tok[:, :], bank(5, SG * P), ACT.Copy).then_inc(b_tok_done, 1)
            nc.scalar.wait_ge(lmat_raw, c + 1)
            nc.scalar.activation(ssd_l[:, :], ssd_l[:, :], ACT.Exp).then_inc(lmat_done, 1)

        def ssd_pool(c):
            heads = slice(c * HS, (c + 1) * HS)
            nc.gpsimd.wait_ge(ea_done, c + 1)
            for g in range(SG):
                e = v4(ssd_e[:, g * 4 * CH:(g + 1) * 4 * CH], 4)
                ins = nc.gpsimd.tensor_tensor(e, e, cb[:, SG + g, chunk(c)].unsqueeze(1).to_broadcast([P, 4, CH]),
                                              ALU.mult)
            ins.then_inc(ce_done, 1)
            nc.gpsimd.wait_ge(xdt_done, c + 1)
            if c == 0:
                nc.gpsimd.wait_ge(decay_done, 1)
            nc.gpsimd.tensor_tensor(v4(xdd[:, :], HS), v4(xdt[:, :], HS),
                                    decay[:, 0, heads].unsqueeze(2).to_broadcast([P, HS, HP]),
                                    ALU.mult).then_inc(xdd_done, 1)
            if c:
                nc.gpsimd.wait_ge(ssd_s_done, c)
                nc.gpsimd.tensor_tensor(v4(ssd_sd[:, :], HS), v4(ssd_s[:, :], HS),
                                        decay[:, 1, heads].unsqueeze(2).to_broadcast([P, HS, HP]),
                                        ALU.mult).then_inc(ssd_sd_done, 1)
            if c + 1 < NCH:
                au_pool(c + 1)

        def au_pool(c):
            if c == 0:
                nc.gpsimd.wait_ge(dt_done, 1)
                nc.gpsimd.wait_ge(ret_b, NCH)
            else:
                nc.gpsimd.wait_ge(ssd_a, c)
            nc.gpsimd.tensor_tensor(v4(ssd_au[:, :], HS), upper.unsqueeze(1).to_broadcast([P, HS, CH]),
                                    a_dt[:, c * HS:(c + 1) * HS].unsqueeze(2).to_broadcast([P, HS, CH]),
                                    ALU.mult).then_inc(au_done, 1)

        def gz_pe():
            cum_pe()

            def after(j):
                (ssd_b_pe if j % 2 else ssd_a_pe)(j // 2)

            gemm(W_GZ, x_tiles, x_lo_done, SPLIT0["mix"], after=after)

        def gz_act():
            cum_act()
            for j in range(8):
                ahead(unit_hi, W_GZ, j // RING, j % RING)
                out = g_t[:, j, :] if j < 4 else z_t[:, j - 4, :]
                nc.scalar.wait_ge(pair_free[j % 2], W_GZ.freed + j // 2 + 1)
                nc.scalar.activation(out, out, ACT.Silu).then_inc(gates_done, 1)
                if j == 1:
                    conv_s_act()
                if j % 2 == 0:
                    ssd_a_act(j // 2)
                else:
                    mem_square(j - 1)
                    mem_square(j)

        def gz_dve():
            cum_dve()
            norm_clear()
            for j in range(8):
                ahead(unit_lo, W_GZ, j // RING, j % RING)
                out = g_t[:, j, :] if j < 4 else z_t[:, j - 4, :]
                nc.vector.wait_ge(unit_done, W_GZ.u0 + j + 1)
                nc.vector.tensor_tensor(two(out), tile_halves(2 * (j % 2)), two(rstd[:, :]),
                                        ALU.mult).then_inc(pair_free[j % 2], 1)
                if j == 1:
                    conv_s_dve()
                if j % 2 == 0:
                    ssd_a_dve(j // 2)
                else:
                    norm_add("mem", j - 1)
                    norm_add("mem", j)
                    ssd_b_dve(j // 2)

        def mem_square(n):
            if n == 0:
                nc.scalar.wait_ge(mem_loaded, 16)
            norm_square("mem", n, mem_t[:, n, :])

        smp_rows = sem("smp_rows")
        ks_done = sem("ks_done")
        xdts_done = sem("xdts_done")
        a_s_exp = sem("a_s_exp")
        dm_done = sem("dm_done")
        decb_raw = sem("decb_raw")
        decb_done = sem("decb_done")
        vm_done = sem("vm_done")
        rs_loaded = [sem("rs_loaded0"), sem("rs_loaded1")]
        rs_outer = sem("rs_outer")
        rs_state = sem("rs_state")
        rs_y = sem("rs_y")
        smp_loaded = sem("smp_loaded")
        masks_done = sem("masks_done")
        y_rows_done = sem("y_rows_done")
        y_back = sem("y_back")
        rs_stored = [sem("rs_stored0"), sem("rs_stored1")]
        rs_r = sem("rs_r")
        xm_done = sem("xm_done")
        sm_loaded = [sem("sm_loaded0"), sem("sm_loaded1")]
        sm_decayed = sem("sm_decayed")
        sm_outer = sem("sm_outer")
        sm_state = sem("sm_state")
        sm_y = sem("sm_y")
        sm_stored = sem("sm_stored")
        sm_r = sem("sm_r")
        gn_centred = sem("gn_centred")
        gn_squared = sem("gn_squared")
        gn_scaled = sem("gn_scaled")
        gn_var = sem("gn_var")
        gn_std = sem("gn_std")
        gn_recip = sem("gn_recip")
        gn_inv_hi = sem("gn_inv_hi")
        gn_inv_lo = sem("gn_inv_lo")
        gn_spread = sem("gn_spread")
        pick_h_made = sem("pick_h_made")
        gated = sem("gated")

        def smp_rows_pe():
            nc.tensor.wait_ge(ssd_y, NCH)
            nc.tensor.wait_ge(ssd_s_done, NCH)
            nc.tensor.wait_ge(rstd_done, NORM_AT["mem"] + 1)
            for i in range(HR):
                nc.tensor.transpose(bank(4, P, i * P, rows=NS), k_t[:, i, 0:NS], ident)
                nc.tensor.transpose(bank(5, P, i * P, rows=NS), cx[:, i, 0:NS], ident)
            for g in range(SG):
                mm = nc.tensor.transpose(bank(6, P, g * P, rows=NS), cb[:, g, 0:NS], ident)
            mm.then_inc(smp_rows, 1)

        def decb_pe():
            nc.tensor.wait_ge(dm_done, 1)
            nc.tensor.wait_ge(lmat_raw, NCH)
            nc.tensor.matmul(bank(7, NS * HS, 128), ones[0:NS, :], dm[:, :], start=True, stop=True).then_inc(decb_raw, 1)

        def smp_rows_act():
            nc.scalar.wait_ge(ssd_b, NCH)
            nc.scalar.wait_ge(ssm_stored, 16)
            nc.scalar.activation(dt_e[0:NS, 0:HS], a_dt[0:NS, NCH * HS:TOKT * HS], ACT.Exp).then_inc(a_s_exp, 1)
            nc.scalar.wait_ge(smp_rows, 1)
            nc.scalar.activation(ks[:, :], bank(4, rows=NS), ACT.Copy, scale=RK_SCALE)
            nc.scalar.activation(bs[:, :], bank(6, SG * P, rows=NS), ACT.Copy).then_inc(ks_done, 1)
            nc.scalar.wait_ge(decb_raw, 1)
            nc.scalar.activation(decb[:, :], bank(7, NS * HS, 128), ACT.Copy).then_inc(decb_done, 1)

        def smp_rows_dve():
            nc.vector.wait_ge(smp_rows, 1)
            nc.vector.tensor_tensor(v4(xdts[:, :], HS), v4(bank(5, rows=NS), HS),
                                    dt_r[0:NS, NCH * HS:TOKT * HS].unsqueeze(2).to_broadcast([NS, HS, HP]),
                                    ALU.mult).then_inc(xdts_done, 1)

        def rs_outer_pe(i):
            nc.tensor.wait_ge(ks_done, 1)
            nc.tensor.wait_ge(xdts_done, 1)
            nc.tensor.wait_ge(vm_done, i + 1)
            if i:
                nc.tensor.wait_ge(rs_state, i)
            for a in range(2):
                mm = nc.tensor.matmul(bank(4 + a), ks[:, i * P:(i + 1) * P], vm[:, i % 2, a * BANK:(a + 1) * BANK],
                                      start=True, stop=True)
            mm.then_inc(rs_outer, 1)

        def rs_y_pe(i):
            nc.tensor.wait_ge(rs_state, i + 1)
            if i == 0:
                nc.tensor.wait_ge(decb_done, 1)
                nc.tensor.wait_ge(masks_done, 1)
            for b in range(NS):
                at = (i * NS + b) * NS
                mm = nc.tensor.matmul(bank(7, P, i * P, rows=NS), q_mask[:, at:at + NS],
                                      st_ret[:, i % 2, b * P:(b + 1) * P], start=b == 0, stop=b == NS - 1)
            mm.then_inc(rs_y, 1)

        def masks_dve():
            nc.vector.wait_ge(smp_loaded, 16)
            nc.vector.wait_ge(xc_done, 9)
            nc.vector.wait_ge(rot_done, 8)
            column = own_column.rearrange("p (a b) -> p a b", a=NS).unsqueeze(1)
            for out, source, n in ((q_mask, q_t[:, :, 0:NS], HR), (c_mask, cb[:, SG:2 * SG, 0:NS], SG)):
                ins = nc.vector.tensor_tensor(out.rearrange("p (h a b) -> p h a b", h=n, a=NS),
                                              source.unsqueeze(3).to_broadcast([P, n, NS, NS]),
                                              column.to_broadcast([P, n, NS, NS]), ALU.mult)
            ins.then_inc(masks_done, 1)

        def y_rows_act(n):
            nc.scalar.wait_ge(*((sm_y, SG) if n else (rs_y, HR)))
            if n:
                nc.scalar.wait_ge(y_back, 1)
            nc.scalar.activation(y_rows, bank(7, rows=NS), ACT.Copy).then_inc(y_rows_done, 1)

        def y_back_pe(n):
            nc.tensor.wait_ge(y_rows_done, n + 1)
            if n:
                nc.tensor.wait_ge(gn_std, 2)
            else:
                nc.tensor.wait_ge(gn_std, 1)
            for i in range(4):
                mm = nc.tensor.transpose(bank(6, NS, i * NS), y_rows[:, i * P:(i + 1) * P], ident[0:NS, 0:NS])
            mm.then_inc(y_back, 1)

        def rs_dve(i):
            nc.vector.wait_ge(rs_outer, i + 1)
            nc.vector.wait_ge(rs_loaded[i % 2], 16 * (i // 2 + 1))
            nc.vector.scalar_tensor_tensor(out=st_ret[:, i % 2, :], in0=st_ret[:, i % 2, :], scalar=GAMMA[i],
                                           in1=ps[:, 4 * BANK:6 * BANK], op0=ALU.mult, op1=ALU.add).then_inc(rs_state, 1)

        def rs_r_act():
            nc.scalar.wait_ge(y_back, 1)
            nc.scalar.wait_ge(masks_done, 1)
            nc.scalar.activation(q_t[:, :, 0:NS], v4(bank(6, HR * NS)), ACT.Copy).then_inc(rs_r, 1)

        def sm_outer_pe(n):
            g = n // 2
            nc.tensor.wait_ge(xm_done, n + 1)
            if n == 0:
                nc.tensor.wait_ge(rs_state, HR)
            else:
                nc.tensor.wait_ge(sm_state, n)
            for a in range(2):
                mm = nc.tensor.matmul(bank(4 + a), bs[:, g * P:(g + 1) * P],
                                      xm[:, 2 * a:2 * a + 2, :].rearrange("p b c -> p (b c)"), start=True, stop=True)
            mm.then_inc(sm_outer, 1)

        def sm_y_pe(g):
            nc.tensor.wait_ge(sm_state, 2 * g + 2)
            if g == 0:
                nc.tensor.wait_ge(y_rows_done, 1)
            for b in range(NS):
                at = (g * NS + b) * NS
                mm = nc.tensor.matmul(bank(7, 4 * HP, g * 4 * HP, rows=NS), c_mask[:, at:at + NS],
                                      st_ssm[:, g, b * 4 * HP:(b + 1) * 4 * HP], start=b == 0, stop=b == NS - 1)
            mm.then_inc(sm_y, 1)

        def sm_dve(n):
            g, q = n // 2, n % 2
            part = st_ssm[:, g, q * 4 * 4 * HP:(q + 1) * 4 * 4 * HP]
            nc.vector.wait_ge(sm_outer, n + 1)
            nc.vector.wait_ge(sm_decayed, g + 1)
            nc.vector.tensor_tensor(part, part, ps[:, 4 * BANK:6 * BANK], ALU.add).then_inc(sm_state, 1)

        def sm_r_dve():
            nc.vector.wait_ge(y_back, 2)
            for i in range(4):
                ins = nc.vector.scalar_tensor_tensor(out=cx[:, i, 0:NS], in0=cx[:, i, 0:NS], scalar=d_skip[:, i:i + 1],
                                                     in1=bank(6, NS, i * NS), op0=ALU.mult, op1=ALU.add)
            ins.then_inc(sm_r, 1)

        eye_s = ident[0:NS, 0:NS]

        def smp_pool():
            def values(i):
                if i >= 2:
                    nc.gpsimd.wait_ge(rs_outer, i - 1)
                nc.gpsimd.tensor_tensor(vm[:, i % 2, :].rearrange("p (b c) -> p b c", b=NS),
                                        vs[:, i * P:(i + 1) * P].unsqueeze(1).to_broadcast([NS, NS, P]),
                                        eye_s.unsqueeze(2).to_broadcast([NS, NS, P]), ALU.mult).then_inc(vm_done, 1)

            def load_ret(i):
                if i >= 2:
                    nc.gpsimd.wait_ge(rs_stored[i % 2], 16 * (i // 2))
                    nc.gpsimd.wait_ge(rs_y, i - 1)
                nc.gpsimd.dma_start(st_ret[:, i % 2, :], A["st_ret"][i]).then_inc(rs_loaded[i % 2], 16)

            def store_ret(i):
                nc.gpsimd.wait_ge(rs_state, i + 1)
                nc.gpsimd.dma_start(A["o_ret_s"][i], st_ret[:, i % 2, :]).then_inc(rs_stored[i % 2], 16)

            def products(n):
                g, q = n // 2, n % 2
                if n:
                    nc.gpsimd.wait_ge(sm_outer, n)
                nc.gpsimd.tensor_tensor(xm[:, :, :],
                                        xdts[:, g * 4 * HP:(g + 1) * 4 * HP].unsqueeze(1).to_broadcast([NS, 4, 4 * HP]),
                                        eye_s[:, 4 * q:4 * q + 4].unsqueeze(2).to_broadcast([NS, 4, 4 * HP]),
                                        ALU.mult).then_inc(xm_done, 1)

            nc.gpsimd.wait_ge(vs_done, 1)
            nc.gpsimd.wait_ge(ssd_b, NCH)
            load_ret(0)
            load_ret(1)
            nc.gpsimd.dma_start(c_smp, A["c_smp"]).then_inc(smp_loaded, 16)
            values(0)
            nc.gpsimd.wait_ge(a_s_exp, 1)
            nc.gpsimd.tensor_tensor(dm[:, :].rearrange("p (b h) -> p b h", b=NS),
                                    dt_e[0:NS, 0:HS].unsqueeze(1).to_broadcast([NS, NS, HS]),
                                    eye_s.unsqueeze(2).to_broadcast([NS, NS, HS]), ALU.mult).then_inc(dm_done, 1)
            values(1)
            nc.gpsimd.wait_ge(xdts_done, 1)
            products(0)
            nc.gpsimd.wait_ge(unit_done, W_XK.u0)
            nc.gpsimd.tensor_tensor(pick_h, ident[0:HR, 0:HR].unsqueeze(2).to_broadcast([HR, HR, P]),
                                    ones[0:HR, :].unsqueeze(1).to_broadcast([HR, HR, P]),
                                    ALU.mult).then_inc(pick_h_made, 1)
            for i in range(HR):
                store_ret(i)
                if i + 2 < HR:
                    values(i + 2)
                    load_ret(i + 2)
            nc.gpsimd.wait_ge(decb_done, 1)
            for par in range(2):
                nc.gpsimd.wait_ge(rs_stored[par], 32)
            nc.gpsimd.wait_ge(rs_y, HR)
            for g in range(SG):
                nc.gpsimd.dma_start(st_ssm[:, g, :], A["st_ssm"][g]).then_inc(sm_loaded[g], 16)
            for g in range(SG):
                nc.gpsimd.wait_ge(sm_loaded[g], 16)
                nc.gpsimd.tensor_tensor(st_ssm[:, g, :].rearrange("p (b h c) -> p b h c", b=NS, h=4),
                                        st_ssm[:, g, :].rearrange("p (b h c) -> p b h c", b=NS, h=4),
                                        decb[:, :].rearrange("p (b h) -> p b h", b=NS)[:, :, 4 * g:4 * g + 4]
                                        .unsqueeze(3).to_broadcast([P, NS, 4, HP]), ALU.mult).then_inc(sm_decayed, 1)
            for n in range(1, 4):
                products(n)
            for g in range(SG):
                nc.gpsimd.wait_ge(sm_state, 2 * g + 2)
                nc.gpsimd.dma_start(A["o_ssm_s"][g], st_ssm[:, g, :]).then_inc(sm_stored, 16)

        def gn_centre_pe(i):
            if i == 0:
                nc.tensor.wait_ge(ks_done, 1)
            else:
                nc.tensor.wait_ge(gn_squared, i)
            nc.tensor.matmul(bank(6), centre, q_t[:, i, NS:T], start=True, stop=True).then_inc(gn_centred, 1)

        def gn_act(i):
            nc.scalar.wait_ge(gn_centred, i + 1)
            nc.scalar.activation(q_t[:, i, NS:T], bank(6), ACT.Copy)
            nc.scalar.activation(gn_s[:, i, NS:T], bank(6), ACT.Square).then_inc(gn_squared, 1)

        def gn_centre_s_pe():
            nc.tensor.wait_ge(rs_r, 1)
            nc.tensor.matmul(bank(6, HR * NS), centre, q_t[:, :, 0:NS], start=True, stop=True).then_inc(gn_centred, 1)

        def gn_s_act():
            nc.scalar.wait_ge(gn_centred, HR + 1)
            nc.scalar.activation(q_t[:, :, 0:NS], v4(bank(6, HR * NS)), ACT.Copy)
            nc.scalar.activation(gn_s[:, :, 0:NS], v4(bank(6, HR * NS)), ACT.Square).then_inc(gn_squared, 1)

        def gn_gate_dve(i):
            nc.vector.wait_ge(gn_squared, i + 1)
            for k, c in ((i, slice(NS, T)),) if i < HR else [(k, slice(0, NS)) for k in range(HR)]:
                ins = nc.vector.scalar_tensor_tensor(out=q_t[:, k, c], in0=q_t[:, k, c], scalar=gain("ret", k),
                                                     in1=g_t[:, k, c], op0=ALU.mult, op1=ALU.mult)
            ins.then_inc(gn_scaled, 1)

        GN_COLS = (slice(NS, T), slice(0, NS))
        GN_INV = (gn_inv, gn_inv_s)

        def gn_var_pe(n):
            nc.tensor.wait_ge(gn_squared, HR + n)
            w = GN_COLS[n].stop - GN_COLS[n].start
            for i in range(HR):
                mm = nc.tensor.matmul(bank(6, w, rows=HR), pick_mean[:, i * HR:(i + 1) * HR], gn_s[:, i, GN_COLS[n]],
                                      start=i == 0, stop=i == HR - 1)
            mm.then_inc(gn_var, 1)

        def gn_std_act(n):
            w = GN_COLS[n].stop - GN_COLS[n].start
            nc.scalar.wait_ge(gn_var, n + 1)
            nc.scalar.activation(GN_INV[n], bank(6, w, rows=HR), ACT.Sqrt, bias=eps[0:HR, :]).then_inc(gn_std, 1)

        def gn_recip_dve(n):
            nc.vector.wait_ge(gn_std, n + 1)
            nc.vector.reciprocal(GN_INV[n], GN_INV[n]).then_inc(gn_recip, 1)

        def gn_hi_act(n):
            nc.scalar.wait_ge(gn_recip, n + 1)
            nc.scalar.activation(inv_hi[:, GN_COLS[n]], GN_INV[n], ACT.Copy).then_inc(gn_inv_hi, 1)

        def gn_lo_dve(n):
            nc.vector.wait_ge(gn_inv_hi, n + 1)
            nc.vector.tensor_tensor(inv_lo[:, GN_COLS[n]], GN_INV[n], f32(inv_hi[:, GN_COLS[n]]),
                                    ALU.subtract).then_inc(gn_inv_lo, 1)

        def gn_spread_pe(i):
            if i == 0:
                nc.tensor.wait_ge(gn_inv_lo, 2)
                nc.tensor.wait_ge(pick_h_made, 1)
                nc.tensor.wait_ge(sm_state, 4)
            else:
                nc.tensor.wait_ge(xf_done, MADE0["ret"] + i)
            for a in range(2):
                cols = slice(a * HT, (a + 1) * HT)
                nc.tensor.matmul(half(4, a), pick_h[:, i, :], inv_lo[:, cols], start=True, stop=False)
                mm = nc.tensor.matmul(half(4, a), pick_h[:, i, :], inv_hi[:, cols], start=False, stop=True)
            mm.then_inc(gn_spread, 1)

        def ret_made_dve(i):
            nc.vector.wait_ge(gn_spread, i + 1)
            if i == 0:
                nc.vector.wait_ge(gn_scaled, HR + 1)
            if i >= 2:
                nc.vector.wait_ge(x_lo_done, SPLIT0["ret"] + i - 1)
            nc.vector.tensor_tensor(two(xf[:, i % 2, :]), tile_halves(4), two(q_t[:, i, :]),
                                    ALU.mult).then_inc(xf_done, 1)

        def ret_hi_act(i):
            nc.scalar.wait_ge(xf_done, MADE0["ret"] + i + 1)
            if i == 0:
                nc.scalar.wait_ge(sm_outer, 4)
                nc.scalar.wait_ge(sm_decayed, SG)
            nc.scalar.activation(ret_hi[:, i, :], xf[:, i % 2, :], ACT.Copy).then_inc(x_hi_done, 1)

        def ret_lo_dve(i):
            nc.vector.wait_ge(x_hi_done, SPLIT0["ret"] + i + 1)
            nc.vector.tensor_tensor(ret_lo[:, i, :], xf[:, i % 2, :], f32(ret_hi[:, i, :]),
                                    ALU.subtract).then_inc(x_lo_done, 1)

        def gated_dve(n):
            if n == 0:
                nc.vector.wait_ge(gates_done, 8)
                nc.vector.wait_ge(ssd_y, NCH)
            if n == 4:
                nc.vector.wait_ge(sm_r, 1)
            part = cx[:, n, NS:T] if n < 4 else cx[:, :, 0:NS]
            gate = z_t[:, n, NS:T] if n < 4 else z_t[:, :, 0:NS]
            nc.vector.tensor_tensor(part, part, gate, ALU.mult).then_inc(gated, 1)

        def gated_square_act(n):
            nc.scalar.wait_ge(gated, n + 1)
            nc.scalar.wait_ge(sq_added, SQ0["ssd"] + n)
            if n < 4:
                ins = nc.scalar.activation(sq[:, n % 2, 0:SEQ], cx[:, n, NS:T], ACT.Square)
            else:
                ins = nc.scalar.activation(v4(sq[:, 0, 0:4 * NS]), cx[:, :, 0:NS], ACT.Square)
            ins.then_inc(sq_done, 1)

        def gated_add_dve(n):
            nc.vector.wait_ge(sq_done, SQD0["ssd"] + n + 1)
            nc.vector.wait_ge(sq_added, SQ0["ssd"] + n + 1)
            if n < 4:
                ins = nc.vector.tensor_tensor(sq_sum[:, NS:T], sq_sum[:, NS:T], sq[:, n % 2, 0:SEQ], ALU.add)
            else:
                ins = nc.vector.tensor_reduce(sq_sum[:, 0:NS], sq[:, 0, 0:4 * NS].rearrange("p (n b) -> p b n", n=4),
                                              AX_X, ALU.add)
            ins.then_inc(sq_added, 1)

        def mem_tiles(k):
            return m_tile(x_hi, k), m_tile(x_lo, k)

        def slots(engine):
            steps = {n: [] for n in range(16)}

            def put(n, name, f):
                if name == engine:
                    steps[n].append(f)

            def each(first, count, *pairs):
                for i in range(count):
                    for late, name, f in pairs:
                        put(first + i + late, name, lambda f=f, i=i: f(i))

            put(0, "pe", lambda: norm_rows_pe("mem", inv_d))
            put(0, "dve", norm_clear)
            put(1, "pe", lambda: norm_spread_pe("mem"))
            put(1, "act", smp_rows_act)
            put(1, "dve", smp_rows_dve)
            put(1, "pe", smp_rows_pe)
            put(1, "pe", decb_pe)
            put(1, "dve", masks_dve)
            each(2, HR, (0, "pe", rs_outer_pe), (0, "dve", rs_dve), (1, "pe", rs_y_pe),
                 (0, "pe", gn_centre_pe), (0, "act", gn_act), (0, "dve", gated_dve), (0, "act", gated_square_act),
                 (1, "dve", gated_add_dve), (1, "dve", gn_gate_dve))
            put(6, "pe", lambda: gn_var_pe(0))
            put(6, "act", lambda: gn_std_act(0))
            put(6, "act", lambda: y_rows_act(0))
            each(6, 4, (0, "pe", sm_outer_pe), (0, "dve", sm_dve))
            put(7, "pe", lambda: y_back_pe(0))
            put(7, "act", rs_r_act)
            put(7, "dve", lambda: gn_recip_dve(0))
            put(8, "pe", gn_centre_s_pe)
            put(8, "act", gn_s_act)
            put(8, "act", lambda: gn_hi_act(0))
            put(8, "dve", lambda: gn_lo_dve(0))
            put(8, "pe", lambda: sm_y_pe(0))
            put(9, "dve", lambda: gn_gate_dve(HR))
            put(9, "pe", lambda: gn_var_pe(1))
            put(9, "act", lambda: gn_std_act(1))
            put(10, "dve", lambda: gn_recip_dve(1))
            put(10, "act", lambda: gn_hi_act(1))
            put(10, "dve", lambda: gn_lo_dve(1))
            put(10, "pe", lambda: sm_y_pe(1))
            put(10, "act", lambda: y_rows_act(1))
            each(11, HR, (0, "pe", gn_spread_pe), (0, "dve", ret_made_dve), (0, "act", ret_hi_act),
                 (1, "dve", ret_lo_dve))
            put(11, "pe", lambda: y_back_pe(1))
            put(11, "dve", sm_r_dve)
            put(12, "dve", lambda: gated_dve(4))
            put(12, "act", lambda: gated_square_act(4))
            put(13, "dve", lambda: gated_add_dve(4))
            put(14, "pe", lambda: norm_rows_pe("ssd", inv_512))
            put(14, "act", lambda: norm_rows_act("ssd"))
            put(14, "dve", lambda: norm_diag_dve("ssd"))
            put(15, "pe", lambda: norm_spread_pe("ssd"))
            put(15, "act", lambda: norm_rstd_act("ssd"))
            return steps

        def xkv_pe():
            steps = slots("pe")

            def after(j):
                for f in steps[j]:
                    f()

            gemm(W_XK, mem_tiles, x_lo_done, SPLIT0["mem"], width=MEM, after=after)
            for pr in range(2):
                nc.tensor.wait_ge(pair_free[pr], W_XV.freed)
            for k in range(8):
                nc.tensor.wait_ge(w_lo, W_XV.u0 + k + 1)
                m_h, m_l = mem_tiles(k)
                for mt in range(MT):
                    for a in range(2):
                        cut, wide = slice(mt * P, (mt + 1) * P), slice(a * BANK, (a + 1) * BANK)
                        mm = three(bank(2 * mt + a), m_h[:, cut], m_l[:, cut], w_hi_t[k % RING][:, wide],
                                   w_lo_t[k % RING][:, wide], k == 0, k == 7)
                mm.then_inc(unit_done, 1)
                after(8 + k)

        def xkv_act():
            nc.scalar.wait_ge(unit_done, W_XK.u0)
            for k in range(8):
                gained_hi("mem", k, mem_t[:, k, :], m_tile(x_hi, k))
            for pr in range(2):
                nc.scalar.wait_ge(pair_free[pr], W_XK.freed)
            norm_rows_act("mem")
            norm_rstd_act("mem")
            steps = slots("act")
            for j in range(8):
                ahead(unit_hi, W_XK, j // RING, j % RING)
                for f in steps[j]:
                    f()
            for j in range(8):
                ahead(unit_hi, W_XV, j // RING, j % RING)
                for f in steps[8 + j]:
                    f()
            nc.scalar.wait_ge(unit_done, W_XV.u0 + 8)
            for mt in range(MT):
                nc.scalar.activation(mem_v[:, mt, :], ps[:, 2 * mt * BANK:(2 * mt + 2) * BANK],
                                     ACT.Copy, scale=row_parts("mem")[1][:, mt:mt + 1]).then_inc(pair_free[mt], 1)
            made_hi_act("ssd", lambda k: ssd_hi[:, k, :])

        def xkv_dve():
            for k in range(8):
                gained_lo("mem", k, mem_t[:, k, :], m_tile(x_hi, k), m_tile(x_lo, k), SPLIT0["mem"] + k + 1)
            norm_diag_dve("mem")
            nc.vector.wait_ge(rstd_done, NORM_AT["mem"] + 1)
            steps = slots("dve")
            for j in range(16):
                st = W_XK if j < 8 else W_XV
                ahead(unit_lo, st, (j % 8) // RING, j % RING)
                if j < 8:
                    nc.vector.wait_ge(unit_done, W_XK.u0 + j + 1)
                    nc.vector.wait_ge(x_lo_done, SPLIT0["mem"] + 8)
                    nc.vector.tensor_tensor(mem_k[:, j, :], bank(2 * (j % 2), MEM), rstd[:, 0:MEM],
                                            ALU.mult).then_inc(pair_free[j % 2], 1)
                for f in steps[j]:
                    f()
            nc.vector.wait_ge(rstd_done, NORM_AT["ssd"] + 1)
            made_dve("ssd", normed("ssd", lambda k: cx[:, k, :]), lambda k: ssd_hi[:, k, :],
                      lambda k: ssd_lo[:, k, :])

        def out_tiles(k):
            if k < 4:
                return ret_hi[:, k, :], ret_lo[:, k, :]
            return ssd_hi[:, k - 4, :], ssd_lo[:, k - 4, :]

        def residual_pe(stage, operand, ready, ready0):
            gemm(stage, operand, ready, ready0)

        def residual_act(stage, next_norm):
            for j in range(8):
                ahead(unit_hi, stage, j // RING, j % RING)
                nc.scalar.wait_ge(pair_free[j % 2], stage.freed + j // 2 + 1)
                h_tile_act(next_norm, j)

        def residual_dve(stage, next_norm):
            norm_clear()
            for j in range(8):
                ahead(unit_lo, stage, j // RING, j % RING)
                nc.vector.wait_ge(unit_done, stage.u0 + j + 1)
                nc.vector.tensor_tensor(two(h[:, j, :]), two(h[:, j, :]), tile_halves(2 * (j % 2)),
                                        ALU.add).then_inc(pair_free[j % 2], 1)
                h_tile_dve(next_norm, j)

        qx_done = sem("qx_done")
        mem_stored = sem("mem_stored")
        sc_done = sem("sc_done")
        mx_done = sem("mx_done")
        ex_done = sem("ex_done")
        pr_done = sem("pr_done")
        pt_done = sem("pt_done")
        at_done = sem("at_done")
        o_done = sem("o_done")
        o_hi = sem("o_hi")
        o_lo = sem("o_lo")
        cache_loaded = [sem(f"cache_loaded{i}") for i in range(3)]
        cache_used = sem("cache_used")
        picks_made = sem("picks_made")
        qr_done = sem("qr_done")
        qr_hi_done = sem("qr_hi_done")
        qr_lo_done = sem("qr_lo_done")
        qb_done = sem("qb_done")
        srow_done = sem("srow_done")
        smx_done = sem("smx_done")
        sex_done = sem("sex_done")
        spr_done = sem("spr_done")
        sr_hi_done = sem("sr_hi_done")
        sr_lo_done = sem("sr_lo_done")
        ab_done = sem("ab_done")
        so_hi = sem("so_hi")
        so_lo = sem("so_lo")
        W_XQ, W_XO = STAGES["xq"], STAGES["xo"]
        NROW = NS * XH

        def q_rows_pe(i):
            for pr in range(2):
                nc.tensor.wait_ge(pair_free[pr], W_XQ.freed + i + 1)
            if i:
                nc.tensor.wait_ge(cache_used, 2 * i - 1)
            for d in range(2):
                mm = nc.tensor.transpose(bank(4, P, d * P, rows=NS), qx(2 * i + d)[:, 0:NS], ident)
            mm.then_inc(qr_done, 1)

        def q_rows_act(i):
            nc.scalar.wait_ge(qr_done, i + 1)
            if i:
                nc.scalar.wait_ge(qb_done, 2 * i)
            nc.scalar.activation(qr_hi[:, :], bank(4, MEM, rows=NS), ACT.Copy).then_inc(qr_hi_done, 1)

        def q_rows_dve(i):
            nc.vector.wait_ge(qr_hi_done, i + 1)
            nc.vector.tensor_tensor(qr_lo[:, :], bank(4, MEM, rows=NS), f32(qr_hi[:, :]),
                                    ALU.subtract).then_inc(qr_lo_done, 1)

        def q_spread_pe(i):
            nc.tensor.wait_ge(qr_lo_done, i + 1)
            if i == 0:
                nc.tensor.wait_ge(picks_made, 1)
            for b in range(NS):
                if i and b == 4:
                    nc.tensor.wait_ge(cache_used, 2 * i)
                out = ps[:, 4 * BANK + b * MEM:4 * BANK + (b + 1) * MEM]
                nc.tensor.matmul(out, pick_q_hi[:, b, :], qr_lo[:, :], start=True, stop=False)
                mm = nc.tensor.matmul(out, pick_q_hi[:, b, :], qr_hi[:, :], start=False, stop=True)
                if b % 4 == 3:
                    mm.then_inc(qb_done, 1)

        def s_scores_dve(i):
            for n in (2 * i, 2 * i + 1):
                nc.vector.wait_ge(cache_loaded[n % 3], 16 * (n // 3 + 1))
                nc.vector.wait_ge(qb_done, n + 1)
                for q in range(4):
                    b = 4 * (n % 2) + q
                    for m in range(MT):
                        keys, at = cache[:, n % 3, (q * MT + m) * MEM:(q * MT + m + 1) * MEM], m * NROW + b * XH + i
                        ins = nc.vector.tensor_tensor_reduce(keys, keys, ps[:, 4 * BANK + b * MEM:4 * BANK + (b + 1) * MEM],
                                                             1.0, 0.0, ALU.mult, ALU.add, att_c[:, 0, at:at + 1])
                ins.then_inc(cache_used, 1)

        def xq_pe():
            def after(j):
                if j >= 2:
                    (q_spread_pe if j % 2 else q_rows_pe)(j // 2 - 1)

            gemm(W_XQ, x_tiles, x_lo_done, SPLIT0["x"], after=after, norm="x")

        def xq_act():
            for j in range(8):
                ahead(unit_hi, W_XQ, j // RING, j % RING)
                if j >= 2 and j % 2 == 0:
                    q_rows_act(j // 2 - 1)

        def xq_dve():
            for j in range(8):
                ahead(unit_lo, W_XQ, j // RING, j % RING)
                nc.vector.wait_ge(unit_done, W_XQ.u0 + j + 1)
                nc.vector.tensor_tensor(two(qx(j)), tile_halves(2 * (j % 2)), two(rstd[:, :]),
                                        ALU.mult).then_inc(pair_free[j % 2], 1)
                if j >= 2:
                    (s_scores_dve if j % 2 else q_rows_dve)(j // 2 - 1)

        def picks_pool():
            nc.gpsimd.wait_ge(unit_done, W_OUT.u0 + 8)
            nc.gpsimd.tensor_tensor(pick_q_hi[:, :, :], ident[0:NS, 0:NS].unsqueeze(2).to_broadcast([NS, NS, P]),
                                    ones[0:NS, :].unsqueeze(1).to_broadcast([NS, NS, P]), ALU.mult).then_inc(picks_made, 1)

        def pick_rows_pool():
            nc.gpsimd.wait_ge(unit_done, W_XQ.u0 + 8)
            nc.gpsimd.tensor_tensor(pick_r, ident[0:NROW, 0:NROW].unsqueeze(2).to_broadcast([NROW, NROW, P]),
                                    ones[0:NROW, :].unsqueeze(1).to_broadcast([NROW, NROW, P]),
                                    ALU.mult).then_inc(picks_made, 1)

        def score_pe(c):
            b = 2 * (c % 2)
            if c < 2:
                nc.tensor.wait_ge(pair_free[c], W_XO.freed)
            else:
                nc.tensor.wait_ge(ex_done, c - 1)
            if c == 0:
                nc.tensor.wait_ge(pair_free[1], W_XO.freed)
            for i in range(XH):
                out = ps[:, b * BANK + i * MEM:b * BANK + (i + 1) * MEM]
                for d in range(2):
                    mm = nc.tensor.matmul(out, qx(2 * i + d)[:, chunk(c)], mem_k[:, 2 * i + d, :],
                                          start=d == 0, stop=d == 1)
            mm.then_inc(sc_done, 1)

        def att_stats(c):
            return (att_s[:, c % 2, i * XH:(i + 1) * XH] for i in range(3))

        def softmax_dve(c):
            mx, total, inv = att_stats(c)
            b = 2 * (c % 2)
            nc.vector.wait_ge(sc_done, c + 1)
            own_v.do(nc.vector.tensor_reduce(mx, ps[:, b * BANK:(b + 2) * BANK].rearrange("p (i m) -> p i m", i=XH),
                                             AX_X, ALU.max))
            nc.vector.tensor_scalar(mx, mx, -X_SCALE, None, ALU.mult).then_inc(mx_done, 1)

        def softmax_act(c):
            mx, total, inv = att_stats(c)
            b = 2 * (c % 2)
            nc.scalar.wait_ge(mx_done, c + 1)
            if c >= 2:
                nc.scalar.wait_ge(pt_done, c - 1)
            for i in range(XH):
                ins = nc.scalar.activation(att_p[:, c % 2, i * MEM:(i + 1) * MEM],
                                           ps[:, b * BANK + i * MEM:b * BANK + (i + 1) * MEM], ACT.Exp,
                                           bias=mx[:, i:i + 1], scale=X_SCALE, accum_out=total[:, i:i + 1])
            ins.then_inc(ex_done, 1)

        def probs_dve(c):
            mx, total, inv = att_stats(c)
            nc.vector.wait_ge(ex_done, c + 1)
            own_v.do(nc.vector.reciprocal(inv, total))
            p = v4(att_p[:, c % 2, :])
            nc.vector.tensor_tensor(p, p, inv.unsqueeze(2).to_broadcast([P, XH, MEM]), ALU.mult).then_inc(pr_done, 1)

        def turn_pe(c):
            nc.tensor.wait_ge(pr_done, c + 1)
            if c == 0:
                nc.tensor.wait_ge(cache_used, NS - 1)
            else:
                nc.tensor.wait_ge(at_done, c)
            for i in range(XH):
                for m in range(MT):
                    mm = nc.tensor.transpose(bank(4 + m, P, i * P), att_p[:, c % 2, i * MEM + m * P:i * MEM + (m + 1) * P],
                                             ident)
            mm.then_inc(pt_done, 1)

        def turned_act(c):
            nc.scalar.wait_ge(pt_done, c + 1)
            if c == 0:
                nc.scalar.wait_ge(qb_done, NS)
            for m, att in enumerate((att_0, att_1)):
                ins = nc.scalar.activation(att[:, :, c * CH:(c + 1) * CH], v4(bank(4 + m)), ACT.Copy)
            ins.then_inc(at_done, 1)

        def o_pe(n):
            i, b = n // 2, n % 4
            if n == 0:
                nc.tensor.wait_ge(at_done, NCH)
            if n >= 4:
                nc.tensor.wait_ge(o_lo, n - 3)
            for m, att in enumerate((att_0, att_1)):
                mm = nc.tensor.matmul(bank(b), mem_v[:, m, n * P:(n + 1) * P], att[:, i, :],
                                      start=m == 0, stop=m == 1)
            mm.then_inc(o_done, 1)

        def o_act(n):
            nc.scalar.wait_ge(o_done, n + 1)
            nc.scalar.activation(o_tiles(n)[0][:, NS:T], bank(n % 4), ACT.Copy).then_inc(o_hi, 1)

        def o_dve(n):
            nc.vector.wait_ge(o_hi, n + 1)
            hi, lo = o_tiles(n)
            nc.vector.tensor_tensor(lo[:, NS:T], bank(n % 4), f32(hi[:, NS:T]), ALU.subtract).then_inc(o_lo, 1)

        def cache_pool():
            picks_pool()
            nc.gpsimd.wait_ge(sm_stored, 32)
            for n in range(2 * NS):
                if n >= 3:
                    nc.gpsimd.wait_ge(cache_used, n - 2)
                if n == NS:
                    pick_rows_pool()
                nc.gpsimd.dma_start(cache[:, n % 3, :], A["cache"][n]).then_inc(cache_loaded[n % 3], 16)

        def s_softmax_pe():
            nc.tensor.wait_ge(cache_used, NS)
            for m in range(MT):
                mm = nc.tensor.transpose(bank(6, P, m * P, rows=NROW), att_c[:, 0, m * NROW:(m + 1) * NROW], ident)
            mm.then_inc(srow_done, 1)

        def s_max_dve():
            nc.vector.wait_ge(srow_done, 1)
            own_v.do(nc.vector.tensor_reduce(s_stat[:, 0:1], bank(6, MEM, rows=NROW), AX_X, ALU.max))
            nc.vector.tensor_scalar(s_stat[:, 0:1], s_stat[:, 0:1], -X_SCALE, None, ALU.mult).then_inc(smx_done, 1)

        def s_exp_act():
            nc.scalar.wait_ge(smx_done, 1)
            nc.scalar.activation(s_rows[:, :], bank(6, MEM, rows=NROW), ACT.Exp, bias=s_stat[:, 0:1], scale=X_SCALE,
                                 accum_out=s_stat[:, 1:2]).then_inc(sex_done, 1)

        def s_probs_dve():
            nc.vector.wait_ge(sex_done, 1)
            own_v.do(nc.vector.reciprocal(s_stat[:, 2:3], s_stat[:, 1:2]))
            nc.vector.tensor_scalar(s_rows[:, :], s_rows[:, :], s_stat[:, 2:3], None, ALU.mult).then_inc(spr_done, 1)

        def s_probs_act():
            nc.scalar.wait_ge(spr_done, 1)
            nc.scalar.wait_ge(unit_done, W_XQ.u0 + 8)
            nc.scalar.activation(sr_hi, s_rows[:, :], ACT.Copy).then_inc(sr_hi_done, 1)

        def s_lo_dve():
            nc.vector.wait_ge(sr_hi_done, 1)
            nc.vector.tensor_tensor(sr_lo, s_rows[:, :], f32(sr_hi), ALU.subtract).then_inc(sr_lo_done, 1)

        def s_spread_pe(b):
            if b == 0:
                nc.tensor.wait_ge(sr_lo_done, 1)
                nc.tensor.wait_ge(picks_made, 2)
            elif b == 1:
                nc.tensor.wait_ge(at_done, NCH)
            else:
                nc.tensor.wait_ge(cache_used, NS + b - 1)
            for i in range(XH):
                at = (6 - 2 * (b % 2)) * BANK + i * MEM
                nc.tensor.matmul(ps[:, at:at + MEM], pick_r[:, b * XH + i, :], sr_lo, start=True, stop=False)
                mm = nc.tensor.matmul(ps[:, at:at + MEM], pick_r[:, b * XH + i, :], sr_hi, start=False, stop=True)
            mm.then_inc(ab_done, 1)

        def s_values_dve(b):
            n = NS + b
            nc.vector.wait_ge(cache_loaded[n % 3], 16 * (n // 3 + 1))
            nc.vector.wait_ge(ab_done, b + 1)
            for t in range(DT):
                values, at = cache[:, n % 3, t * MEM:(t + 1) * MEM], (6 - 2 * (b % 2)) * BANK + (t // 2) * MEM
                ins = nc.vector.tensor_tensor_reduce(values, values, ps[:, at:at + MEM], 1.0, 0.0, ALU.mult, ALU.add,
                                                     att_c[:, 1, t * NS + b:t * NS + b + 1])
            ins.then_inc(cache_used, 1)

        def so_act():
            nc.scalar.wait_ge(cache_used, 2 * NS)
            for a, hi in enumerate((oa_hi, ob_hi)):
                ins = nc.scalar.activation(hi[:, :, 0:NS], v4(att_c[:, 1, a * 4 * NS:(a + 1) * 4 * NS]), ACT.Copy)
            ins.then_inc(so_hi, 1)

        def so_dve():
            nc.vector.wait_ge(so_hi, 1)
            for a, (hi, lo) in enumerate(((oa_hi, oa_lo), (ob_hi, ob_lo))):
                ins = nc.vector.tensor_tensor(lo[:, :, 0:NS], v4(att_c[:, 1, a * 4 * NS:(a + 1) * 4 * NS]),
                                              f32(hi[:, :, 0:NS]), ALU.subtract)
            ins.then_inc(so_lo, 1)

        def att_pe():
            q_rows_pe(XH - 1)
            score_pe(0)
            q_spread_pe(XH - 1)
            score_pe(1)
            s_softmax_pe()
            turn_pe(0)
            score_pe(2)
            turn_pe(1)
            score_pe(3)
            s_spread_pe(0)
            turn_pe(2)
            turn_pe(3)
            for n in range(8):
                o_pe(n)
                if n < 7:
                    s_spread_pe(n + 1)
            nc.tensor.wait_ge(so_lo, 1)

        def att_act():
            q_rows_act(XH - 1)
            softmax_act(0)
            softmax_act(1)
            s_exp_act()
            turned_act(0)
            softmax_act(2)
            s_probs_act()
            turned_act(1)
            softmax_act(3)
            turned_act(2)
            turned_act(3)
            for n in range(8):
                o_act(n)
            so_act()

        def att_dve():
            q_rows_dve(XH - 1)
            softmax_dve(0)
            s_scores_dve(XH - 1)
            probs_dve(0)
            softmax_dve(1)
            s_max_dve()
            probs_dve(1)
            s_probs_dve()
            softmax_dve(2)
            s_lo_dve()
            probs_dve(2)
            softmax_dve(3)
            probs_dve(3)
            for b in range(NS):
                s_values_dve(b)
                o_dve(b)
            so_dve()

        def final_dve():
            norm_diag_dve("final")
            nc.vector.wait_ge(rstd_done, NORM_AT["final"] + 1)
            nc.vector.wait_ge(unit_done, UNITS)
            for k in range(DT):
                normed("final", lambda k: h[:, k, :])(k, y_out[:, k, :]).then_inc(xf_done, 1)


        LAST_UNIT = [UNITS if len(PLAN) == 4 else STAGES[{"ffn1": "qk", "mix": "xq", "xattn": "up2"}[PLAN[-1]]].u0]
        block = ctx.enter_context(nc.Block())

        def load_unit(v, j, src, cols, first=False):
            if not first:
                nc.sync.wait_ge(w_lo, v - RAW + 1)
            nc.sync.dma_start(w_raw[j % RAW][:, 0:cols], src).then_inc(w_loaded[j % RAW], 16)

        @block.sync
        def _(sp):
            sp.dma_start(gains[:, :], A["gains"]).then_inc(gains_loaded, 16)
            sp.dma_start(h[:, 0:2, :], A["xT"][:, 0:2, :]).then_inc(h_loaded[0], 16)
            for name, st in STAGES.items():
                if st.u0 >= LAST_UNIT[0]:
                    break
                src = A["w_" + name]
                head = RAW if st.u0 == 0 else 0
                for n in range(head):
                    load_unit(n, n, src[n], st.cols, first=True)
                    if n == 0:
                        for q in range(1, 4):
                            sp.dma_start(h[:, 2 * q:2 * q + 2, :], A["xT"][:, 2 * q:2 * q + 2, :]).then_inc(h_loaded[q], 16)
                    else:
                        sp.dma_start(square[:, :], A["c_square"]).then_inc(square_loaded, 16)
                with sp.Fori(head // 2, st.units // 2) as i:
                    for j in range(2):
                        load_unit(i * 2 + (st.u0 + j), (st.u0 + j) % 2,
                                  src[bass.ds(i * 2 + j, 1)].rearrange("o p c -> (o p) c"), st.cols)
            r = NORM_AT["final"]
            if len(PLAN) == 4:
                for k in range(0, DT, 2):
                    sp.wait_ge(xf_done, MADE0["final"] + k + 2)
                    sp.dma_start(A["o_y"][:, k:k + 2, :], y_out[:, k:k + 2, :]).then_inc(y_stored, 16)
                sp.wait_ge(y_stored, 16 * (DT // 2))

        @block.scalar
        def _(act):
            act.sem_inc(pair_free[0], 1)
            act.sem_inc(pair_free[1], 1)
            split_first(0)
            act.wait_ge(gains_loaded, 16)
            for n in range(DT):
                if n % 2 == 0:
                    act.wait_ge(h_loaded[n // 2], 16)
                gained_hi("ffn1", n, h[:, n, :], x_hi[:, n, :])
                norm_square("ffn1", n, h[:, n, :])
                if n in (1, 5):
                    split_first(1 + n // 4)
            act.wait_ge(square_loaded, 16)
            ffn_act("up1", "down1", "ffn1", "mix", 0)
            if len(PLAN) > 1:
                norm_of_h_act("mix")
                qk_act()
                v_act()
                xbc_act()
                gz_act()
                xkv_act()
                residual_act(W_OUT, "x")
            if len(PLAN) > 2:
                norm_of_h_act("x")
                xq_act()
                att_act()
                residual_act(W_XO, "ffn2")
            if len(PLAN) > 3:
                act.wait_ge(mem_stored, 32)
                ffn_act("up2", "down2", "ffn2", "final", 1)
                norm_rows_act("final")
                norm_rstd_act("final")

        @block.vector
        def _(dve):
            unit_lo(0, 0, UNIT_COLS[0])
            dve.wait_ge(gains_loaded, 16)
            for n in range(DT):
                gained_lo("ffn1", n, h[:, n, :], x_hi[:, n, :], x_lo[:, n, :], n + 1)
                if n in (1, 5):
                    unit_lo(1 + n // 4, 1 + n // 4, UNIT_COLS[1])
            dve.wait_ge(square_loaded, 16)
            ffn_dve("up1", "down1", "ffn1", "mix", 0)
            if len(PLAN) > 1:
                norm_of_h_dve("mix")
                qk_dve()
                v_dve()
                xbc_dve()
                gz_dve()
                xkv_dve()
                residual_dve(W_OUT, "x")
            if len(PLAN) > 2:
                norm_of_h_dve("x")
                xq_dve()
                att_dve()
                residual_dve(W_XO, "ffn2")
            if len(PLAN) > 3:
                dve.wait_ge(mem_stored, 32)
                ffn_dve("up2", "down2", "ffn2", "final", 1)
                final_dve()

        @block.tensor
        def _(pe):
            pe.wait_ge(square_loaded, 16)
            ffn_pe("up1", "down1", "ffn1", 0)
            if len(PLAN) > 1:
                gemm(W_QK, x_tiles, x_lo_done, SPLIT0["mix"], norm="mix")
                v_pe()
                xbc_pe()
                gz_pe()
                xkv_pe()
                gemm(W_OUT, out_tiles, x_lo_done, SPLIT0["ret"])
            if len(PLAN) > 2:
                xq_pe()
                att_pe()
                gemm(W_XO, o_tiles, o_lo, 0)
            if len(PLAN) > 3:
                ffn_pe("up2", "down2", "ffn2", 1)
                norm_rows_pe("final", inv_d)
                norm_spread_pe("final")

        @block.gpsimd
        def _(pool):
            norm_clear(pool)
            for n in range(DT):
                norm_add("ffn1", n, eng=pool)
            if len(PLAN) > 1:
                pool.wait_ge(unit_done, U_MIX)
                for dst, src in ((rope[:, :, :], "c_rope"), (c_ret[:, :], "c_ret"), (triangle[:, :], "c_triangle"),
                                 (small[:, :], "small"), (wdt[:, :], "wdt"), (conv_s[:, 0:TAPS - 1, :], "conv_s")):
                    pool.dma_start(dst, A[src]).then_inc(mix_loaded, 16)
                nc.gpsimd.memset(conv_in[:, :, 0:TAPS - 1], 0.0).then_inc(pads_clear, 1)
                pool.wait_ge(ret_s_done, NCH)
                pool.dma_start(A["o_ret_p"], ret_s[:, (NCH - 1) % 2, :]).then_inc(ret_stored, 16)
                pool.wait_ge(ret_stored, 16)
                pool.dma_start(mem_t[:, :, :], A["memT"]).then_inc(mem_loaded, 16)
                au_pool(0)
                for c in range(NCH):
                    ssd_pool(c)
                pool.wait_ge(ssd_s_done, NCH)
                pool.dma_start(A["o_ssm_p"], ssd_s[:, :]).then_inc(ssm_stored, 16)
                pool.wait_ge(ssm_stored, 16)
                pool.wait_ge(conv_s_sum, 1)
                pool.dma_start(A["o_conv_p"], conv_last[:, :, :]).then_inc(ssm_stored, 16)
                pool.dma_start(A["o_conv_s"], conv_s[:, 1:TAPS, :]).then_inc(ssm_stored, 16)
                smp_pool()
                pool.wait_ge(rs_loaded[0], 32)
            if len(PLAN) > 2:
                pool.wait_ge(unit_done, W_XK.u0 + 8)
                for pr in range(2):
                    pool.wait_ge(pair_free[pr], W_XV.freed)
                pool.dma_start(A["o_mem_k"], mem_k[:, :, :]).then_inc(mem_stored, 16)
                for pr in range(2):
                    pool.wait_ge(pair_free[pr], W_OUT.freed)
                pool.dma_start(A["o_mem_v"], mem_v[:, :, :]).then_inc(mem_stored, 16)
                cache_pool()
                pool.wait_ge(ssm_stored, 48)
                pool.wait_ge(sm_stored, 32)
                pool.wait_ge(mem_stored, 32)


def tiled(w):
    k, n = w.shape
    return w.reshape(k // P, P, n // P, P).transpose(2, 1, 0, 3).reshape(n // P, P, -1)


def feature_major(x):
    return x.T.reshape(-1, P, x.shape[0]).transpose(1, 0, 2)


def columns(v):
    return v.reshape(-1, P).T


def lay_out(i):
    i = {k: np.asarray(v) for k, v in i.items()}
    a = dict(tables())
    cat = np.concatenate
    a["xT"] = feature_major(cat([i["x_sample"][:, 0], i["x_prompt"][0]], 0))
    a["gains"] = cat([columns(i[n].reshape(-1)) for n in
                      ("ffn1_norm", "mem_norm", "mix_norm", "x_norm", "ffn2_norm", "final_norm", "ret_gn_gain",
                       "ssd_norm")], 1)
    for f in ("1", "2"):
        up = [tiled(i[f"ffn{f}_w{w}"][0]) for w in ("1", "3")]
        a["w_up" + f] = np.stack(up, 1).reshape(2 * FT, P, -1)
        down = i[f"ffn{f}_w2"][0].reshape(2, KH, P, DT, P)
        a["w_down" + f] = down.transpose(3, 0, 2, 1, 4).reshape(2 * DT, P, -1)
    w_in = i["w_in"][0]
    a["w_qk"] = tiled(w_in[:, 0:1024])
    a["w_v"] = w_in[:, 1024:1536].reshape(4, 2, P, 512).transpose(0, 2, 1, 3).reshape(4, P, 1024)
    a["w_gz"] = tiled(w_in[:, 1536:2560])
    a["w_xbc"] = tiled(w_in[:, 2560:3584])
    a["wdt"] = w_in[:, 3584:].reshape(DT, P, HS).transpose(1, 0, 2).reshape(P, DT * HS)
    a["small"] = cat([i["conv_w"][0].reshape(TAPS, 8, P).transpose(2, 0, 1).reshape(P, TAPS * 8),
                      columns(i["conv_b"][0]), np.broadcast_to(i["dt_bias"][0], (P, HS)),
                      np.broadcast_to(i["A_log"][0], (P, HS)),
                      columns(np.repeat(i["D_skip"][0], HP))], 1)
    a["conv_s"] = i["state_conv"][0].reshape(NS, TAPS - 1, 8, P).transpose(3, 1, 2, 0).reshape(P, TAPS - 1, 8 * NS)
    a["memT"] = feature_major(i["mem_prompt"][0])
    a["w_out"] = tiled(i["w_out"][0])
    a["w_xk"], a["w_xq"], a["w_xo"] = tiled(i["w_xk"][0]), tiled(i["w_xq"][0]), tiled(i["w_xo"][0])
    a["w_xv"] = i["w_xv"][0].reshape(8, P, D)
    a["st_ret"] = i["state_ret"][0].transpose(1, 2, 0, 3).reshape(HR, P, NS * P)
    a["st_ssm"] = i["state_ssm"][0].reshape(NS, SG, 4, HP, P).transpose(1, 4, 0, 2, 3).reshape(SG, P, -1)
    keys = i["cache_mem_k"][0].reshape(2, 4, MT, P, XH, D // XH).transpose(4, 0, 3, 1, 2, 5).reshape(2 * XH, P, -1)
    values = i["cache_mem_v"][0].reshape(NS, MEM, DT, P).transpose(0, 3, 2, 1).reshape(NS, P, DT * MEM)
    a["cache"] = cat([keys, values], 0)
    return a


OUTS = {"o_y": (P, DT, T), "o_ret_p": (P, HR * P), "o_ssm_p": (P, HS * HP), "o_conv_p": (P, 8, TAPS - 1),
        "o_conv_s": (P, TAPS - 1, 8 * NS), "o_ret_s": (HR, P, NS * P), "o_ssm_s": (SG, P, NS * 4 * HP),
        "o_mem_k": (P, DT, MEM), "o_mem_v": (P, MT, D)}


def give(r):
    y = r["o_y"].transpose(2, 1, 0).reshape(T, D)
    return (y[NS:].reshape(1, SEQ, D), y[:NS].reshape(NS, 1, D),
            r["o_ret_p"].reshape(P, HR, P).transpose(1, 0, 2)[None, None],
            r["o_ssm_p"].reshape(P, HS, HP).transpose(1, 2, 0)[None, None],
            r["o_conv_p"].transpose(2, 1, 0).reshape(1, 1, TAPS - 1, D),
            r["o_mem_k"].transpose(2, 1, 0).reshape(1, 1, MEM, XH, D // XH),
            r["o_mem_v"].transpose(1, 0, 2).reshape(1, 1, MEM, XH, D // XH),
            r["o_ret_s"].reshape(HR, P, NS, P).transpose(2, 0, 1, 3)[None],
            r["o_ssm_s"].reshape(SG, P, NS, 4, HP).transpose(2, 0, 3, 4, 1).reshape(1, NS, HS, HP, P),
            r["o_conv_s"].reshape(P, TAPS - 1, 8, NS).transpose(3, 1, 2, 0).reshape(1, NS, TAPS - 1, D))


def kernel(**inputs):
    import numpy as _np
    import concourse.bacc as _bacc
    from concourse.bass_utils import run_bass_kernel_spmd as _run

    nc = _bacc.Bacc("TRN2", target_bir_lowering=False, num_devices=1)
    arrays = {"in_" + n: _np.ascontiguousarray(a) for n, a in lay_out(inputs).items()}
    A = {n[3:]: nc.dram_tensor(n, a.shape, F32, kind="ExternalInput").ap() for n, a in arrays.items()}
    for n, shape in OUTS.items():
        A[n] = nc.dram_tensor(n, shape, F32, kind="ExternalOutput").ap()
    build(nc, A)
    r = _run(nc, [arrays], core_ids=[0]).results[0]
    return give(r)
```

```python
from contextlib import ExitStack

import numpy as np

import concourse.bass as bass
from concourse import mybir

F32 = mybir.dt.float32
F32R = mybir.dt.float32r
ALU = mybir.AluOpType
ACT = mybir.ActivationFunctionType
AX_X = mybir.AxisListType.X

P = 128
D = 1024
DT = D // P
SEQ = 512
NS = 8
T = NS + SEQ
HT = T // 2
BANK = 512
FF = 2816
FT = FF // P
KH = FT // 2
HR = 4
HS = 8
HP = 64
SG = 2
CH = 128
NCH = SEQ // CH
MEM = 256
MT = MEM // P
XH = 4
TAPS = 4
EPS = 1e-6
RK_SCALE = 128.0 ** -0.5
X_SCALE = 256.0 ** -0.5
NEG = -1.0e30
LOW = 32
R3 = 2 * LOW + NS
PIECE = NS * P
PIECES = 8
TOKT = 5
LEAD = 3
RING = 4
RAW = 2
GAMMA = [float(np.exp(np.log1p(-np.exp2(np.float64(-5.0 - h))))) for h in range(HR)]

STAGE_LIST = [
    ("up1", 2 * FT, 1024, FT),
    ("down1", 2 * DT, KH * P, DT // 2),
    ("qk", 8, 1024, 4),
    ("v", 4, 1024, 1),
    ("xbc", 8, 1024, 4),
    ("gz", 8, 1024, 4),
    ("xk", 8, 1024, 4),
    ("xv", 8, 1024, 1),
    ("out", 8, 1024, 4),
    ("xq", 8, 1024, 4),
    ("xo", 8, 1024, 4),
    ("up2", 2 * FT, 1024, FT),
    ("down2", 2 * DT, KH * P, DT // 2),
]

NORM_LIST = [("ffn1", 8, T), ("mix", 8, T), ("mem", 8, MEM), ("ssd", 5, T), ("x", 8, T), ("ffn2", 8, T),
             ("final", 8, T)]
SPLIT_LIST = [("ffn1", 8), ("mix", 8), ("mem", 8), ("ret", 4), ("ssd", 4), ("x", 8), ("ffn2", 8)]
MADE_LIST = [("ret", 4), ("ssd", 4), ("final", 8)]


class Stage:

    def __init__(self, name, units, cols, u0, freed):
        self.name, self.units, self.cols, self.u0, self.freed = name, units, cols, u0, freed
        self.loops = units // RING


def make_stages():
    out, u0, freed = {}, 0, 1
    for name, units, cols, tiles in STAGE_LIST:
        out[name] = Stage(name, units, cols, u0, freed)
        u0, freed = u0 + units, freed + tiles
    return out, u0


def starts(items, extra):
    out, at = {}, 0
    for it in items:
        out[it[0]] = at
        at += it[1] + extra
    return out


STAGES, UNITS = make_stages()
UNIT_COLS = [s.cols for s in STAGES.values() for _ in range(s.units)]
NORM_AT = {n[0]: i for i, n in enumerate(NORM_LIST)}
NORM_TILES = {n[0]: n[1] for n in NORM_LIST}
NORM_COLS = {n[0]: n[2] for n in NORM_LIST}
SQ0 = starts(NORM_LIST, 1)
SPLIT0 = starts(SPLIT_LIST, 0)
SPLIT_TILES = dict(SPLIT_LIST)
MADE0 = starts(MADE_LIST, 0)


def tables():
    half = 64
    inv = (10000.0 ** (-np.arange(half) / half)).astype(np.float32)
    pos = np.concatenate([np.full(NS, 4096.0), np.arange(SEQ)]).astype(np.float32)
    ang = (inv[:, None] * pos[None, :]).astype(np.float32)
    c, s = np.cos(ang), np.sin(ang)
    rope = np.stack([np.concatenate([c, c]), np.concatenate([s, -s])], 1)
    log_g = np.log1p(-np.exp2(-5.0 - np.arange(HR)))
    i = np.arange(CH)
    diff = i[None, :] - i[:, None]
    dmat = np.where(diff >= 0, np.exp(log_g[:, None, None] * np.maximum(diff, 0)), 0.0) * RK_SCALE
    q_dec = np.exp(log_g[:, None] * (i[None, :] + 1.0))
    k_dec = np.exp(log_g[None, :] * (CH - 1.0 - i[:, None])) * RK_SCALE
    ret = np.concatenate([dmat.transpose(1, 0, 2).reshape(P, -1),
                          np.broadcast_to(q_dec.reshape(1, -1), (P, HR * CH)), k_dec], 1)
    eye = np.eye(P)
    upper = (diff >= 0).astype(np.float32)
    mask = np.where(diff >= 0, 0.0, NEG)
    small = np.zeros((P, 8 + LOW))
    small[:, 8:] = i[:, None] % LOW == np.arange(LOW)[None, :]
    small[:, 0], small[:, 1], small[:, 2] = 1 / D, 1 / (HS * HP), EPS
    square = np.concatenate([eye, np.ones((P, P)), small], 1)
    triangle = np.concatenate([eye - 1.0 / P, upper, mask], 1)
    f = lambda a: np.ascontiguousarray(a, dtype=np.float32)
    own_column = np.broadcast_to(np.eye(NS).reshape(1, -1), (P, NS * NS))
    smp = np.concatenate([own_column, np.broadcast_to(np.eye(HR).reshape(1, -1) / P, (P, HR * HR))], 1)
    return {"c_smp": f(smp), "c_rope": f(rope), "c_ret": f(ret), "c_square": f(square), "c_triangle": f(triangle)}


def build(nc, A):
    ctx = ExitStack()
    with ctx:
        def sb(name, shape, dt=F32, stack=ctx):
            return stack.enter_context(nc.sbuf_tensor(name, shape, dt))

        def sem(name):
            return ctx.enter_context(nc.semaphore(name))

        ps = ctx.enter_context(nc.psum_tensor("ps", [P, 8 * BANK], F32))

        def bank(b, n=BANK, at=0, rows=P, row0=0):
            return ps[row0:row0 + rows, b * BANK + at:b * BANK + at + n]

        def half(b, x):
            return ps[:, (b + x) * BANK:(b + x) * BANK + HT]

        def tile_halves(b):
            return ps[:, b * BANK:(b + 2) * BANK].rearrange("p (a c) -> p a c", a=2)[:, :, 0:HT]

        def two(ap):
            return ap.rearrange("p (a c) -> p a c", a=2)

        def f32(ap):
            return ap.bitcast(F32)

        h = sb("h", [P, DT, T])
        x_hi = sb("x_hi", [P, DT, T], F32R)
        x_lo = sb("x_lo", [P, DT, T], F32R)
        w_raw = [sb(f"w_raw{i}", [P, KH * P]) for i in range(RAW)]
        w_hi_t = [sb(f"w_hi{i}", [P, KH * P], F32R) for i in range(RING)]
        w_lo_t = [sb(f"w_lo{i}", [P, KH * P], F32R) for i in range(RING)]
        gains = sb("gains", [P, 6 * DT + HR + HR])
        square = sb("square", [P, 2 * P + 8 + LOW])
        xf = sb("xf", [P, 2, T])
        sq = sb("sq", [P, 2, T])
        sq_sum = sb("sq_sum", [P, T])
        rstd = sb("rstd", [P, T])
        row_std = sb("row_std", [P, 2, TOKT + MT])
        diag = sq[:, :, :].rearrange("p a c -> p (a c)")[:, 0:TOKT * P].rearrange("p (t c) -> p t c", t=TOKT)
        ident, ones = (square[:, i * P:(i + 1) * P] for i in range(2))
        inv_d, inv_512, eps = (square[:, 2 * P + i:2 * P + i + 1] for i in range(3))
        fold = square[:, 2 * P + 8:2 * P + 8 + LOW]
        GAIN0 = {"ffn1": 0, "mem": 8, "mix": 16, "x": 24, "ffn2": 32, "final": 40, "ret": 48, "ssd": 52}

        def gain(name, k):
            return gains[:, GAIN0[name] + k:GAIN0[name] + k + 1]

        ffn = ExitStack()
        gu_hi = sb("gu_hi", [P, FT, T], F32R, ffn)
        gu_lo = sb("gu_lo", [P, FT, T], F32R, ffn)
        ffn.close()

        mix = ExitStack()

        def region(name, cols, *groups):
            out = []
            for g in groups:
                part = ExitStack()
                out += [sb(n, shape, F32R if n.endswith("_hi") or n.endswith("_lo") else F32, part)
                        for n, shape in g]
                part.close()
            sb("hold_" + name, [P, cols], F32, mix)
            return out

        HT4 = 4 * T
        q_t, att_p, oa_lo = region("q", HT4, [("q_t", [P, HR, T])], [("att_p", [P, 2, XH * MEM])],
                           [("oa_lo", [P, 4, T])])
        k_t, gn_s, mem_v = region("k", HT4, [("k_t", [P, HR, T])], [("gn_s", [P, HR, T])], [("mem_v", [P, MT, D])])
        cx, qx_a, oa_hi = region("cx", HT4, [("cx", [P, 4, T])], [("qx_a", [P, 4, T])], [("oa_hi", [P, 4, T])])
        cb, ssd_hi, qx_b, ob_hi = region("cb", HT4, [("cb", [P, 4, T])], [("ssd_hi", [P, 4, T])],
                                         [("qx_b", [P, 4, T])], [("ob_hi", [P, 4, T])])
        g_t, ret_lo, pick_q_hi, qr_hi, att_0 = region("g", HT4, [("g_t", [P, HR, T])],
                                                             [("ret_lo", [P, HR, T])],
                                                             [("pick_q_hi", [LOW + NS, NS, P]),
                                                              ("qr_hi", [LOW + NS, 2 * P])],
                                                             [("att_0", [P, XH, SEQ])])
        z_t, ssd_lo, att_1 = region("z", HT4, [("z_t", [P, 4, T])], [("ssd_lo", [P, 4, T])],
                                    [("att_1", [P, XH, SEQ])])
        ret_s, c_ret, mem_t, mem_k, ob_lo = region("h", HT4,
                                            [("ret_s", [P, 2, HR * P]), ("c_ret", [P, 2 * HR * CH + HR])],
                                            [("mem_t", [P, 8, MEM])], [("mem_k", [P, 8, MEM])],
                                            [("ob_lo", [P, 4, T])])
        (v_t, ret_w, ret_k, ret_qd, rope, conv_in,
         ssd_au, ssd_l, ssd_e, xdt, xdd, b_tok, _, ssd_sd, ssd_s,
         ks_hi, xdts_hi, bs_hi, dm, decb, blocks_hi, state,
         ret_hi,
         cache, s_rows, s_stat, y_out) = region("scratch", 6528,
                         [("v_t", [P, NCH, HR * P]), ("ret_w", [P, HR * CH]), ("ret_k", [P, HR * P]),
                          ("ret_qd", [P, HR * CH]), ("rope", [P, 2, T]), ("conv_in", [P, 2, SEQ + TAPS - 1])],
                         [("ssd_au", [P, HS * CH]), ("ssd_l", [P, HS * CH]), ("ssd_e", [P, HS * CH]),
                          ("xdt", [P, HS * HP]), ("xdd", [P, HS * HP]), ("b_tok", [P, SG * P]),
                          ("to_third_buffer", [P, 128]), ("ssd_sd", [P, HS * HP]), ("ssd_s", [P, HS * HP])],
                         [("ks_hi", [R3, HR * P]), ("xdts_hi", [R3, HS * HP]), ("bs_hi", [R3, SG * P]),
                          ("dm", [NS, NS * HS]), ("decb", [P, NS * HS]), ("blocks_hi", [R3, 2, PIECE]),
                          ("state", [P, 3, PIECE])],
                         [("ret_hi", [P, HR, T])],
                         [("cache", [P, 3, 2048]), ("s_rows", [NS * XH, MEM]), ("s_stat", [NS * XH, 4])],
                         [("y_out", [P, DT, T])])
        vs = sb("vs", [R3, HR * P], F32R, mix)
        triangle = sb("triangle", [P, 3 * P], F32, mix)
        centre, upper, mask = (triangle[:, i * P:(i + 1) * P] for i in range(3))
        small = sb("small", [P, TAPS * 8 + 8 + 8 + 8 + 4], F32, mix)
        conv_w = small[:, 0:TAPS * 8].rearrange("p (t n) -> p t n", t=TAPS)
        conv_b, dt_bias, a_log, d_skip = small[:, 32:40], small[:, 40:48], small[:, 48:56], small[:, 56:60]
        conv_s = sb("conv_s", [P, TAPS, 8 * NS], F32, mix)
        conv_last = sb("conv_last", [P, 8, TAPS - 1], F32, mix)
        wdt = sb("wdt", [P, DT * HS], F32, mix)
        wdt_hi = sb("wdt_hi", [P, DT * HS], F32R, mix)
        wdt_lo = sb("wdt_lo", [P, DT * HS], F32R, mix)
        NDT = TOKT * HS
        dts = sb("dts", [P, 10, NDT], F32, mix)
        dt_x, dt_ab, dt_e, dt_u, dt_d, dt_m, dt_t, a_dt, dt_r, a_cum = (dts[:, i, :] for i in range(10))
        a_exp = sb("a_exp", [P, HS], F32, mix)
        decay = sb("decay", [P, 2, NCH * HS], F32, mix)
        att_s = sb("att_s", [P, 2, 3 * XH], F32, mix)
        att_c = sb("att_c", [P, 2, 4 * NS * 2], F32, mix)

        def chunk(c):
            return slice(NS + c * CH, NS + (c + 1) * CH)

        def conv_tile(n):
            return cx[:, n, :] if n < 4 else cb[:, n - 4, :]

        def qx(n):
            return qx_a[:, n, :] if n < 4 else qx_b[:, n - 4, :]

        def o_tiles(n):
            return (oa_hi[:, n, :], oa_lo[:, n, :]) if n < 4 else (ob_hi[:, n - 4, :], ob_lo[:, n - 4, :])

        def flat(t):
            return t[:, :, :].rearrange("p k c -> p (k c)")

        def m_tile(t, k):
            return flat(t)[:, k * MEM:(k + 1) * MEM]

        y_rows = cb[0:NS, 0, NS:T]
        q_mask, c_mask = cb[:, 1, NS:NS + HR * NS * NS], cb[:, 1, NS + HR * NS * NS:NS + (HR + SG) * NS * NS]
        gn_inv, gn_inv_s = cb[0:HR, 2, NS:T], cb[0:HR, 3, NS:2 * NS]
        c_smp = cb[:, 3, 2 * NS:2 * NS + NS * NS + HR * HR]
        own_column, pick_mean = c_smp[:, 0:NS * NS], c_smp[:, NS * NS:NS * NS + HR * HR]

        pick_h = flat(x_hi)[0:LOW + HR, DT * MEM:DT * MEM + HR * P].rearrange("p (h c) -> p h c", h=HR)
        inv_parts = flat(x_lo)[0:LOW + HR, DT * MEM:DT * MEM + T]
        inv_hi, inv_lo = inv_parts[0:HR, :], inv_parts[LOW:LOW + HR, :]

        pick_r = flat(x_hi)[0:LOW + NS * XH, 0:NS * XH * P].rearrange("p (r c) -> p r c", r=NS * XH)
        sr = flat(x_lo)[0:LOW + NS * XH, 0:MEM]

        mix.close()

        gains_loaded = sem("gains_loaded")
        square_loaded = sem("square_loaded")
        h_loaded = [sem(f"h_loaded{i}") for i in range(4)]
        w_loaded = [sem(f"w_loaded{i}") for i in range(RAW)]
        w_hi = sem("w_hi")
        w_lo = sem("w_lo")
        unit_done = sem("unit_done")
        pair_free = [sem("pair0_free"), sem("pair1_free")]
        gu_hi_done = sem("gu_hi_done")
        gu_lo_done = sem("gu_lo_done")
        sq_done = sem("sq_done")
        sq_added = sem("sq_added")
        rows_done = sem("rows_done")
        row_std_done = sem("row_std_done")
        row_inv_done = sem("row_inv_done")
        diag_done = sem("diag_done")
        spread_done = sem("spread_done")
        rstd_done = sem("rstd_done")
        xf_done = sem("xf_done")
        x_hi_done = sem("x_hi_done")
        x_lo_done = sem("x_lo_done")
        y_stored = sem("y_stored")

        def unit_hi(v, j, cols):
            nc.scalar.wait_ge(w_loaded[j % RAW], w_load_count(v, j))
            nc.scalar.wait_ge(unit_done, v - RING + 1)
            nc.scalar.activation(w_hi_t[j][:, 0:cols], w_raw[j % RAW][:, 0:cols], ACT.Copy).then_inc(w_hi, 1)

        def w_load_count(v, j):
            if isinstance(v, int):
                return 16 * (v // 2 + 1)
            return (v - j) * 8 + 16 * (j // 2 + 1)

        def unit_lo(v, j, cols):
            nc.vector.wait_ge(w_hi, v + 1)
            nc.vector.tensor_tensor(w_lo_t[j][:, 0:cols], w_raw[j % RAW][:, 0:cols], f32(w_hi_t[j][:, 0:cols]),
                                    ALU.subtract).then_inc(w_lo, 1)

        def ahead(split, stage, i, j):
            if isinstance(i, int):
                v = stage.u0 + RING * i + j + LEAD
                if v < UNITS:
                    if v < RING and split is unit_hi:
                        split_first(v)
                    else:
                        split(v, v % RING, UNIT_COLS[v])
            else:
                split(i * RING + (stage.u0 + j + LEAD), (j + LEAD) % RING, stage.cols)

        def split_first(v):
            nc.scalar.wait_ge(w_loaded[v % RAW], 16 * (v // RAW + 1))
            nc.scalar.activation(w_hi_t[v][:, 0:UNIT_COLS[v]], w_raw[v % RAW][:, 0:UNIT_COLS[v]],
                                 ACT.Copy).then_inc(w_hi, 1)

        def turns(eng, stage, body):
            first = 1 if stage.u0 == 0 else 0
            if stage.loops > 2:
                if first:
                    body(0)
                with eng.Fori(first, stage.loops - 1) as i:
                    body(i)
                body(stage.loops - 1)
            else:
                for i in range(stage.loops):
                    body(i)

        def three(out, w_h, w_l, m_h, m_l, start, stop):
            nc.tensor.matmul(out, w_h, m_l, start=start, stop=False)
            nc.tensor.matmul(out, w_l, m_h, start=False, stop=False)
            return nc.tensor.matmul(out, w_h, m_h, start=False, stop=stop)

        def tile_products(slot, blocks, b, operand, k0, first, last, width=T, ready=None, within=None):
            n = width // 2 if width > BANK else width
            mm = None
            for kk in range(blocks):
                if ready:
                    nc.tensor.wait_ge(ready[0], ready[1] + k0 + kk + 1)
                w_h, w_l = (w[slot][:, kk * P:(kk + 1) * P] for w in (w_hi_t, w_lo_t))
                m_h, m_l = operand(k0 + kk)
                s, e = first and kk == 0, last and kk == blocks - 1
                for a in range(width // n):
                    cut = slice(a * n, (a + 1) * n)
                    mm = three(ps[:, (b + a) * BANK:(b + a) * BANK + n], w_h, w_l, m_h[:, cut], m_l[:, cut], s, e)
                if within and kk == blocks // 2:
                    within()
            return mm

        def gemm(stage, operand, ready, ready0, per_tile=1, width=T, after=None, norm=None):
            blocks = stage.cols // P

            def turn(i, norm=None):
                for j in range(RING):
                    u = i * RING + (stage.u0 + j)
                    tile = j // per_tile
                    b = 2 * (tile % 2)
                    first, last = j % per_tile == 0, j % per_tile == per_tile - 1
                    nc.tensor.wait_ge(w_lo, u + 1)
                    if first:
                        nc.tensor.wait_ge(pair_free[tile % 2],
                                          i * (RING // per_tile // 2) + (stage.freed + tile // 2))
                    tile_products(j, blocks, b, operand, (j % per_tile) * blocks, first, last, width,
                                  (ready, ready0) if tile == 0 else None,
                                  (lambda: norm_spread_pe(norm)) if norm and j == 1 else None).then_inc(unit_done, 1)
                    if norm and j == 0:
                        norm_rows_pe(norm, inv_d)
                    if after:
                        after(i * RING + j)

            if after:
                for i in range(stage.loops):
                    turn(i, norm if i == 0 else None)
            elif norm:
                turn(0, norm)
                with nc.tensor.Fori(1, stage.loops) as i:
                    turn(i)
            else:
                with nc.tensor.Fori(0, stage.loops) as i:
                    turn(i)

        def norm_clear(eng=nc.vector):
            eng.memset(sq_sum[:, :], 0.0).then_inc(sq_added, 1)

        def norm_square(name, n, source, i=None):
            w = NORM_COLS[name]
            nc.scalar.wait_ge(sq_added, SQ0[name] + n if i is None else i * 2 + (SQ0[name] + n))
            nc.scalar.activation(sq[:, n % 2, 0:w], source, ACT.Square).then_inc(sq_done, 1)

        SQD0 = starts(NORM_LIST, 0)

        def norm_add(name, n, i=None, eng=nc.vector):
            w = NORM_COLS[name]
            a, b = SQD0[name] + n + 1, SQ0[name] + n + 1
            eng.wait_ge(sq_done, a if i is None else i * 2 + a)
            eng.wait_ge(sq_added, b if i is None else i * 2 + b)
            eng.tensor_tensor(sq_sum[:, 0:w], sq_sum[:, 0:w], sq[:, n % 2, 0:w],
                                    ALU.add).then_inc(sq_added, 1)

        def row_tiles(w):
            if w == MEM:
                return [(t * P, P, t * P) for t in range(MT)]
            return [(NS + c * CH, CH, c * CH) for c in range(NCH)] + [(0, NS, SEQ)]

        def norm_rows_pe(name, inv_n):
            w = NORM_COLS[name]
            if name == "ffn1":
                nc.tensor.wait_ge(square_loaded, 16)
            nc.tensor.wait_ge(sq_added, SQ0[name] + NORM_TILES[name] + 1)
            for t, (c0, _, _) in enumerate(row_tiles(w)):
                mm = nc.tensor.matmul(bank(6, 1, t), sq_sum[:, c0:c0 + P], inv_n, start=True, stop=True)
            mm.then_inc(rows_done, 1)

        def row_parts(name):
            n, at = len(row_tiles(NORM_COLS[name])), TOKT if name == "mem" else 0
            return row_std[:, 0, at:at + n], row_std[:, 1, at:at + n], n

        def norm_rows_act(name):
            root, _, n = row_parts(name)
            nc.scalar.wait_ge(rows_done, NORM_AT[name] + 1)
            nc.scalar.activation(root, bank(6, n), ACT.Sqrt, bias=eps).then_inc(row_std_done, 1)

        def norm_diag_dve(name):
            root, inv, n = row_parts(name)
            r = NORM_AT[name]
            nc.vector.wait_ge(row_std_done, r + 1)
            nc.vector.reciprocal(inv, root).then_inc(row_inv_done, 1)
            nc.vector.wait_ge(row_inv_done, r + 1)
            nc.vector.tensor_tensor(diag[:, 0:n, :], ident.unsqueeze(1).to_broadcast([P, n, P]),
                                    inv.unsqueeze(2).to_broadcast([P, n, P]),
                                    ALU.mult).then_inc(diag_done, 1)

        def norm_spread_pe(name, b=4):
            nc.tensor.wait_ge(diag_done, NORM_AT[name] + 1)
            for t, (_, n, to) in enumerate(row_tiles(NORM_COLS[name])):
                mm = nc.tensor.matmul(ps[:, b * BANK + to:b * BANK + to + n], ones, diag[:, t, 0:n],
                                      start=True, stop=True)
            mm.then_inc(spread_done, 1)

        def norm_rstd_act(name, b=4):
            w = NORM_COLS[name]
            nc.scalar.wait_ge(spread_done, NORM_AT[name] + 1)
            lead = w % P
            if lead:
                nc.scalar.activation(rstd[:, 0:lead], bank(b + 1, lead), ACT.Copy)
            nc.scalar.activation(rstd[:, lead:w], bank(b, w - lead), ACT.Copy).then_inc(rstd_done, 1)


        def gained_hi(name, k, source, dest):
            nc.scalar.activation(dest, source, ACT.Copy, scale=gain(name, k)).then_inc(x_hi_done, 1)

        def gained_lo(name, k, source, hi, dest, count):
            nc.vector.wait_ge(x_hi_done, count)
            nc.vector.scalar_tensor_tensor(out=dest, in0=source, scalar=gain(name, k), in1=f32(hi), op0=ALU.mult,
                                           op1=ALU.subtract).then_inc(x_lo_done, 1)

        def x_tiles(k):
            return x_hi[:, k, :], x_lo[:, k, :]

        def norm_of_h_act(name):
            norm_rows_act(name)
            norm_rstd_act(name)

        def norm_of_h_dve(name):
            norm_diag_dve(name)
            nc.vector.wait_ge(rstd_done, NORM_AT[name] + 1)

        def h_tile_act(name, n, i=None):
            k = n if i is None else i * 2 + n
            norm_square(name, n, h[:, k, :], i)
            if isinstance(k, int):
                nc.scalar.activation(x_hi[:, k, :], h[:, k, :], ACT.Copy, scale=gain(name, k)).then_inc(x_hi_done, 1)
            else:
                nc.scalar.activation(x_hi[:, k, :], h[:, k, :], ACT.Copy,
                                     scale=gains[:, bass.ds(k + GAIN0[name], 1)]).then_inc(x_hi_done, 1)

        def h_tile_dve(name, n, i=None):
            k = n if i is None else i * 2 + n
            g = gain(name, k) if isinstance(k, int) else gains[:, bass.ds(k + GAIN0[name], 1)]
            nc.vector.wait_ge(x_hi_done, k + (SPLIT0[name] + 1))
            nc.vector.scalar_tensor_tensor(out=x_lo[:, k, :], in0=h[:, k, :], scalar=g, in1=f32(x_hi[:, k, :]),
                                           op0=ALU.mult, op1=ALU.subtract).then_inc(x_lo_done, 1)
            norm_add(name, n, i)

        silu_done = sem("silu_done")
        gu_done = sem("gu_done")

        def ffn_pe(up, down, norm, f):
            gemm(STAGES[up], x_tiles, x_lo_done, SPLIT0[norm], norm=norm)
            gemm(STAGES[down], lambda k: (gu_hi[:, k, :], gu_lo[:, k, :]), gu_lo_done, f * FT, per_tile=2)

        def ffn_act(up, down, norm, next_norm, f):
            up, down = STAGES[up], STAGES[down]
            norm_of_h_act(norm)

            def up_turn(i):
                for j in range(RING):
                    jj = j // 2
                    if j % 2 == 0:
                        ahead(unit_hi, up, i, j)
                        nc.scalar.wait_ge(pair_free[0], i * 2 + (up.freed + jj + 1))
                        nc.scalar.activation(sq[:, 0, :], sq[:, 0, :], ACT.Silu).then_inc(silu_done, 1)
                    else:
                        ahead(unit_hi, up, i, j)
                        nc.scalar.wait_ge(gu_done, i * 2 + (f * FT + jj + 1))
                        nc.scalar.activation(gu_hi[:, i * 2 + jj, :], xf[:, jj, :], ACT.Copy).then_inc(gu_hi_done, 1)

            def down_turn(i):
                for j in range(RING):
                    ahead(unit_hi, down, i, j)
                    if j % 2:
                        nc.scalar.wait_ge(pair_free[j // 2], i + (down.freed + 1))
                        if next_norm == "final":
                            norm_square(next_norm, j // 2, h[:, i * 2 + j // 2, :], i)
                        else:
                            h_tile_act(next_norm, j // 2, i)

            turns(nc.scalar, up, up_turn)
            turns(nc.scalar, down, down_turn)

        def ffn_dve(up, down, norm, next_norm, f):
            up, down = STAGES[up], STAGES[down]
            norm_of_h_dve(norm)

            def up_turn(i):
                for j in range(RING):
                    jj, product = j // 2, xf[:, j // 2, :]
                    nc.vector.wait_ge(unit_done, i * RING + (up.u0 + j + 1))
                    if j % 2 == 0:
                        nc.vector.tensor_tensor(two(sq[:, 0, :]), tile_halves(0), two(rstd[:, :]),
                                                ALU.mult).then_inc(pair_free[0], 1)
                        ahead(unit_lo, up, i, j)
                        continue
                    if not (isinstance(i, int) and f * FT + i * 2 + jj == 0):
                        nc.vector.wait_ge(gu_lo_done, i * 2 + (f * FT + jj))
                    nc.vector.tensor_tensor(two(product), tile_halves(2), two(rstd[:, :]),
                                            ALU.mult).then_inc(pair_free[1], 1)
                    ahead(unit_lo, up, i, j)
                    nc.vector.wait_ge(pair_free[1], i * 2 + (up.freed + jj + 1))
                    nc.vector.wait_ge(silu_done, i * 2 + (f * FT + jj + 1))
                    nc.vector.tensor_tensor(product, product, sq[:, 0, :], ALU.mult).then_inc(gu_done, 1)
                    nc.vector.wait_ge(gu_hi_done, i * 2 + (f * FT + jj + 1))
                    nc.vector.tensor_tensor(gu_lo[:, i * 2 + jj, :], product, f32(gu_hi[:, i * 2 + jj, :]),
                                            ALU.subtract).then_inc(gu_lo_done, 1)

            def down_turn(i):
                for j in range(RING):
                    ahead(unit_lo, down, i, j)
                    if j % 2:
                        tile = h[:, i * 2 + j // 2, :]
                        nc.vector.wait_ge(unit_done, i * RING + (down.u0 + j + 1))
                        nc.vector.scalar_tensor_tensor(out=two(tile), in0=tile_halves(2 * (j // 2)), scalar=0.5,
                                                       in1=two(tile), op0=ALU.mult,
                                                       op1=ALU.add).then_inc(pair_free[j // 2], 1)
                        (norm_add if next_norm == "final" else h_tile_dve)(next_norm, j // 2, i)

            turns(nc.vector, up, up_turn)
            norm_clear()
            turns(nc.vector, down, down_turn)

        mix_loaded = sem("mix_loaded")
        pads_clear = sem("pads_clear")
        dt_w_hi = sem("dt_w_hi")
        dt_w_lo = sem("dt_w_lo")
        dve_step = sem("dve_step")
        rot_done = sem("rot_done")
        vs_hi_done = sem("vs_hi_done")
        vs_done = sem("vs_done")
        dt_first = sem("dt_first")
        dt_copied = sem("dt_copied")
        dt_raw = sem("dt_raw")
        dt_abs = sem("dt_abs")
        dt_exp = sem("dt_exp")
        dt_one = sem("dt_one")
        dt_log = sem("dt_log")
        dt_done = sem("dt_done")
        a_exp_done = sem("a_exp_done")
        conv_done = sem("conv_done")
        xc_done = sem("xc_done")
        conv_s_sum = sem("conv_s_sum")
        last_kept = sem("last_kept")
        ret_a = sem("ret_a")
        ret_w_done = sem("ret_w_done")
        ret_b = sem("ret_b")
        ret_y = sem("ret_y")
        ret_s_done = sem("ret_s_done")
        ret_stored = sem("ret_stored")
        cum_raw = sem("cum_raw")
        cum_done = sem("cum_done")
        cum_diff = sem("cum_diff")
        decay_done = sem("decay_done")
        au_done = sem("au_done")
        ssd_a = sem("ssd_a")
        xdt_done = sem("xdt_done")
        b_tok_done = sem("b_tok_done")
        lmat_raw = sem("lmat_raw")
        lmat_done = sem("lmat_done")
        ea_done = sem("ea_done")
        ce_done = sem("ce_done")
        xdd_done = sem("xdd_done")
        ssd_sd_done = sem("ssd_sd_done")
        ssd_w_done = sem("ssd_w_done")
        ssd_b = sem("ssd_b")
        ssd_y = sem("ssd_y")
        ssd_s_done = sem("ssd_s_done")
        ssm_stored = sem("ssm_stored")
        mem_loaded = sem("mem_loaded")
        gates_done = sem("gates_done")

        RET_TABLES = 2 * HR * CH
        CDEC = [float(np.exp(np.log1p(-np.exp2(np.float64(-5.0 - i))) * CH)) for i in range(HR)]
        U_MIX = STAGES["qk"].u0
        W_QK, W_V, W_XBC, W_GZ = (STAGES[n] for n in ("qk", "v", "xbc", "gz"))
        W_XK, W_XV, W_OUT = (STAGES[n] for n in ("xk", "xv", "out"))

        class Own:

            def __init__(self, eng, s):
                self.eng, self.sem, self.n = eng, s, 0

            def do(self, ins):
                self.n += 1
                ins.then_inc(self.sem, 1)
                self.eng.wait_ge(self.sem, self.n)

        own_v = Own(nc.vector, dve_step)

        def v4(ap, n=HR):
            return ap.rearrange("p (h c) -> p h c", h=n)

        def qk_dve():
            nc.vector.wait_ge(mix_loaded, 96)
            for a in range(2):
                ins = nc.vector.tensor_tensor(rope[:, a, :], rope[:, a, :], rstd[:, :], ALU.mult)
            own_v.do(ins)
            for j in range(8):
                if j:
                    ahead(unit_lo, W_QK, j // RING, j % RING)
                b, pr = 2 * (j % 2), j % 2
                out = q_t[:, j, :] if j < HR else k_t[:, j - HR, :]
                nc.vector.wait_ge(unit_done, W_QK.u0 + j + 1)
                if j:
                    nc.vector.wait_ge(rot_done, j)
                for lo, hi in ((0, 64), (64, 0)):
                    src = ps[hi:hi + 64, b * BANK:(b + 2) * BANK].rearrange("p (a c) -> p a c", a=2)[:, :, 0:HT]
                    nc.vector.tensor_tensor(two(xf[lo:lo + 64, 0, :]), src, two(rope[hi:hi + 64, 1, :]), ALU.mult)
                nc.vector.tensor_tensor(two(xf[:, 1, :]), tile_halves(b), two(rope[:, 0, :]),
                                        ALU.mult).then_inc(pair_free[pr], 1)
                nc.vector.wait_ge(pair_free[pr], W_QK.freed + j // 2 + 1)
                nc.vector.tensor_tensor(out, xf[:, 0, :], xf[:, 1, :], ALU.add).then_inc(rot_done, 1)
                if j == 0:
                    ahead(unit_lo, W_QK, 0, 0)
                    nc.vector.wait_ge(dt_w_hi, 1)
                    nc.vector.tensor_tensor(wdt_lo[:, :], wdt[:, :], f32(wdt_hi[:, :]),
                                            ALU.subtract).then_inc(dt_w_lo, 1)

        def qk_act():
            nc.scalar.wait_ge(mix_loaded, 96)
            nc.scalar.activation(wdt_hi[:, :], wdt[:, :], ACT.Copy).then_inc(dt_w_hi, 1)
            for j in range(8):
                ahead(unit_hi, W_QK, j // RING, j % RING)

        def token_cols(t):
            return chunk(t) if t < NCH else slice(0, P)

        def v_pe():
            nc.tensor.wait_ge(dt_w_lo, 1)
            for k in range(DT):
                cut = slice(k * HS, (k + 1) * HS)
                for a in range(2):
                    cols = slice(a * HT, (a + 1) * HT)
                    mm = three(bank(6 + a, HT, rows=HS), wdt_hi[:, cut], wdt_lo[:, cut], x_hi[:, k, cols],
                               x_lo[:, k, cols], k == 0, k == DT - 1)
            mm.then_inc(dt_first, 1)
            for pr in range(2):
                nc.tensor.wait_ge(pair_free[pr], W_V.freed)
            for j in range(4):
                nc.tensor.wait_ge(w_lo, W_V.u0 + j + 1)
                for t in range(TOKT):
                    for kk in range(2):
                        k = 2 * j + kk
                        x_h, x_l = x_hi[:, k, token_cols(t)], x_lo[:, k, token_cols(t)]
                        w_h, w_l = (w[j][:, kk * BANK:(kk + 1) * BANK] for w in (w_hi_t, w_lo_t))
                        mm = three(bank(t), x_h, x_l, w_h, w_l, k == 0, k == DT - 1)
                mm.then_inc(unit_done, 1)
            nc.tensor.wait_ge(dt_copied, 1)
            for t in range(TOKT):
                mm = nc.tensor.transpose(bank(5, HS, t * HS), xf[0:HS, 0, token_cols(t)], ident[0:HS, 0:HS])
            mm.then_inc(dt_raw, 1)

        def v_act():
            nc.scalar.activation(a_exp[:, :], a_log, ACT.Exp).then_inc(a_exp_done, 1)
            for j in range(4):
                ahead(unit_hi, W_V, 0, j)
                if j == 0:
                    nc.scalar.wait_ge(dt_first, 1)
                    nc.scalar.wait_ge(rot_done, 8)
                    nc.scalar.activation(two(xf[0:HS, 0, :]), tile_halves(6)[0:HS], ACT.Copy).then_inc(dt_copied, 1)
            nc.scalar.wait_ge(unit_done, W_V.u0 + 4)
            for t in range(NCH):
                ins = nc.scalar.activation(v_t[:, t, :], bank(t), ACT.Copy, scale=row_std[:, 1, t:t + 1])
                if t % 2:
                    ins.then_inc(pair_free[t // 2], 1)
            nc.scalar.wait_ge(pads_clear, 2)
            for r in (0, 2 * LOW):
                ins = nc.scalar.activation(vs[r:r + NS, :], bank(4, rows=NS), ACT.Copy,
                                           scale=row_std[0:NS, 1, NCH:NCH + 1])
            ins.then_inc(vs_hi_done, 1)
            nc.scalar.wait_ge(dt_abs, 1)
            nc.scalar.activation(dt_e, dt_ab, ACT.Exp, scale=-1.0).then_inc(dt_exp, 1)
            nc.scalar.wait_ge(dt_one, 1)
            nc.scalar.activation(dt_u, dt_u, ACT.Ln).then_inc(dt_log, 1)

        def v_dve():
            for j in range(4):
                ahead(unit_lo, W_V, 0, j)
            do = own_v.do

            def heads(ap):
                return ap.rearrange("p (t h) -> p t h", h=HS)

            nc.vector.wait_ge(dt_raw, 1)
            do(nc.vector.tensor_tensor(heads(dt_x), heads(bank(5, NDT)),
                                       row_parts("mix")[1].unsqueeze(2).to_broadcast([P, TOKT, HS]), ALU.mult))
            do(nc.vector.tensor_tensor(heads(dt_x), heads(dt_x),
                                       dt_bias.unsqueeze(1).to_broadcast([P, TOKT, HS]), ALU.add))
            nc.vector.scalar_tensor_tensor(out=dt_ab, in0=dt_x, scalar=-1.0, in1=dt_x, op0=ALU.mult,
                                           op1=ALU.max).then_inc(dt_abs, 1)
            nc.vector.wait_ge(vs_hi_done, 1)
            nc.vector.scalar_tensor_tensor(out=vs[LOW:LOW + NS, :], in0=bank(4, rows=NS),
                                           scalar=row_std[0:NS, 1, NCH:NCH + 1], in1=f32(vs[0:NS, :]), op0=ALU.mult,
                                           op1=ALU.subtract).then_inc(vs_done, 1)
            nc.vector.wait_ge(dt_exp, 1)
            do(nc.vector.tensor_scalar(dt_u, dt_e, 1.0, None, ALU.add))
            do(nc.vector.tensor_scalar(dt_d, dt_u, -1.0, None, ALU.add))
            do(nc.vector.tensor_scalar(dt_m, dt_d, 0.0, None, ALU.is_equal))
            nc.vector.tensor_tensor(dt_d, dt_d, dt_m, ALU.add).then_inc(dt_one, 1)
            nc.vector.wait_ge(dt_one, 1)
            do(nc.vector.reciprocal(dt_t, dt_d))
            nc.vector.wait_ge(dt_log, 1)
            do(nc.vector.tensor_tensor(dt_u, dt_u, dt_m, ALU.add))
            do(nc.vector.tensor_tensor(dt_u, dt_u, dt_e, ALU.mult))
            do(nc.vector.tensor_tensor(dt_u, dt_u, dt_t, ALU.mult))
            do(nc.vector.scalar_tensor_tensor(out=dt_r, in0=dt_x, scalar=0.0, in1=dt_u, op0=ALU.max, op1=ALU.add))
            nc.vector.wait_ge(a_exp_done, 1)
            nc.vector.scalar_tensor_tensor(out=heads(a_dt), in0=heads(dt_r), scalar=-1.0,
                                           in1=a_exp[:, :].unsqueeze(1).to_broadcast([P, TOKT, HS]),
                                           op0=ALU.mult, op1=ALU.mult).then_inc(dt_done, 1)

        def ret_a_pe(c):
            if c == 0:
                nc.tensor.wait_ge(rot_done, 8)
                nc.tensor.wait_ge(vs_done, 1)
                nc.tensor.wait_ge(dt_abs, 1)
            else:
                nc.tensor.wait_ge(ret_w_done, c)
            for i in range(HR):
                nc.tensor.matmul(bank(4, CH, i * CH), k_t[:, i, chunk(c)], q_t[:, i, chunk(c)], start=True, stop=True)
                mm = nc.tensor.transpose(bank(5, P, i * P), k_t[:, i, chunk(c)], ident)
            mm.then_inc(ret_a, 1)

        def ret_b_pe(c):
            nc.tensor.wait_ge(ret_w_done, c + 1)
            if c:
                nc.tensor.wait_ge(ret_y, c)
                nc.tensor.wait_ge(ret_s_done, c)
            for i in range(HR):
                cut = slice(i * P, (i + 1) * P)
                nc.tensor.matmul(bank(6, CH, i * CH), v_t[:, c, cut], ret_w[:, cut], start=True, stop=c == 0)
                if c:
                    nc.tensor.matmul(bank(6, CH, i * CH), ret_s[:, (c - 1) % 2, cut], ret_qd[:, cut],
                                     start=False, stop=True)
            for i in range(HR):
                cut = slice(i * P, (i + 1) * P)
                mm = nc.tensor.matmul(bank(7, P, i * P), ret_k[:, cut], v_t[:, c, cut], start=True, stop=True)
            mm.then_inc(ret_b, 1)

        def ret_a_dve(c):
            nc.vector.wait_ge(ret_a, c + 1)
            if c:
                nc.vector.wait_ge(ret_b, c)
            nc.vector.tensor_tensor(ret_w[:, :], bank(4), c_ret[:, 0:HR * CH], ALU.mult)
            nc.vector.tensor_tensor(v4(ret_k[:, :]), v4(bank(5)),
                                    c_ret[:, RET_TABLES:RET_TABLES + HR].unsqueeze(2).to_broadcast([P, HR, P]),
                                    ALU.mult)
            nc.vector.tensor_tensor(v4(ret_qd[:, :]), q_t[:, :, chunk(c)], v4(c_ret[:, HR * CH:2 * HR * CH]),
                                    ALU.mult).then_inc(ret_w_done, 1)

        def ret_b_dve(c):
            nc.vector.wait_ge(ret_b, c + 1)
            if c == 0:
                nc.vector.tensor_copy(ret_s[:, 0, :], bank(7)).then_inc(ret_s_done, 1)
                return
            nc.vector.wait_ge(ret_s_done, c)
            for i in range(HR):
                cut = slice(i * P, (i + 1) * P)
                ins = nc.vector.scalar_tensor_tensor(out=ret_s[:, c % 2, cut], in0=ret_s[:, (c - 1) % 2, cut],
                                                     scalar=CDEC[i], in1=bank(7, P, i * P), op0=ALU.mult, op1=ALU.add)
            ins.then_inc(ret_s_done, 1)

        def ret_b_act(c):
            nc.scalar.wait_ge(ret_b, c + 1)
            nc.scalar.activation(q_t[:, :, chunk(c)], v4(bank(6)), ACT.Copy).then_inc(ret_y, 1)

        def xbc_pe():
            def after(j):
                (ret_b_pe if j % 2 else ret_a_pe)(j // 2)

            gemm(W_XBC, x_tiles, x_lo_done, SPLIT0["mix"], after=after)

        def xbc_act():
            nc.scalar.wait_ge(pads_clear, 1)

            def silu(n):
                nc.scalar.wait_ge(conv_done, n + 1)
                nc.scalar.activation(conv_tile(n)[:, NS:T], sq[:, n % 2, 0:SEQ], ACT.Silu).then_inc(xc_done, 1)

            for j in range(8):
                ahead(unit_hi, W_XBC, j // RING, j % RING)
                if j:
                    silu(j - 1)
                if j % 2:
                    ret_b_act(j // 2)
            silu(7)

        def xbc_dve():
            do = own_v.do
            nc.vector.wait_ge(pads_clear, 1)
            for j in range(8):
                ahead(unit_lo, W_XBC, j // RING, j % RING)
                acc = sq[:, j % 2, 0:SEQ]
                b, pr, lead = 2 * (j % 2), j % 2, TAPS - 1
                nc.vector.wait_ge(unit_done, W_XBC.u0 + j + 1)
                if j >= 2:
                    nc.vector.wait_ge(last_kept, j - 1)
                nc.vector.tensor_tensor(conv_in[:, j % 2, lead:lead + HT - NS], ps[:, b * BANK + NS:b * BANK + HT],
                                        rstd[:, NS:HT], ALU.mult)
                nc.vector.tensor_tensor(conv_in[:, j % 2, lead + HT - NS:lead + SEQ], half(b, 1), rstd[:, HT:T],
                                        ALU.mult)
                nc.vector.tensor_tensor(conv_s[:, TAPS - 1, j * NS:(j + 1) * NS], ps[:, b * BANK:b * BANK + NS],
                                        rstd[:, 0:NS], ALU.mult).then_inc(pair_free[pr], 1)
                nc.vector.wait_ge(pair_free[pr], W_XBC.freed + j // 2 + 1)
                if j >= 2:
                    nc.vector.wait_ge(xc_done, j - 1)
                do(nc.vector.tensor_scalar(acc, conv_in[:, j % 2, 0:SEQ], conv_w[:, 0, j:j + 1],
                                           conv_b[:, j:j + 1], ALU.mult, ALU.add))
                for t in range(1, TAPS):
                    ins = nc.vector.scalar_tensor_tensor(out=acc, in0=conv_in[:, j % 2, t:t + SEQ],
                                                         scalar=conv_w[:, t, j:j + 1], in1=acc,
                                                         op0=ALU.mult, op1=ALU.add)
                    if t < TAPS - 1:
                        do(ins)
                ins.then_inc(conv_done, 1)
                nc.vector.tensor_copy(conv_last[:, j, :], conv_in[:, j % 2, SEQ:SEQ + TAPS - 1]).then_inc(last_kept, 1)
                if j % 2 == 0:
                    ret_a_dve(j // 2)
                else:
                    ret_b_dve(j // 2)

        def conv_s_dve():
            do = own_v.do
            taps = xf[:, 0, 0:TAPS * 8 * NS]
            total = xf[:, 1, 0:8 * NS]
            do(nc.vector.tensor_tensor(taps.rearrange("p (x b) -> p x b", b=NS),
                                       conv_s[:, :, :].rearrange("p t (n b) -> p (t n) b", b=NS),
                                       small[:, 0:TAPS * 8].unsqueeze(2).to_broadcast([P, TAPS * 8, NS]), ALU.mult))
            do(nc.vector.tensor_reduce(total, taps.rearrange("p (t x) -> p x t", t=TAPS), AX_X, ALU.add))
            nc.vector.tensor_tensor(total.rearrange("p (n b) -> p n b", b=NS),
                                    total.rearrange("p (n b) -> p n b", b=NS),
                                    conv_b.unsqueeze(2).to_broadcast([P, 8, NS]), ALU.add).then_inc(conv_s_sum, 1)

        def conv_s_act():
            nc.scalar.wait_ge(conv_s_sum, 1)
            for n, out in enumerate((cx, cb)):
                ins = nc.scalar.activation(out[:, :, 0:NS],
                                           xf[:, 1, n * 4 * NS:(n + 1) * 4 * NS].rearrange("p (n b) -> p n b", b=NS),
                                           ACT.Silu)
            ins.then_inc(xc_done, 1)

        def cum_pe():
            nc.tensor.wait_ge(dt_done, 1)
            nc.tensor.wait_ge(ret_w_done, NCH)
            nc.tensor.matmul(bank(4, NCH * HS), upper, a_dt[:, 0:NCH * HS], start=True, stop=True)
            nc.tensor.matmul(bank(4, NCH * HS, NCH * HS), ones, a_dt[:, 0:NCH * HS],
                             start=True, stop=True).then_inc(cum_raw, 1)

        def cum_dve():
            n = NCH * HS
            nc.vector.wait_ge(cum_raw, 1)
            nc.vector.tensor_copy(a_cum[:, 0:n], bank(4, n)).then_inc(cum_done, 1)
            nc.vector.tensor_copy(decay[:, 1, :], bank(4, n, n))
            nc.vector.wait_ge(cum_done, 1)
            nc.vector.tensor_tensor(decay[:, 0, :], bank(4, n, n), a_cum[:, 0:n], ALU.subtract).then_inc(cum_diff, 1)

        def cum_act():
            nc.scalar.wait_ge(cum_diff, 1)
            nc.scalar.activation(decay[:, :, :], decay[:, :, :], ACT.Exp).then_inc(decay_done, 1)
            nc.scalar.activation(dt_e[0:NS, 0:HS], a_dt[0:NS, NCH * HS:TOKT * HS], ACT.Exp).then_inc(a_s_exp, 1)

        def ssd_a_pe(c):
            if c == 0:
                nc.tensor.wait_ge(xc_done, 8)
                nc.tensor.wait_ge(cum_diff, 1)
                nc.tensor.wait_ge(ret_y, NCH)
                nc.tensor.wait_ge(ret_s_done, NCH)
            else:
                nc.tensor.wait_ge(ssd_y, c)
                nc.tensor.wait_ge(ssd_s_done, c)
                nc.tensor.wait_ge(lmat_raw, c)
                nc.tensor.wait_ge(ea_done, c)
            nc.tensor.wait_ge(au_done, c + 1)
            for i in range(4):
                nc.tensor.transpose(bank(4, P, i * P), cx[:, i, chunk(c)], ident)
            for g in range(SG):
                nc.tensor.transpose(bank(5, P, g * P), cb[:, g, chunk(c)], ident)
            for g in range(SG):
                nc.tensor.matmul(bank(5, CH, (SG + g) * CH), cb[:, g, chunk(c)], cb[:, SG + g, chunk(c)],
                                 start=True, stop=True)
            for a in range(2):
                mm = nc.tensor.matmul(bank(6 + a), ones, ssd_au[:, a * BANK:(a + 1) * BANK], start=True, stop=True)
            mm.then_inc(ssd_a, 1)

        def ssd_b_pe(c):
            nc.tensor.wait_ge(ssd_w_done, c + 1)
            nc.tensor.wait_ge(ce_done, c + 1)
            nc.tensor.wait_ge(xdd_done, c + 1)
            nc.tensor.wait_ge(b_tok_done, c + 1)
            if c:
                nc.tensor.wait_ge(ssd_s_done, c)
            for i in range(HS):
                out = bank(4, CH, (i // 2) * CH, rows=HP, row0=HP * (i % 2))
                cut, wide = slice(i * HP, (i + 1) * HP), slice(i * CH, (i + 1) * CH)
                nc.tensor.matmul(out, xdt[:, cut], ssd_l[:, wide], start=True, stop=c == 0)
                if c:
                    nc.tensor.matmul(out, ssd_s[:, cut], ssd_e[:, wide], start=False, stop=True)
            for g in range(SG):
                mm = nc.tensor.matmul(bank(5, 4 * HP, g * 4 * HP), b_tok[:, g * P:(g + 1) * P],
                                      xdd[:, g * 4 * HP:(g + 1) * 4 * HP], start=True, stop=True)
            mm.then_inc(ssd_b, 1)

        def ssd_a_dve(c):
            heads = slice(c * HS, (c + 1) * HS)
            nc.vector.wait_ge(ssd_a, c + 1)
            if c:
                nc.vector.wait_ge(ssd_b, c)
            nc.vector.tensor_tensor(v4(xdt[:, :], HS), v4(bank(4), HS),
                                    dt_r[:, heads].unsqueeze(2).to_broadcast([P, HS, HP]),
                                    ALU.mult).then_inc(xdt_done, 1)
            nc.vector.wait_ge(ea_done, c + 1)
            for i in range(HS):
                ins = nc.vector.scalar_tensor_tensor(out=ssd_l[:, i * CH:(i + 1) * CH],
                                                     in0=ps[:, 6 * BANK + i * CH:6 * BANK + (i + 1) * CH],
                                                     scalar=a_cum[:, c * HS + i:c * HS + i + 1], in1=mask,
                                                     op0=ALU.subtract, op1=ALU.min)
            ins.then_inc(lmat_raw, 1)
            nc.vector.wait_ge(lmat_done, c + 1)
            for g in range(SG):
                w = v4(ssd_l[:, g * 4 * CH:(g + 1) * 4 * CH], 4)
                ins = nc.vector.tensor_tensor(w, bank(5, CH, (SG + g) * CH).unsqueeze(1).to_broadcast([P, 4, CH]), w,
                                              ALU.mult)
            ins.then_inc(ssd_w_done, 1)

        def ssd_b_dve(c):
            nc.vector.wait_ge(ssd_b, c + 1)
            for i in range(4):
                ins = nc.vector.scalar_tensor_tensor(out=cx[:, i, chunk(c)], in0=cx[:, i, chunk(c)],
                                                     scalar=d_skip[:, i:i + 1], in1=bank(4, CH, i * CH),
                                                     op0=ALU.mult, op1=ALU.add)
            ins.then_inc(ssd_y, 1)
            if c == 0:
                nc.vector.tensor_copy(ssd_s[:, :], bank(5)).then_inc(ssd_s_done, 1)
            else:
                nc.vector.wait_ge(ssd_sd_done, c)
                nc.vector.tensor_tensor(ssd_s[:, :], ssd_sd[:, :], bank(5), ALU.add).then_inc(ssd_s_done, 1)

        def ssd_a_act(c):
            nc.scalar.wait_ge(ssd_a, c + 1)
            if c:
                nc.scalar.wait_ge(ssd_b, c)
            nc.scalar.activation(ssd_e[:, :], ps[:, 6 * BANK:8 * BANK], ACT.Exp).then_inc(ea_done, 1)
            nc.scalar.activation(b_tok[:, :], bank(5, SG * P), ACT.Copy).then_inc(b_tok_done, 1)
            nc.scalar.wait_ge(lmat_raw, c + 1)
            nc.scalar.activation(ssd_l[:, :], ssd_l[:, :], ACT.Exp).then_inc(lmat_done, 1)

        def ssd_pool(c):
            heads = slice(c * HS, (c + 1) * HS)
            nc.gpsimd.wait_ge(ea_done, c + 1)
            for g in range(SG):
                e = v4(ssd_e[:, g * 4 * CH:(g + 1) * 4 * CH], 4)
                ins = nc.gpsimd.tensor_tensor(e, e, cb[:, SG + g, chunk(c)].unsqueeze(1).to_broadcast([P, 4, CH]),
                                              ALU.mult)
            ins.then_inc(ce_done, 1)
            nc.gpsimd.wait_ge(xdt_done, c + 1)
            if c == 0:
                nc.gpsimd.wait_ge(decay_done, 1)
            nc.gpsimd.tensor_tensor(v4(xdd[:, :], HS), v4(xdt[:, :], HS),
                                    decay[:, 0, heads].unsqueeze(2).to_broadcast([P, HS, HP]),
                                    ALU.mult).then_inc(xdd_done, 1)
            if c:
                nc.gpsimd.wait_ge(ssd_s_done, c)
                nc.gpsimd.tensor_tensor(v4(ssd_sd[:, :], HS), v4(ssd_s[:, :], HS),
                                        decay[:, 1, heads].unsqueeze(2).to_broadcast([P, HS, HP]),
                                        ALU.mult).then_inc(ssd_sd_done, 1)
            if c + 1 < NCH:
                au_pool(c + 1)

        def au_pool(c):
            if c == 0:
                nc.gpsimd.wait_ge(dt_done, 1)
                nc.gpsimd.wait_ge(ret_b, NCH)
            else:
                nc.gpsimd.wait_ge(ssd_a, c)
            nc.gpsimd.tensor_tensor(v4(ssd_au[:, :], HS), upper.unsqueeze(1).to_broadcast([P, HS, CH]),
                                    a_dt[:, c * HS:(c + 1) * HS].unsqueeze(2).to_broadcast([P, HS, CH]),
                                    ALU.mult).then_inc(au_done, 1)

        def gz_pe():
            cum_pe()

            def after(j):
                (ssd_b_pe if j % 2 else ssd_a_pe)(j // 2)

            gemm(W_GZ, x_tiles, x_lo_done, SPLIT0["mix"], after=after)

        def gz_act():
            cum_act()
            for j in range(8):
                ahead(unit_hi, W_GZ, j // RING, j % RING)
                out = g_t[:, j, :] if j < 4 else z_t[:, j - 4, :]
                nc.scalar.wait_ge(pair_free[j % 2], W_GZ.freed + j // 2 + 1)
                nc.scalar.activation(out, out, ACT.Silu).then_inc(gates_done, 1)
                if j == 1:
                    conv_s_act()
                if j % 2 == 0:
                    ssd_a_act(j // 2)
                else:
                    mem_square(j - 1)
                    mem_square(j)

        def gz_dve():
            cum_dve()
            norm_clear()
            for j in range(8):
                ahead(unit_lo, W_GZ, j // RING, j % RING)
                out = g_t[:, j, :] if j < 4 else z_t[:, j - 4, :]
                nc.vector.wait_ge(unit_done, W_GZ.u0 + j + 1)
                nc.vector.tensor_tensor(two(out), tile_halves(2 * (j % 2)), two(rstd[:, :]),
                                        ALU.mult).then_inc(pair_free[j % 2], 1)
                if j == 1:
                    conv_s_dve()
                if j % 2 == 0:
                    ssd_a_dve(j // 2)
                else:
                    norm_add("mem", j - 1)
                    norm_add("mem", j)
                    if j < 7:
                        ssd_b_dve(j // 2)

        def mem_square(n):
            if n == 0:
                nc.scalar.wait_ge(mem_loaded, 16)
            norm_square("mem", n, mem_t[:, n, :])

        smp_rows = sem("smp_rows")
        smp_clear = sem("smp_clear")
        ks_done = sem("ks_done")
        smp_lo_done = sem("smp_lo_done")
        xdts_done = sem("xdts_done")
        a_s_exp = sem("a_s_exp")
        dm_done = sem("dm_done")
        decb_raw = sem("decb_raw")
        decb_done = sem("decb_done")
        block_done = sem("block_done")
        state_loaded = [sem(f"state_loaded{i}") for i in range(3)]
        state_decayed = sem("state_decayed")
        outer_done = sem("outer_done")
        state_done = sem("state_done")
        y_done = sem("y_done")
        state_stored = [sem(f"state_stored{i}") for i in range(3)]
        smp_loaded = sem("smp_loaded")
        masks_done = sem("masks_done")
        y_rows_done = sem("y_rows_done")
        y_back = sem("y_back")
        rs_r = sem("rs_r")
        sm_r = sem("sm_r")
        gn_centred = sem("gn_centred")
        gn_squared = sem("gn_squared")
        gn_scaled = sem("gn_scaled")
        gn_var = sem("gn_var")
        gn_std = sem("gn_std")
        gn_recip = sem("gn_recip")
        gn_inv_hi = sem("gn_inv_hi")
        gn_inv_lo = sem("gn_inv_lo")
        gn_spread = sem("gn_spread")
        pick_h_made = sem("pick_h_made")
        gated = sem("gated")

        def smp_rows_pe():
            nc.tensor.wait_ge(ssd_y, NCH)
            nc.tensor.wait_ge(ssd_s_done, NCH)
            nc.tensor.wait_ge(rstd_done, NORM_AT["mem"] + 1)
            for i in range(HR):
                nc.tensor.transpose(bank(4, P, i * P, rows=NS), k_t[:, i, 0:NS], ident)
                nc.tensor.transpose(bank(5, P, i * P, rows=NS), cx[:, i, 0:NS], ident)
            for g in range(SG):
                mm = nc.tensor.transpose(bank(6, P, g * P, rows=NS), cb[:, g, 0:NS], ident)
            mm.then_inc(smp_rows, 1)

        def decb_pe():
            nc.tensor.wait_ge(dm_done, 1)
            nc.tensor.wait_ge(lmat_raw, NCH)
            nc.tensor.matmul(bank(7, NS * HS, 128), ones[0:NS, :], dm[:, :], start=True, stop=True).then_inc(decb_raw, 1)

        def smp_rows_act():
            nc.scalar.wait_ge(smp_rows, 1)
            nc.scalar.wait_ge(smp_clear, 3)
            for r in (0, LOW):
                nc.scalar.activation(ks_hi[r:r + NS, :], bank(4, rows=NS), ACT.Copy, scale=RK_SCALE)
                nc.scalar.activation(bs_hi[r:r + NS, :], bank(6, SG * P, rows=NS), ACT.Copy).then_inc(ks_done, 1)
            nc.scalar.wait_ge(xdts_done, 1)
            for r in (0, 2 * LOW):
                ins = nc.scalar.activation(xdts_hi[r:r + NS, :], y_rows, ACT.Copy)
            ins.then_inc(ks_done, 1)
            nc.scalar.wait_ge(decb_raw, 1)
            nc.scalar.activation(decb[:, :], bank(7, NS * HS, 128), ACT.Copy).then_inc(decb_done, 1)

        def smp_rows_dve():
            nc.vector.wait_ge(smp_rows, 1)
            nc.vector.tensor_tensor(v4(y_rows, HS), v4(bank(5, rows=NS), HS),
                                    dt_r[0:NS, NCH * HS:TOKT * HS].unsqueeze(2).to_broadcast([NS, HS, HP]),
                                    ALU.mult).then_inc(xdts_done, 1)
            nc.vector.wait_ge(ks_done, 3)
            nc.vector.scalar_tensor_tensor(out=ks_hi[2 * LOW:R3, :], in0=bank(4, rows=NS), scalar=RK_SCALE,
                                           in1=f32(ks_hi[0:NS, :]), op0=ALU.mult, op1=ALU.subtract)
            nc.vector.tensor_tensor(bs_hi[2 * LOW:R3, :], bank(6, SG * P, rows=NS), f32(bs_hi[0:NS, :]), ALU.subtract)
            nc.vector.tensor_tensor(xdts_hi[LOW:LOW + NS, :], y_rows, f32(xdts_hi[0:NS, :]),
                                    ALU.subtract).then_inc(smp_lo_done, 1)

        BUFFER = (0, 2, 1)

        def outer_pe(p):
            if p == 0:
                nc.tensor.wait_ge(smp_lo_done, 1)
            else:
                nc.tensor.wait_ge(state_done, p)
            nc.tensor.wait_ge(block_done, p + 1)
            rows = ks_hi[:, p * P:(p + 1) * P] if p < HR else bs_hi[:, (p - HR) // 2 * P:((p - HR) // 2 + 1) * P]
            for a in range(2):
                mm = nc.tensor.matmul(bank(4 + a), rows, blocks_hi[:, p % 2, a * BANK:(a + 1) * BANK],
                                      start=True, stop=True)
            mm.then_inc(outer_done, 1)

        def state_dve(p):
            nc.vector.wait_ge(outer_done, p + 1)
            outer, piece = ps[:, 4 * BANK:4 * BANK + PIECE], state[:, BUFFER[p % 3], :]
            if p < HR:
                nc.vector.wait_ge(state_loaded[p % 3], 16 * (p // 3 + 1))
                ins = nc.vector.scalar_tensor_tensor(out=piece, in0=piece, scalar=GAMMA[p], in1=outer,
                                                     op0=ALU.mult, op1=ALU.add)
            else:
                nc.vector.wait_ge(state_decayed, p - HR + 1)
                ins = nc.vector.tensor_tensor(piece, piece, outer, ALU.add)
            ins.then_inc(state_done, 1)

        def y_pe(p):
            nc.tensor.wait_ge(state_done, p + 1)
            if p == 0:
                nc.tensor.wait_ge(decb_done, 1)
                nc.tensor.wait_ge(masks_done, 1)
            if p == HR:
                nc.tensor.wait_ge(y_rows_done, 1)
            if p < HR:
                n, w, out = NS, P, bank(7, P, p * P, rows=NS)
                mask = [q_mask[:, (p * NS + b) * NS:(p * NS + b + 1) * NS] for b in range(NS)]
            else:
                g, q = (p - HR) // 2, (p - HR) % 2
                n, w, out = NS // 2, 4 * HP, bank(7, 4 * HP, g * 4 * HP, rows=NS)
                mask = [c_mask[:, (g * NS + 4 * q + b) * NS:(g * NS + 4 * q + b + 1) * NS] for b in range(4)]
            for b in range(n):
                mm = nc.tensor.matmul(out, mask[b], state[:, BUFFER[p % 3], b * w:(b + 1) * w],
                                      start=b == 0 and (p < HR or q == 0), stop=b == n - 1 and (p < HR or q == 1))
            mm.then_inc(y_done, 1)

        def masks_dve():
            nc.vector.wait_ge(smp_loaded, 16)
            nc.vector.wait_ge(xc_done, 9)
            nc.vector.wait_ge(rot_done, 8)
            column = own_column.rearrange("p (a b) -> p a b", a=NS).unsqueeze(1)
            for out, source, n in ((q_mask, q_t[:, :, 0:NS], HR), (c_mask, cb[:, SG:2 * SG, 0:NS], SG)):
                ins = nc.vector.tensor_tensor(out.rearrange("p (h a b) -> p h a b", h=n, a=NS),
                                              source.unsqueeze(3).to_broadcast([P, n, NS, NS]),
                                              column.to_broadcast([P, n, NS, NS]), ALU.mult)
            ins.then_inc(masks_done, 1)

        def y_rows_act(n):
            nc.scalar.wait_ge(y_done, HR * (n + 1))
            if n:
                nc.scalar.wait_ge(y_back, 1)
            nc.scalar.activation(y_rows, bank(7, rows=NS), ACT.Copy).then_inc(y_rows_done, 1)

        def y_back_pe(n):
            nc.tensor.wait_ge(y_rows_done, n + 1)
            if n:
                nc.tensor.wait_ge(gn_std, 2)
            else:
                nc.tensor.wait_ge(gn_std, 1)
            for i in range(4):
                mm = nc.tensor.transpose(bank(6, NS, i * NS), y_rows[:, i * P:(i + 1) * P], ident[0:NS, 0:NS])
            mm.then_inc(y_back, 1)

        def rs_r_act():
            nc.scalar.wait_ge(y_back, 1)
            nc.scalar.wait_ge(masks_done, 1)
            nc.scalar.activation(q_t[:, :, 0:NS], v4(bank(6, HR * NS)), ACT.Copy).then_inc(rs_r, 1)

        def sm_r_dve():
            nc.vector.wait_ge(y_back, 2)
            for i in range(4):
                ins = nc.vector.scalar_tensor_tensor(out=cx[:, i, 0:NS], in0=cx[:, i, 0:NS], scalar=d_skip[:, i:i + 1],
                                                     in1=bank(6, NS, i * NS), op0=ALU.mult, op1=ALU.add)
            ins.then_inc(sm_r, 1)

        eye_s = ident[0:NS, 0:NS]

        def spread_ones(out, rows, n):
            return nc.gpsimd.tensor_tensor(out, fold[0:rows, 0:n].unsqueeze(2).to_broadcast([rows, n, P]),
                                           ones[0:rows, :].unsqueeze(1).to_broadcast([rows, n, P]), ALU.mult)

        def smp_pool():
            def block(p):
                if p >= 2:
                    nc.gpsimd.wait_ge(outer_done, p - 1)
                if p < HR:
                    n, w, source, own = NS, P, vs[:, p * P:(p + 1) * P], fold[0:R3, 0:NS]
                else:
                    g, q = (p - HR) // 2, (p - HR) % 2
                    n, w, source, own = 4, 4 * HP, xdts_hi[:, g * 4 * HP:(g + 1) * 4 * HP], fold[0:R3, 4 * q:4 * q + 4]
                nc.gpsimd.tensor_tensor(blocks_hi[:, p % 2, :].rearrange("p (b c) -> p b c", b=n),
                                        f32(source).unsqueeze(1).to_broadcast([R3, n, w]),
                                        own.unsqueeze(2).to_broadcast([R3, n, w]), ALU.mult).then_inc(block_done, 1)

            def of_piece(retention, ssd, p):
                if p < HR:
                    return A[retention][p]
                g, q = (p - HR) // 2, (p - HR) % 2
                return A[ssd][g][:, q * PIECE:(q + 1) * PIECE]

            def load(p):
                if p >= 3:
                    nc.gpsimd.wait_ge(state_stored[p % 3], 16 * (p // 3))
                    nc.gpsimd.wait_ge(y_done, p - 2)
                nc.gpsimd.dma_start(state[:, BUFFER[p % 3], :], of_piece("st_ret", "st_ssm", p)).then_inc(state_loaded[p % 3], 16)

            def store(p):
                nc.gpsimd.wait_ge(state_done, p + 1)
                nc.gpsimd.dma_start(of_piece("o_ret_s", "o_ssm_s", p), state[:, BUFFER[p % 3], :]).then_inc(state_stored[p % 3], 16)

            def decay(p):
                g, q = (p - HR) // 2, (p - HR) % 2
                piece = state[:, BUFFER[p % 3], :].rearrange("p (b h c) -> p b h c", b=4, h=4)
                nc.gpsimd.wait_ge(state_loaded[p % 3], 16 * (p // 3 + 1))
                if p == HR:
                    nc.gpsimd.wait_ge(decb_done, 1)
                nc.gpsimd.tensor_tensor(piece, piece,
                                        decb[:, :].rearrange("p (b h) -> p b h", b=NS)[:, 4 * q:4 * q + 4,
                                                                                       4 * g:4 * g + 4]
                                        .unsqueeze(3).to_broadcast([P, 4, 4, HP]), ALU.mult).then_inc(state_decayed, 1)

            nc.gpsimd.wait_ge(vs_done, 1)
            nc.gpsimd.wait_ge(ssd_b, NCH)
            nc.gpsimd.wait_ge(a_s_exp, 1)
            nc.gpsimd.tensor_tensor(dm[:, :].rearrange("p (b h) -> p b h", b=NS),
                                    dt_e[0:NS, 0:HS].unsqueeze(1).to_broadcast([NS, NS, HS]),
                                    eye_s.unsqueeze(2).to_broadcast([NS, NS, HS]), ALU.mult).then_inc(dm_done, 1)
            nc.gpsimd.dma_start(c_smp, A["c_smp"]).then_inc(smp_loaded, 16)
            load(0)
            for t in (ks_hi, bs_hi, xdts_hi):
                nc.gpsimd.memset(f32(t[:, :]), 0.0).then_inc(smp_clear, 1)
            load(1)
            nc.gpsimd.wait_ge(ssd_s_done, NCH)
            nc.gpsimd.dma_start(A["o_ssm_p"], ssd_s[:, :]).then_inc(ssm_stored, 16)
            block(0)
            block(1)
            nc.gpsimd.wait_ge(ssm_stored, 16)
            load(2)
            nc.gpsimd.wait_ge(smp_lo_done, 1)
            nc.gpsimd.wait_ge(unit_done, W_XK.u0)
            nc.gpsimd.memset(f32(inv_parts), 0.0).then_inc(pick_h_made, 1)
            spread_ones(pick_h, LOW + HR, HR).then_inc(pick_h_made, 1)
            for p in range(PIECES):
                store(p)
                if p + 2 < PIECES:
                    block(p + 2)
                    if p + 2 >= HR:
                        decay(p + 2)
                if p + 3 < PIECES:
                    load(p + 3)
            nc.gpsimd.dma_start(A["o_conv_p"], conv_last[:, :, :]).then_inc(ssm_stored, 16)
            nc.gpsimd.dma_start(A["o_conv_s"], conv_s[:, 1:TAPS, :]).then_inc(ssm_stored, 16)

        def gn_centre_pe(i):
            if i == 0:
                nc.tensor.wait_ge(smp_lo_done, 1)
            else:
                nc.tensor.wait_ge(gn_squared, i)
            nc.tensor.matmul(bank(6), centre, q_t[:, i, NS:T], start=True, stop=True).then_inc(gn_centred, 1)

        def gn_act(i):
            nc.scalar.wait_ge(gn_centred, i + 1)
            nc.scalar.activation(q_t[:, i, NS:T], bank(6), ACT.Copy)
            nc.scalar.activation(gn_s[:, i, NS:T], bank(6), ACT.Square).then_inc(gn_squared, 1)

        def gn_centre_s_pe():
            nc.tensor.wait_ge(rs_r, 1)
            nc.tensor.matmul(bank(6, HR * NS), centre, q_t[:, :, 0:NS], start=True, stop=True).then_inc(gn_centred, 1)

        def gn_s_act():
            nc.scalar.wait_ge(gn_centred, HR + 1)
            nc.scalar.activation(q_t[:, :, 0:NS], v4(bank(6, HR * NS)), ACT.Copy)
            nc.scalar.activation(gn_s[:, :, 0:NS], v4(bank(6, HR * NS)), ACT.Square).then_inc(gn_squared, 1)

        def gn_gate_dve(i):
            nc.vector.wait_ge(gn_squared, i + 1)
            for k, c in ((i, slice(NS, T)),) if i < HR else [(k, slice(0, NS)) for k in range(HR)]:
                ins = nc.vector.scalar_tensor_tensor(out=q_t[:, k, c], in0=q_t[:, k, c], scalar=gain("ret", k),
                                                     in1=g_t[:, k, c], op0=ALU.mult, op1=ALU.mult)
            ins.then_inc(gn_scaled, 1)

        GN_COLS = (slice(NS, T), slice(0, NS))
        GN_INV = (gn_inv, gn_inv_s)

        def gn_var_pe(n):
            nc.tensor.wait_ge(gn_squared, HR + n)
            w = GN_COLS[n].stop - GN_COLS[n].start
            for i in range(HR):
                mm = nc.tensor.matmul(bank(6, w, rows=HR), pick_mean[:, i * HR:(i + 1) * HR], gn_s[:, i, GN_COLS[n]],
                                      start=i == 0, stop=i == HR - 1)
            mm.then_inc(gn_var, 1)

        def gn_std_act(n):
            w = GN_COLS[n].stop - GN_COLS[n].start
            nc.scalar.wait_ge(gn_var, n + 1)
            nc.scalar.activation(GN_INV[n], bank(6, w, rows=HR), ACT.Sqrt, bias=eps[0:HR, :]).then_inc(gn_std, 1)

        def gn_recip_dve(n):
            nc.vector.wait_ge(gn_std, n + 1)
            nc.vector.reciprocal(GN_INV[n], GN_INV[n]).then_inc(gn_recip, 1)

        def gn_hi_act(n):
            nc.scalar.wait_ge(gn_recip, n + 1)
            if n == 0:
                nc.scalar.wait_ge(pick_h_made, 1)
            nc.scalar.activation(inv_hi[:, GN_COLS[n]], GN_INV[n], ACT.Copy).then_inc(gn_inv_hi, 1)

        def gn_lo_dve(n):
            nc.vector.wait_ge(gn_inv_hi, n + 1)
            nc.vector.tensor_tensor(inv_lo[:, GN_COLS[n]], GN_INV[n], f32(inv_hi[:, GN_COLS[n]]),
                                    ALU.subtract).then_inc(gn_inv_lo, 1)

        def gn_spread_pe(i):
            if i == 0:
                nc.tensor.wait_ge(gn_inv_lo, 2)
                nc.tensor.wait_ge(pick_h_made, 2)
                nc.tensor.wait_ge(state_done, PIECES)
            else:
                nc.tensor.wait_ge(xf_done, MADE0["ret"] + i)
            for a in range(2):
                cols = slice(a * HT, (a + 1) * HT)
                mm = nc.tensor.matmul(half(4, a), pick_h[:, i, :], inv_parts[:, cols], start=True, stop=True)
            mm.then_inc(gn_spread, 1)

        def ret_made_dve(i):
            nc.vector.wait_ge(gn_spread, i + 1)
            if i == 0:
                nc.vector.wait_ge(gn_scaled, HR + 1)
            if i >= 2:
                nc.vector.wait_ge(x_lo_done, SPLIT0["ret"] + i - 1)
            nc.vector.tensor_tensor(two(xf[:, i % 2, :]), tile_halves(4), two(q_t[:, i, :]),
                                    ALU.mult).then_inc(xf_done, 1)

        def ret_hi_act(i):
            nc.scalar.wait_ge(xf_done, MADE0["ret"] + i + 1)
            if i == 0:
                nc.scalar.wait_ge(outer_done, PIECES)
                nc.scalar.wait_ge(state_decayed, PIECES - HR)
            nc.scalar.activation(ret_hi[:, i, :], xf[:, i % 2, :], ACT.Copy).then_inc(x_hi_done, 1)

        def ret_lo_dve(i):
            nc.vector.wait_ge(x_hi_done, SPLIT0["ret"] + i + 1)
            nc.vector.tensor_tensor(ret_lo[:, i, :], xf[:, i % 2, :], f32(ret_hi[:, i, :]),
                                    ALU.subtract).then_inc(x_lo_done, 1)

        def gated_dve(n):
            if n == 0:
                nc.vector.wait_ge(gates_done, 8)
                nc.vector.wait_ge(ssd_y, NCH)
            if n == 4:
                nc.vector.wait_ge(sm_r, 1)
            part = cx[:, n, NS:T] if n < 4 else cx[:, :, 0:NS]
            gate = z_t[:, n, NS:T] if n < 4 else z_t[:, :, 0:NS]
            nc.vector.tensor_tensor(part, part, gate, ALU.mult).then_inc(gated, 1)

        def gated_square_act(n):
            nc.scalar.wait_ge(gated, n + 1)
            nc.scalar.wait_ge(sq_added, SQ0["ssd"] + n)
            if n < 4:
                ins = nc.scalar.activation(sq[:, n % 2, 0:SEQ], cx[:, n, NS:T], ACT.Square)
            else:
                ins = nc.scalar.activation(v4(sq[:, 0, 0:4 * NS]), cx[:, :, 0:NS], ACT.Square)
            ins.then_inc(sq_done, 1)

        def gated_add_dve(n):
            nc.vector.wait_ge(sq_done, SQD0["ssd"] + n + 1)
            nc.vector.wait_ge(sq_added, SQ0["ssd"] + n + 1)
            if n < 4:
                ins = nc.vector.tensor_tensor(sq_sum[:, NS:T], sq_sum[:, NS:T], sq[:, n % 2, 0:SEQ], ALU.add)
            else:
                ins = nc.vector.tensor_reduce(sq_sum[:, 0:NS], sq[:, 0, 0:4 * NS].rearrange("p (n b) -> p b n", n=4),
                                              AX_X, ALU.add)
            ins.then_inc(sq_added, 1)

        def ssd_made_dve(k):
            if k == 0:
                nc.vector.wait_ge(rstd_done, NORM_AT["ssd"] + 1)
            nc.vector.wait_ge(x_lo_done, SPLIT0["ssd"] + k - 1)
            nc.vector.scalar_tensor_tensor(out=xf[:, k % 2, :], in0=cx[:, k, :], scalar=gain("ssd", k), in1=rstd[:, :],
                                           op0=ALU.mult, op1=ALU.mult).then_inc(xf_done, 1)

        def ssd_hi_act(k):
            nc.scalar.wait_ge(xf_done, MADE0["ssd"] + k + 1)
            nc.scalar.activation(ssd_hi[:, k, :], xf[:, k % 2, :], ACT.Copy).then_inc(x_hi_done, 1)

        def ssd_lo_dve(k):
            nc.vector.wait_ge(x_hi_done, SPLIT0["ssd"] + k + 1)
            nc.vector.tensor_tensor(ssd_lo[:, k, :], xf[:, k % 2, :], f32(ssd_hi[:, k, :]),
                                    ALU.subtract).then_inc(x_lo_done, 1)

        def mem_tiles(k):
            return m_tile(x_hi, k), m_tile(x_lo, k)

        def slots(engine):
            steps = {n: [] for n in range(16)}

            def put(n, name, f):
                if name == engine:
                    steps[n].append(f)

            def each(first, count, *pairs):
                for i in range(count):
                    for late, name, f in pairs:
                        put(first + i + late, name, lambda f=f, i=i: f(i))

            put(0, "pe", lambda: norm_spread_pe("mem", 7))
            put(0, "dve", norm_clear)
            put(1, "act", smp_rows_act)
            put(1, "dve", smp_rows_dve)
            put(1, "pe", smp_rows_pe)
            put(1, "pe", decb_pe)
            put(1, "dve", masks_dve)
            put(7, "pe", lambda: y_back_pe(0))
            put(11, "pe", lambda: y_back_pe(1))
            each(2, PIECES, (0, "pe", outer_pe), (0, "dve", state_dve), (1, "pe", y_pe))
            each(2, HR, (0, "pe", gn_centre_pe), (0, "act", gn_act), (0, "dve", gated_dve),
                 (0, "act", gated_square_act), (1, "dve", gated_add_dve), (1, "dve", gn_gate_dve))
            put(6, "pe", lambda: gn_var_pe(0))
            put(6, "act", lambda: gn_std_act(0))
            put(6, "act", lambda: y_rows_act(0))
            put(7, "act", rs_r_act)
            put(7, "dve", lambda: gn_recip_dve(0))
            put(7, "pe", gn_centre_s_pe)
            put(7, "act", gn_s_act)
            put(8, "act", lambda: gn_hi_act(0))
            put(8, "dve", lambda: gn_lo_dve(0))
            put(8, "dve", lambda: gn_gate_dve(HR))
            put(8, "pe", lambda: gn_var_pe(1))
            put(8, "act", lambda: gn_std_act(1))
            put(9, "dve", lambda: gn_recip_dve(1))
            put(9, "act", lambda: gn_hi_act(1))
            put(9, "dve", lambda: gn_lo_dve(1))
            put(10, "act", lambda: y_rows_act(1))
            each(10, HR, (0, "pe", gn_spread_pe), (0, "dve", ret_made_dve), (0, "act", ret_hi_act),
                 (1, "dve", ret_lo_dve))
            put(11, "dve", sm_r_dve)
            put(11, "dve", lambda: gated_dve(4))
            put(11, "act", lambda: gated_square_act(4))
            put(11, "dve", lambda: gated_add_dve(4))
            put(12, "pe", lambda: norm_rows_pe("ssd", inv_512))
            put(12, "act", lambda: norm_rows_act("ssd"))
            put(12, "dve", lambda: norm_diag_dve("ssd"))
            put(13, "pe", lambda: norm_spread_pe("ssd", 6))
            put(13, "act", lambda: norm_rstd_act("ssd", 6))
            put(14, "act", lambda: mem_v_act(0))
            for k in range(4):
                put(14 + k // 2, "act", lambda k=k: ssd_hi_act(k))
            put(15, "act", lambda: mem_v_act(1))
            for k, f in ((0, ssd_made_dve), (1, ssd_made_dve), (0, ssd_lo_dve), (1, ssd_lo_dve)):
                for n in range(2):
                    put(14 + n, "dve", lambda k=k, f=f, n=n: f(2 * n + k))
            return steps

        def xkv_pe():
            steps = slots("pe")

            def after(j):
                for f in steps[j]:
                    f()

            norm_rows_pe("mem", inv_d)
            gemm(W_XK, mem_tiles, x_lo_done, SPLIT0["mem"], width=MEM, after=after)
            for pr in range(2):
                nc.tensor.wait_ge(pair_free[pr], W_XV.freed)
            for k in range(8):
                nc.tensor.wait_ge(w_lo, W_XV.u0 + k + 1)
                m_h, m_l = mem_tiles(k)
                for mt in range(MT):
                    for a in range(2):
                        cut, wide = slice(mt * P, (mt + 1) * P), slice(a * BANK, (a + 1) * BANK)
                        mm = three(bank(2 * mt + a), m_h[:, cut], m_l[:, cut], w_hi_t[k % RING][:, wide],
                                   w_lo_t[k % RING][:, wide], k == 0, k == 7)
                mm.then_inc(unit_done, 1)
                after(8 + k)

        def mem_v_act(mt):
            nc.scalar.wait_ge(unit_done, W_XV.u0 + 8)
            nc.scalar.activation(mem_v[:, mt, :], ps[:, 2 * mt * BANK:(2 * mt + 2) * BANK],
                                 ACT.Copy, scale=row_parts("mem")[1][:, mt:mt + 1]).then_inc(pair_free[mt], 1)

        def xkv_act():
            nc.scalar.wait_ge(unit_done, W_XK.u0)
            for k in range(8):
                gained_hi("mem", k, mem_t[:, k, :], m_tile(x_hi, k))
            for pr in range(2):
                nc.scalar.wait_ge(pair_free[pr], W_XK.freed)
            norm_rows_act("mem")
            norm_rstd_act("mem", 7)
            steps = slots("act")
            for j in range(8):
                ahead(unit_hi, W_XK, j // RING, j % RING)
                for f in steps[j]:
                    f()
            for j in range(8):
                ahead(unit_hi, W_XV, j // RING, j % RING)
                for f in steps[8 + j]:
                    f()

        def xkv_dve():
            for k in range(8):
                gained_lo("mem", k, mem_t[:, k, :], m_tile(x_hi, k), m_tile(x_lo, k), SPLIT0["mem"] + k + 1)
            norm_diag_dve("mem")
            ssd_b_dve(NCH - 1)
            nc.vector.wait_ge(rstd_done, NORM_AT["mem"] + 1)
            steps = slots("dve")
            for j in range(16):
                st = W_XK if j < 8 else W_XV
                ahead(unit_lo, st, (j % 8) // RING, j % RING)
                if j < 8:
                    nc.vector.wait_ge(unit_done, W_XK.u0 + j + 1)
                    nc.vector.wait_ge(x_lo_done, SPLIT0["mem"] + 8)
                    nc.vector.tensor_tensor(mem_k[:, j, :], bank(2 * (j % 2), MEM), rstd[:, 0:MEM],
                                            ALU.mult).then_inc(pair_free[j % 2], 1)
                for f in steps[j]:
                    f()

        def out_tiles(k):
            if k < 4:
                return ret_hi[:, k, :], ret_lo[:, k, :]
            return ssd_hi[:, k - 4, :], ssd_lo[:, k - 4, :]

        def residual_act(stage, next_norm):
            for j in range(8):
                ahead(unit_hi, stage, j // RING, j % RING)
                nc.scalar.wait_ge(pair_free[j % 2], stage.freed + j // 2 + 1)
                h_tile_act(next_norm, j)

        def residual_dve(stage, next_norm):
            norm_clear()
            for j in range(8):
                ahead(unit_lo, stage, j // RING, j % RING)
                nc.vector.wait_ge(unit_done, stage.u0 + j + 1)
                nc.vector.tensor_tensor(two(h[:, j, :]), two(h[:, j, :]), tile_halves(2 * (j % 2)),
                                        ALU.add).then_inc(pair_free[j % 2], 1)
                h_tile_dve(next_norm, j)

        mem_stored = sem("mem_stored")
        sc_done = sem("sc_done")
        mx_done = sem("mx_done")
        ex_done = sem("ex_done")
        inv_done = sem("inv_done")
        pr_done = sem("pr_done")
        pt_done = sem("pt_done")
        at_done = sem("at_done")
        o_done = sem("o_done")
        o_hi = sem("o_hi")
        o_lo = sem("o_lo")
        cache_loaded = [sem(f"cache_loaded{i}") for i in range(3)]
        cache_used = sem("cache_used")
        picks_made = sem("picks_made")
        qr_done = sem("qr_done")
        qr_hi_done = sem("qr_hi_done")
        qr_lo_done = sem("qr_lo_done")
        qb_done = sem("qb_done")
        srow_done = sem("srow_done")
        smx_done = sem("smx_done")
        sex_done = sem("sex_done")
        spr_done = sem("spr_done")
        sr_hi_done = sem("sr_hi_done")
        sr_lo_done = sem("sr_lo_done")
        ab_done = sem("ab_done")
        so_hi = sem("so_hi")
        so_lo = sem("so_lo")
        W_XQ, W_XO = STAGES["xq"], STAGES["xo"]
        NROW = NS * XH

        def q_rows_pe(i):
            for pr in range(2):
                nc.tensor.wait_ge(pair_free[pr], W_XQ.freed + i + 1)
            if i:
                nc.tensor.wait_ge(cache_used, 2 * i - 1)
            for d in range(2):
                mm = nc.tensor.transpose(bank(4, P, d * P, rows=NS), qx(2 * i + d)[:, 0:NS], ident)
            mm.then_inc(qr_done, 1)

        def q_rows_act(i):
            nc.scalar.wait_ge(qr_done, i + 1)
            if i == 0:
                nc.scalar.wait_ge(picks_made, 2)
            if i:
                nc.scalar.wait_ge(qb_done, 2 * i)
            nc.scalar.activation(qr_hi[0:NS, :], bank(4, MEM, rows=NS), ACT.Copy).then_inc(qr_hi_done, 1)

        def q_rows_dve(i):
            nc.vector.wait_ge(qr_hi_done, i + 1)
            nc.vector.tensor_tensor(qr_hi[LOW:LOW + NS, :], bank(4, MEM, rows=NS), f32(qr_hi[0:NS, :]),
                                    ALU.subtract).then_inc(qr_lo_done, 1)

        def q_spread_pe(i):
            nc.tensor.wait_ge(qr_lo_done, i + 1)
            if i == 0:
                nc.tensor.wait_ge(picks_made, 2)
            for b in range(NS):
                if i and b == 4:
                    nc.tensor.wait_ge(cache_used, 2 * i)
                out = ps[:, 4 * BANK + b * MEM:4 * BANK + (b + 1) * MEM]
                mm = nc.tensor.matmul(out, pick_q_hi[:, b, :], qr_hi[:, :], start=True, stop=True)
                if b % 4 == 3:
                    mm.then_inc(qb_done, 1)

        def s_scores_dve(i):
            for n in (2 * i, 2 * i + 1):
                nc.vector.wait_ge(cache_loaded[n % 3], 16 * (n // 3 + 1))
                nc.vector.wait_ge(qb_done, n + 1)
                for q in range(4):
                    b = 4 * (n % 2) + q
                    for m in range(MT):
                        keys, at = cache[:, n % 3, (q * MT + m) * MEM:(q * MT + m + 1) * MEM], m * NROW + b * XH + i
                        query = ps[:, 4 * BANK + b * MEM:4 * BANK + (b + 1) * MEM]
                        ins = nc.vector.tensor_tensor_reduce(keys, keys, query, 1.0, 0.0,
                                                             ALU.mult, ALU.add, att_c[:, 0, at:at + 1])
                ins.then_inc(cache_used, 1)

        def xq_pe():
            def after(j):
                if j >= 2:
                    (q_spread_pe if j % 2 else q_rows_pe)(j // 2 - 1)

            gemm(W_XQ, x_tiles, x_lo_done, SPLIT0["x"], after=after, norm="x")

        def xq_act():
            for j in range(8):
                ahead(unit_hi, W_XQ, j // RING, j % RING)
                if j >= 2 and j % 2 == 0:
                    q_rows_act(j // 2 - 1)

        def xq_dve():
            for j in range(8):
                nc.vector.wait_ge(unit_done, W_XQ.u0 + j + 1)
                nc.vector.tensor_tensor(two(qx(j)), tile_halves(2 * (j % 2)), two(rstd[:, :]),
                                        ALU.mult).then_inc(pair_free[j % 2], 1)
                ahead(unit_lo, W_XQ, j // RING, j % RING)
                if j >= 2:
                    (s_scores_dve if j % 2 else q_rows_dve)(j // 2 - 1)

        def picks_pool():
            nc.gpsimd.wait_ge(unit_done, W_OUT.u0 + 8)
            nc.gpsimd.memset(f32(qr_hi[:, :]), 0.0).then_inc(picks_made, 1)
            spread_ones(pick_q_hi[:, :, :], LOW + NS, NS).then_inc(picks_made, 1)

        def pick_rows_pool():
            nc.gpsimd.wait_ge(unit_done, W_XQ.u0 + 8)
            spread_ones(pick_r, LOW + NROW, NROW).then_inc(picks_made, 1)

        def score_pe(c):
            b = 2 * (c % 2)
            if c < 2:
                nc.tensor.wait_ge(pair_free[c], W_XO.freed)
            else:
                nc.tensor.wait_ge(ex_done, c - 1)
            if c == 0:
                nc.tensor.wait_ge(pair_free[1], W_XO.freed)
            for i in range(XH):
                out = ps[:, b * BANK + i * MEM:b * BANK + (i + 1) * MEM]
                for d in range(2):
                    mm = nc.tensor.matmul(out, qx(2 * i + d)[:, chunk(c)], mem_k[:, 2 * i + d, :],
                                          start=d == 0, stop=d == 1)
            mm.then_inc(sc_done, 1)

        def att_stats(c):
            return (att_s[:, c % 2, i * XH:(i + 1) * XH] for i in range(3))

        def softmax_dve(c):
            mx, total, inv = att_stats(c)
            b = 2 * (c % 2)
            nc.vector.wait_ge(sc_done, c + 1)
            own_v.do(nc.vector.tensor_reduce(mx, ps[:, b * BANK:(b + 2) * BANK].rearrange("p (i m) -> p i m", i=XH),
                                             AX_X, ALU.max))
            nc.vector.tensor_scalar(mx, mx, -X_SCALE, None, ALU.mult).then_inc(mx_done, 1)

        def softmax_act(c):
            mx, total, inv = att_stats(c)
            b = 2 * (c % 2)
            nc.scalar.wait_ge(mx_done, c + 1)
            if c >= 2:
                nc.scalar.wait_ge(pt_done, c - 1)
            for i in range(XH):
                ins = nc.scalar.activation(att_p[:, c % 2, i * MEM:(i + 1) * MEM],
                                           ps[:, b * BANK + i * MEM:b * BANK + (i + 1) * MEM], ACT.Exp,
                                           bias=mx[:, i:i + 1], scale=X_SCALE, accum_out=total[:, i:i + 1])
            ins.then_inc(ex_done, 1)

        def probs_dve(c):
            mx, total, inv = att_stats(c)
            nc.vector.wait_ge(ex_done, c + 1)
            nc.vector.reciprocal(inv, total).then_inc(inv_done, 1)

        def probs_act(c):
            mx, total, inv = att_stats(c)
            nc.scalar.wait_ge(inv_done, c + 1)
            for i in range(XH):
                p = att_p[:, c % 2, i * MEM:(i + 1) * MEM]
                ins = nc.scalar.activation(p, p, ACT.Copy, scale=inv[:, i:i + 1])
            ins.then_inc(pr_done, 1)

        def probs_pool(c):
            mx, total, inv = att_stats(c)
            nc.gpsimd.wait_ge(inv_done, c + 1)
            p = v4(att_p[:, c % 2, :])
            nc.gpsimd.tensor_tensor(p, p, inv.unsqueeze(2).to_broadcast([P, XH, MEM]), ALU.mult).then_inc(pr_done, 1)

        def turn_pe(c):
            nc.tensor.wait_ge(pr_done, c + 1)
            if c == 0:
                nc.tensor.wait_ge(cache_used, NS - 1)
            else:
                nc.tensor.wait_ge(at_done, c)
            for i in range(XH):
                for m in range(MT):
                    mm = nc.tensor.transpose(bank(4 + m, P, i * P), att_p[:, c % 2, i * MEM + m * P:i * MEM + (m + 1) * P],
                                             ident)
            mm.then_inc(pt_done, 1)

        def turned_act(c):
            nc.scalar.wait_ge(pt_done, c + 1)
            if c == 0:
                nc.scalar.wait_ge(qb_done, NS)
            for m, att in enumerate((att_0, att_1)):
                ins = nc.scalar.activation(att[:, :, c * CH:(c + 1) * CH], v4(bank(4 + m)), ACT.Copy)
            ins.then_inc(at_done, 1)

        O_BANKS = (0, 1, 4, 5)

        def o_pe(n):
            i, b = n // 2, O_BANKS[n % 4]
            if n == 0:
                nc.tensor.wait_ge(at_done, NCH)
            if n >= 4:
                nc.tensor.wait_ge(o_lo, n - 3)
            for m, att in enumerate((att_0, att_1)):
                mm = nc.tensor.matmul(bank(b), mem_v[:, m, n * P:(n + 1) * P], att[:, i, :],
                                      start=m == 0, stop=m == 1)
            mm.then_inc(o_done, 1)

        def o_act(n):
            nc.scalar.wait_ge(o_done, n + 1)
            nc.scalar.activation(o_tiles(n)[0][:, NS:T], bank(O_BANKS[n % 4]), ACT.Copy).then_inc(o_hi, 1)

        def o_dve(n):
            nc.vector.wait_ge(o_hi, n + 1)
            hi, lo = o_tiles(n)
            nc.vector.tensor_tensor(lo[:, NS:T], bank(O_BANKS[n % 4]), f32(hi[:, NS:T]), ALU.subtract).then_inc(o_lo, 1)

        def cache_pool():
            picks_pool()
            for i in range(3):
                nc.gpsimd.wait_ge(state_stored[i], 16 * len(range(i, PIECES, 3)))
            for n in range(2 * NS):
                if n == NS + 3:
                    for c in range(1, NCH):
                        probs_pool(c)
                if n >= 3:
                    nc.gpsimd.wait_ge(cache_used, n - 2)
                if n == NS:
                    pick_rows_pool()
                nc.gpsimd.dma_start(cache[:, n % 3, :], A["cache"][n]).then_inc(cache_loaded[n % 3], 16)

        def s_softmax_pe():
            nc.tensor.wait_ge(cache_used, NS)
            for m in range(MT):
                mm = nc.tensor.transpose(bank(6, P, m * P, rows=NROW), att_c[:, 0, m * NROW:(m + 1) * NROW], ident)
            mm.then_inc(srow_done, 1)

        def s_max_dve():
            nc.vector.wait_ge(srow_done, 1)
            own_v.do(nc.vector.tensor_reduce(s_stat[:, 0:1], bank(6, MEM, rows=NROW), AX_X, ALU.max))
            nc.vector.tensor_scalar(s_stat[:, 0:1], s_stat[:, 0:1], -X_SCALE, None, ALU.mult).then_inc(smx_done, 1)

        def s_exp_act():
            nc.scalar.wait_ge(smx_done, 1)
            nc.scalar.activation(s_rows[:, :], bank(6, MEM, rows=NROW), ACT.Exp, bias=s_stat[:, 0:1], scale=X_SCALE,
                                 accum_out=s_stat[:, 1:2]).then_inc(sex_done, 1)

        def s_probs_dve():
            nc.vector.wait_ge(sex_done, 1)
            own_v.do(nc.vector.reciprocal(s_stat[:, 2:3], s_stat[:, 1:2]))
            nc.vector.tensor_scalar(s_rows[:, :], s_rows[:, :], s_stat[:, 2:3], None, ALU.mult).then_inc(spr_done, 1)

        def s_probs_act():
            nc.scalar.wait_ge(spr_done, 1)
            nc.scalar.wait_ge(unit_done, W_XQ.u0 + 8)
            nc.scalar.activation(sr[0:NROW, :], s_rows[:, :], ACT.Copy).then_inc(sr_hi_done, 1)

        def s_lo_dve():
            nc.vector.wait_ge(sr_hi_done, 1)
            nc.vector.tensor_tensor(sr[LOW:LOW + NROW, :], s_rows[:, :], f32(sr[0:NROW, :]), ALU.subtract).then_inc(sr_lo_done, 1)

        def s_spread_pe(b):
            if b == 0:
                nc.tensor.wait_ge(sr_lo_done, 1)
                nc.tensor.wait_ge(picks_made, 3)
            elif b == 1:
                nc.tensor.wait_ge(ex_done, NCH)
            else:
                nc.tensor.wait_ge(cache_used, NS + b - 1)
            for i in range(XH):
                at = (6 - 4 * (b % 2)) * BANK + i * MEM
                mm = nc.tensor.matmul(ps[:, at:at + MEM], pick_r[:, b * XH + i, :], sr, start=True, stop=True)
            mm.then_inc(ab_done, 1)

        def s_values_dve(b):
            n = NS + b
            nc.vector.wait_ge(cache_loaded[n % 3], 16 * (n // 3 + 1))
            nc.vector.wait_ge(ab_done, b + 1)
            for t in range(DT):
                values, at = cache[:, n % 3, t * MEM:(t + 1) * MEM], (6 - 4 * (b % 2)) * BANK + (t // 2) * MEM
                ins = nc.vector.tensor_tensor_reduce(values, values, ps[:, at:at + MEM], 1.0, 0.0, ALU.mult, ALU.add,
                                                     att_c[:, 1, t * NS + b:t * NS + b + 1])
            ins.then_inc(cache_used, 1)

        def so_act():
            nc.scalar.wait_ge(cache_used, 2 * NS)
            for a, hi in enumerate((oa_hi, ob_hi)):
                ins = nc.scalar.activation(hi[:, :, 0:NS], v4(att_c[:, 1, a * 4 * NS:(a + 1) * 4 * NS]), ACT.Copy)
            ins.then_inc(so_hi, 1)

        def so_dve():
            nc.vector.wait_ge(so_hi, 1)
            for a, (hi, lo) in enumerate(((oa_hi, oa_lo), (ob_hi, ob_lo))):
                ins = nc.vector.tensor_tensor(lo[:, :, 0:NS], v4(att_c[:, 1, a * 4 * NS:(a + 1) * 4 * NS]),
                                              f32(hi[:, :, 0:NS]), ALU.subtract)
            ins.then_inc(so_lo, 1)

        def att_pe():
            score_pe(0)
            q_rows_pe(XH - 1)
            score_pe(1)
            q_spread_pe(XH - 1)
            score_pe(2)
            s_softmax_pe()
            turn_pe(0)
            score_pe(3)
            turn_pe(1)
            s_spread_pe(0)
            turn_pe(2)
            s_spread_pe(1)
            turn_pe(3)
            for n in range(8):
                if n < 6:
                    s_spread_pe(n + 2)
                o_pe(n)
            nc.tensor.wait_ge(so_lo, 1)

        def att_act():
            softmax_act(0)
            q_rows_act(XH - 1)
            probs_act(0)
            softmax_act(1)
            s_exp_act()
            turned_act(0)
            s_probs_act()
            softmax_act(2)
            turned_act(1)
            softmax_act(3)
            turned_act(2)
            turned_act(3)
            for n in range(7):
                o_act(n)
            so_act()
            o_act(7)

        def att_dve():
            softmax_dve(0)
            q_rows_dve(XH - 1)
            probs_dve(0)
            softmax_dve(1)
            s_scores_dve(XH - 1)
            softmax_dve(2)
            s_max_dve()
            probs_dve(1)
            s_probs_dve()
            s_lo_dve()
            softmax_dve(3)
            probs_dve(2)
            s_values_dve(0)
            probs_dve(3)
            s_values_dve(1)
            for b in range(2, NS):
                s_values_dve(b)
                o_dve(b - 2)
            o_dve(NS - 2)
            so_dve()
            o_dve(NS - 1)

        def final_dve():
            norm_diag_dve("final")
            nc.vector.wait_ge(rstd_done, NORM_AT["final"] + 1)
            nc.vector.wait_ge(unit_done, UNITS)
            for k in range(DT):
                nc.vector.scalar_tensor_tensor(out=y_out[:, k, :], in0=h[:, k, :], scalar=gain("final", k),
                                               in1=rstd[:, :], op0=ALU.mult, op1=ALU.mult).then_inc(xf_done, 1)

        block = ctx.enter_context(nc.Block())

        def load_unit(v, j, src, cols, first=False):
            if not first:
                nc.sync.wait_ge(w_lo, v - RAW + 1)
            nc.sync.dma_start(w_raw[j % RAW][:, 0:cols], src).then_inc(w_loaded[j % RAW], 16)

        @block.sync
        def _(sp):
            sp.dma_start(gains[:, :], A["gains"]).then_inc(gains_loaded, 16)
            for name, st in STAGES.items():
                src = A["w_" + name]
                head = RAW if st.u0 == 0 else 0
                for n in range(head):
                    load_unit(n, n, src[n], st.cols, first=True)
                    if n == 0:
                        for q in range(4):
                            sp.dma_start(h[:, 2 * q:2 * q + 2, :], A["xT"][:, 2 * q:2 * q + 2, :]).then_inc(h_loaded[q], 16)
                    else:
                        sp.dma_start(square[:, :], A["c_square"]).then_inc(square_loaded, 16)
                with sp.Fori(head // 2, st.units // 2) as i:
                    for j in range(2):
                        load_unit(i * 2 + (st.u0 + j), (st.u0 + j) % 2,
                                  src[bass.ds(i * 2 + j, 1)].rearrange("o p c -> (o p) c"), st.cols)
            for k in range(0, DT, 2):
                sp.wait_ge(xf_done, MADE0["final"] + k + 2)
                sp.dma_start(A["o_y"][:, k:k + 2, :], y_out[:, k:k + 2, :]).then_inc(y_stored, 16)
            sp.wait_ge(y_stored, 16 * (DT // 2))

        @block.scalar
        def _(act):
            act.sem_inc(pair_free[0], 1)
            act.sem_inc(pair_free[1], 1)
            split_first(0)
            act.wait_ge(gains_loaded, 16)
            for n in range(DT):
                if n % 2 == 0:
                    act.wait_ge(h_loaded[n // 2], 16)
                gained_hi("ffn1", n, h[:, n, :], x_hi[:, n, :])
                norm_square("ffn1", n, h[:, n, :])
                if n in (3, 7):
                    split_first(1 + n // 4)
            act.wait_ge(square_loaded, 16)
            ffn_act("up1", "down1", "ffn1", "mix", 0)
            norm_of_h_act("mix")
            qk_act()
            v_act()
            xbc_act()
            gz_act()
            xkv_act()
            residual_act(W_OUT, "x")
            norm_of_h_act("x")
            xq_act()
            att_act()
            residual_act(W_XO, "ffn2")
            act.wait_ge(mem_stored, 32)
            ffn_act("up2", "down2", "ffn2", "final", 1)
            norm_rows_act("final")
            norm_rstd_act("final")

        @block.vector
        def _(dve):
            unit_lo(0, 0, UNIT_COLS[0])
            dve.wait_ge(gains_loaded, 16)
            for n in range(DT):
                gained_lo("ffn1", n, h[:, n, :], x_hi[:, n, :], x_lo[:, n, :], n + 1)
                if n in (3, 7):
                    unit_lo(1 + n // 4, 1 + n // 4, UNIT_COLS[1])
            dve.wait_ge(square_loaded, 16)
            ffn_dve("up1", "down1", "ffn1", "mix", 0)
            norm_of_h_dve("mix")
            qk_dve()
            v_dve()
            xbc_dve()
            gz_dve()
            xkv_dve()
            residual_dve(W_OUT, "x")
            norm_of_h_dve("x")
            xq_dve()
            att_dve()
            residual_dve(W_XO, "ffn2")
            dve.wait_ge(mem_stored, 32)
            ffn_dve("up2", "down2", "ffn2", "final", 1)
            final_dve()

        @block.tensor
        def _(pe):
            ffn_pe("up1", "down1", "ffn1", 0)
            gemm(W_QK, x_tiles, x_lo_done, SPLIT0["mix"], norm="mix")
            v_pe()
            xbc_pe()
            gz_pe()
            xkv_pe()
            gemm(W_OUT, out_tiles, x_lo_done, SPLIT0["ret"])
            xq_pe()
            att_pe()
            gemm(W_XO, o_tiles, o_lo, 0)
            ffn_pe("up2", "down2", "ffn2", 1)
            norm_rows_pe("final", inv_d)
            norm_spread_pe("final")

        @block.gpsimd
        def _(pool):
            norm_clear(pool)
            for n in range(DT):
                norm_add("ffn1", n, eng=pool)
            pool.wait_ge(unit_done, U_MIX)
            for dst, src in ((rope[:, :, :], "c_rope"), (c_ret[:, :], "c_ret"), (triangle[:, :], "c_triangle"),
                             (small[:, :], "small"), (wdt[:, :], "wdt"), (conv_s[:, 0:TAPS - 1, :], "conv_s")):
                pool.dma_start(dst, A[src]).then_inc(mix_loaded, 16)
            nc.gpsimd.memset(conv_in[:, :, 0:TAPS - 1], 0.0).then_inc(pads_clear, 1)
            nc.gpsimd.memset(f32(vs[:, :]), 0.0).then_inc(pads_clear, 1)
            pool.wait_ge(ret_s_done, NCH)
            pool.dma_start(A["o_ret_p"], ret_s[:, (NCH - 1) % 2, :]).then_inc(ret_stored, 16)
            au_pool(0)
            pool.wait_ge(ret_stored, 16)
            pool.dma_start(mem_t[:, :, :], A["memT"]).then_inc(mem_loaded, 16)
            for c in range(NCH):
                ssd_pool(c)
            smp_pool()
            pool.wait_ge(unit_done, W_XK.u0 + 8)
            for pr in range(2):
                pool.wait_ge(pair_free[pr], W_XV.freed)
            pool.dma_start(A["o_mem_k"], mem_k[:, :, :]).then_inc(mem_stored, 16)
            for pr in range(2):
                pool.wait_ge(pair_free[pr], W_OUT.freed)
            pool.dma_start(A["o_mem_v"], mem_v[:, :, :]).then_inc(mem_stored, 16)
            cache_pool()
            pool.wait_ge(ssm_stored, 48)
            for i in range(3):
                pool.wait_ge(state_stored[i], 16 * len(range(i, PIECES, 3)))
            pool.wait_ge(mem_stored, 32)


def tiled(w):
    k, n = w.shape
    return w.reshape(k // P, P, n // P, P).transpose(2, 1, 0, 3).reshape(n // P, P, -1)


def feature_major(x):
    return x.T.reshape(-1, P, x.shape[0]).transpose(1, 0, 2)


def columns(v):
    return v.reshape(-1, P).T


def lay_out(i):
    i = {k: np.asarray(v) for k, v in i.items()}
    a = dict(tables())
    cat = np.concatenate
    a["xT"] = feature_major(cat([i["x_sample"][:, 0], i["x_prompt"][0]], 0))
    a["gains"] = cat([columns(i[n].reshape(-1)) for n in
                      ("ffn1_norm", "mem_norm", "mix_norm", "x_norm", "ffn2_norm", "final_norm", "ret_gn_gain",
                       "ssd_norm")], 1)
    for f in ("1", "2"):
        up = [tiled(i[f"ffn{f}_w{w}"][0]) for w in ("1", "3")]
        a["w_up" + f] = np.stack(up, 1).reshape(2 * FT, P, -1)
        down = i[f"ffn{f}_w2"][0].reshape(2, KH, P, DT, P)
        a["w_down" + f] = down.transpose(3, 0, 2, 1, 4).reshape(2 * DT, P, -1)
    w_in = i["w_in"][0]
    a["w_qk"] = tiled(w_in[:, 0:1024])
    a["w_v"] = w_in[:, 1024:1536].reshape(4, 2, P, 512).transpose(0, 2, 1, 3).reshape(4, P, 1024)
    a["w_gz"] = tiled(w_in[:, 1536:2560])
    a["w_xbc"] = tiled(w_in[:, 2560:3584])
    a["wdt"] = w_in[:, 3584:].reshape(DT, P, HS).transpose(1, 0, 2).reshape(P, DT * HS)
    a["small"] = cat([i["conv_w"][0].reshape(TAPS, 8, P).transpose(2, 0, 1).reshape(P, TAPS * 8),
                      columns(i["conv_b"][0]), np.broadcast_to(i["dt_bias"][0], (P, HS)),
                      np.broadcast_to(i["A_log"][0], (P, HS)),
                      columns(np.repeat(i["D_skip"][0], HP))], 1)
    a["conv_s"] = i["state_conv"][0].reshape(NS, TAPS - 1, 8, P).transpose(3, 1, 2, 0).reshape(P, TAPS - 1, 8 * NS)
    a["memT"] = feature_major(i["mem_prompt"][0])
    a["w_out"] = tiled(i["w_out"][0])
    a["w_xk"], a["w_xq"], a["w_xo"] = tiled(i["w_xk"][0]), tiled(i["w_xq"][0]), tiled(i["w_xo"][0])
    a["w_xv"] = i["w_xv"][0].reshape(8, P, D)
    a["st_ret"] = i["state_ret"][0].transpose(1, 2, 0, 3).reshape(HR, P, NS * P)
    a["st_ssm"] = i["state_ssm"][0].reshape(NS, SG, 4, HP, P).transpose(1, 4, 0, 2, 3).reshape(SG, P, -1)
    keys = i["cache_mem_k"][0].reshape(2, 4, MT, P, XH, D // XH).transpose(4, 0, 3, 1, 2, 5).reshape(2 * XH, P, -1)
    values = i["cache_mem_v"][0].reshape(NS, MEM, DT, P).transpose(0, 3, 2, 1).reshape(NS, P, DT * MEM)
    a["cache"] = cat([keys, values], 0)
    return a


OUTS = {"o_y": (P, DT, T), "o_ret_p": (P, HR * P), "o_ssm_p": (P, HS * HP), "o_conv_p": (P, 8, TAPS - 1),
        "o_conv_s": (P, TAPS - 1, 8 * NS), "o_ret_s": (HR, P, NS * P), "o_ssm_s": (SG, P, NS * 4 * HP),
        "o_mem_k": (P, DT, MEM), "o_mem_v": (P, MT, D)}


def give(r):
    y = r["o_y"].transpose(2, 1, 0).reshape(T, D)
    return (y[NS:].reshape(1, SEQ, D), y[:NS].reshape(NS, 1, D),
            r["o_ret_p"].reshape(P, HR, P).transpose(1, 0, 2)[None, None],
            r["o_ssm_p"].reshape(P, HS, HP).transpose(1, 2, 0)[None, None],
            r["o_conv_p"].transpose(2, 1, 0).reshape(1, 1, TAPS - 1, D),
            r["o_mem_k"].transpose(2, 1, 0).reshape(1, 1, MEM, XH, D // XH),
            r["o_mem_v"].transpose(1, 0, 2).reshape(1, 1, MEM, XH, D // XH),
            r["o_ret_s"].reshape(HR, P, NS, P).transpose(2, 0, 1, 3)[None],
            r["o_ssm_s"].reshape(SG, P, NS, 4, HP).transpose(2, 0, 3, 4, 1).reshape(1, NS, HS, HP, P),
            r["o_conv_s"].reshape(P, TAPS - 1, 8, NS).transpose(3, 1, 2, 0).reshape(1, NS, TAPS - 1, D))


def kernel(**inputs):
    import numpy as _np
    import concourse.bacc as _bacc
    from concourse.bass_utils import run_bass_kernel_spmd as _run

    nc = _bacc.Bacc("TRN2", target_bir_lowering=False, num_devices=1)
    arrays = {"in_" + n: _np.ascontiguousarray(a) for n, a in lay_out(inputs).items()}
    A = {n[3:]: nc.dram_tensor(n, a.shape, F32, kind="ExternalInput").ap() for n, a in arrays.items()}
    for n, shape in OUTS.items():
        A[n] = nc.dram_tensor(n, shape, F32, kind="ExternalOutput").ap()
    build(nc, A)
    r = _run(nc, [arrays], core_ids=[0]).results[0]
    return give(r)
```
